# Optimizing a Trainium2 kernel written in Bass

```python
import jax, jax.numpy as jnp
from jax import lax
import numpy as np

D_MODEL = 1024
BATCH = 1
SEQ = 256
DEPTH = 1
DEC_BATCH = 8
DEC_SEQ = 4
PAST_LEN = 1024
PAGE_SIZE = 128

HG_HEADS = 4
HG_DK = 128
HG_DV = 128
HG_WIDTH = HG_HEADS * HG_DV
HG_CHUNK = 32
NSA_HEADS = 8
NSA_KV_HEADS = 2
NSA_HPG = NSA_HEADS // NSA_KV_HEADS
NSA_HD = 64
NSA_WIDTH = NSA_HEADS * NSA_HD
KV_WIDTH = NSA_KV_HEADS * NSA_HD
CMP_BLOCK = 32
CMP_STRIDE = 16
CMP_RATIO = CMP_BLOCK // CMP_STRIDE
CMP_HIDDEN = 128
SEL_BLOCK = 64
N_SEL = 16
WINDOW = 512
WIN_Q_BLOCK = 128
SEL_Q_BLOCK = 16
MIX_WIDTH = HG_WIDTH + NSA_WIDTH
N_MEM = 256
MEM_HEADS = 4
MEM_HD = D_MODEL // MEM_HEADS
PEER_HEADS = 8
PEER_NKEYS = 128
PEER_EXPERTS = PEER_NKEYS * PEER_NKEYS
PEER_KEY_DIM = 128
PEER_TOPK = 16
PEER_TOKEN_BLOCK = 256
DN_ALPHA = (2.0 * DEPTH) ** 0.25
DN_BETA = (8.0 * DEPTH) ** -0.25
LN_EPS = 1e-5
NEG_INF = -1e30

IN_SIZES = (HG_HEADS * HG_DK, HG_HEADS * HG_DK, HG_WIDTH, HG_WIDTH,
            NSA_WIDTH, KV_WIDTH, KV_WIDTH, KV_WIDTH, KV_WIDTH, KV_WIDTH, KV_WIDTH, 3 * NSA_HEADS)
IN_IS_VALUE = (False, False, True, False, False, False, True, False, True, False, True, False)
IN_OFFSETS = tuple(sum(IN_SIZES[:i + 1]) for i in range(len(IN_SIZES) - 1))
IN_COLS = sum(IN_SIZES)

kernel_name = 'hymba_hgrn2_nsa_peer_decode_step'

def layer_norm(x, g, b):
    xf = x.astype(jnp.float32)
    xc = xf - jnp.mean(xf, -1, keepdims=True)
    var = jnp.mean(xc * xc, -1, keepdims=True)
    return (xc * lax.rsqrt(var + LN_EPS) * g + b).astype(x.dtype)

def rms_norm(x, g):
    xf = x.astype(jnp.float32)
    return xf * lax.rsqrt(jnp.mean(xf * xf, -1, keepdims=True) + LN_EPS) * g

def alibi_slopes():
    s = 2.0 ** (-8.0 * np.arange(1, NSA_HEADS + 1) / NSA_HEADS)
    return jnp.asarray(s, jnp.float32).reshape(NSA_KV_HEADS, NSA_HPG)

def masked_softmax(s, mask):
    p = jax.nn.softmax(jnp.where(mask, s, NEG_INF), axis=-1)
    return jnp.where(mask, p, 0.0)

def hgrn_features(zq, zf, zi, lb):
    B, T, _ = zq.shape
    zf = zf.astype(jnp.float32)
    f = lb + (1.0 - lb) * jax.nn.sigmoid(zf)
    log_f = jnp.log(f)
    k = (1.0 - lb) * jax.nn.sigmoid(-zf)
    heads = lambda a, d: a.astype(jnp.float32).reshape(B, T, HG_HEADS, d).transpose(0, 2, 1, 3)
    return heads(zq, HG_DK), heads(k, HG_DK), heads(zi, HG_DV), heads(log_f, HG_DK)

def hgrn_recurrence(q, k, v, log_f, s0, chunk):
    B, H, T, _ = q.shape
    n = T // chunk
    split = lambda a: jnp.moveaxis(a.reshape(B, H, n, chunk, a.shape[-1]), 2, 0)
    causal = jnp.tril(jnp.ones((chunk, chunk), bool))[:, :, None]

    def step(S, inp):
        qc, kc, vc, lc = inp
        G = jnp.cumsum(lc, axis=2)
        rel = jnp.where(causal, G[:, :, :, None, :] - G[:, :, None, :, :], -jnp.inf)
        att = jnp.einsum('bhtd,bhsd,bhtsd->bhts', qc, kc, jnp.exp(rel))
        o = jnp.einsum('bhtd,bhde->bhte', qc * jnp.exp(G), S) + jnp.einsum('bhts,bhse->bhte', att, vc)
        G_end = G[:, :, -1]
        S = jnp.exp(G_end)[..., None] * S + jnp.einsum('bhsd,bhse->bhde', kc * jnp.exp(G_end[:, :, None] - G), vc)
        return S, o

    S, o = lax.scan(step, s0, (split(q), split(k), split(v), split(log_f)))
    return jnp.moveaxis(o, 0, 2).reshape(B, H, T, -1), S

def hgrn_readout(o, zg, norm_g):
    B, H, T, _ = o.shape
    o = rms_norm(o, norm_g).transpose(0, 2, 1, 3).reshape(B, T, HG_WIDTH)
    return o * jax.nn.sigmoid(zg.astype(jnp.float32))

def cmp_partials(k, w1):
    B, T, G, D = k.shape
    n_sub = T // CMP_STRIDE
    ks = k[:, :n_sub * CMP_STRIDE].reshape(B, n_sub, CMP_STRIDE, G, D)
    return jnp.einsum('bnpgd,rpdh->rbngh', ks, w1.reshape(CMP_RATIO, CMP_STRIDE, D, CMP_HIDDEN))

def cmp_finish(a, b1, w2, b2):
    n_cmp = a.shape[2] - CMP_RATIO + 1
    h = b1 + sum(a[r, :, r:r + n_cmp] for r in range(CMP_RATIO))
    return jnp.einsum('bngh,hd->bngd', jax.nn.gelu(h), w2) + b2

def nsa_cmp_attend(q, qpos, kc, vc, slopes):
    B, Tq = q.shape[:2]
    n_cmp = kc.shape[1]
    qg = q.reshape(B, Tq, NSA_KV_HEADS, NSA_HPG, NSA_HD)
    s = jnp.einsum('btgjd,bcgd->bgjtc', qg, kc).astype(jnp.float32) * NSA_HD ** -0.5
    kend = jnp.arange(n_cmp) * CMP_STRIDE + CMP_BLOCK - 1
    dist = qpos[:, None] - kend[None, :]
    p = masked_softmax(s - slopes[:, :, None, None] * dist.astype(jnp.float32), dist >= 0)
    o = jnp.einsum('bgjtc,bcgd->btgjd', p.astype(vc.dtype), vc).reshape(B, Tq, NSA_HEADS, NSA_HD)
    return o, p

def cmp_to_slc(n_cmp, n_slc):
    cs = np.arange(n_cmp)[:, None] * CMP_STRIDE
    ss = np.arange(n_slc)[None, :] * SEL_BLOCK
    shared = np.clip(np.minimum(cs + CMP_BLOCK, ss + SEL_BLOCK) - np.maximum(cs, ss), 0, None)
    return jnp.asarray(shared / CMP_STRIDE, jnp.float32)

def nsa_select(p_cmp, qpos, n_slc):
    n_cmp = p_cmp.shape[-1]
    imp = jnp.einsum('bgjtc,cn->bgtn', p_cmp, cmp_to_slc(n_cmp, n_slc))
    blk = jnp.arange(n_slc)
    elig = (blk * SEL_BLOCK)[None, :] <= qpos[:, None]
    force = (blk[None, :] == (qpos // SEL_BLOCK)[:, None]) | (blk == 0)[None, :]
    imp = jnp.where(force, jnp.inf, jnp.where(elig, imp, -jnp.inf))
    return lax.top_k(imp, min(N_SEL, n_slc))[1]

def nsa_slc_attend(q, qpos, kpos, kg, vg, slopes):
    B, Tq = q.shape[:2]
    qg = q.reshape(B, Tq, NSA_KV_HEADS, NSA_HPG, NSA_HD)
    s = jnp.einsum('btgjd,bgtnsd->bgjtns', qg, kg).astype(jnp.float32) * NSA_HD ** -0.5
    dist = qpos[None, None, :, None, None] - kpos
    s = s - slopes[None, :, :, None, None, None] * dist[:, :, None].astype(jnp.float32)
    shp = s.shape
    mask = (dist >= 0).reshape(B, NSA_KV_HEADS, 1, Tq, -1)
    p = masked_softmax(s.reshape(*shp[:4], -1), mask).reshape(shp)
    o = jnp.einsum('bgjtns,bgtnsd->btgjd', p.astype(vg.dtype), vg)
    return o.reshape(B, Tq, NSA_HEADS, NSA_HD)

def nsa_win_attend(q, qpos, k, v, kpos, slopes):
    B, Tq = q.shape[:2]
    qg = q.reshape(B, Tq, NSA_KV_HEADS, NSA_HPG, NSA_HD)
    s = jnp.einsum('btgjd,bsgd->bgjts', qg, k).astype(jnp.float32) * NSA_HD ** -0.5
    dist = qpos[:, None] - kpos[None, :]
    mask = (dist >= 0) & (dist < WINDOW) & (kpos >= 0)[None, :]
    p = masked_softmax(s - slopes[:, :, None, None] * dist.astype(jnp.float32), mask)
    o = jnp.einsum('bgjts,bsgd->btgjd', p.astype(v.dtype), v)
    return o.reshape(B, Tq, NSA_HEADS, NSA_HD)

def prompt_slc(q, pos, idx, k, v, slopes):
    B, T = q.shape[:2]
    nb = T // SEL_Q_BLOCK
    qb = q.reshape(B, nb, SEL_Q_BLOCK, NSA_HEADS, NSA_HD).swapaxes(0, 1)
    ib = idx.reshape(B, NSA_KV_HEADS, nb, SEL_Q_BLOCK, -1).transpose(2, 0, 1, 3, 4)
    pb = pos.reshape(nb, SEL_Q_BLOCK)
    bi = jnp.arange(B)[:, None, None, None, None]
    gi = jnp.arange(NSA_KV_HEADS)[None, :, None, None, None]

    def one(args):
        qq, ii, pp = args
        kpos = ii[..., None] * SEL_BLOCK + jnp.arange(SEL_BLOCK)
        return nsa_slc_attend(qq, pp, kpos, k[bi, kpos, gi], v[bi, kpos, gi], slopes)

    o = lax.map(one, (qb, ib, pb))
    return o.swapaxes(0, 1).reshape(B, T, NSA_HEADS, NSA_HD)

def prompt_win(q, k, v, slopes):
    B, T = q.shape[:2]
    nb = T // WIN_Q_BLOCK
    span = WINDOW + WIN_Q_BLOCK
    pad = ((0, 0), (WINDOW, 0), (0, 0), (0, 0))
    kp, vp = jnp.pad(k, pad), jnp.pad(v, pad)
    qb = q.reshape(B, nb, WIN_Q_BLOCK, NSA_HEADS, NSA_HD).swapaxes(0, 1)

    def one(args):
        i, qq = args
        start = i * WIN_Q_BLOCK
        kk = lax.dynamic_slice_in_dim(kp, start, span, axis=1)
        vv = lax.dynamic_slice_in_dim(vp, start, span, axis=1)
        qpos = start + jnp.arange(WIN_Q_BLOCK)
        kpos = start - WINDOW + jnp.arange(span)
        return nsa_win_attend(qq, qpos, kk, vv, kpos, slopes)

    o = lax.map(one, (jnp.arange(nb), qb))
    return o.swapaxes(0, 1).reshape(B, T, NSA_HEADS, NSA_HD)

def gather_paged(pool, page_table, new, kpos):
    B = new.shape[0]
    bi = jnp.arange(B)[:, None, None, None, None]
    gi = jnp.arange(NSA_KV_HEADS)[None, :, None, None, None]
    page = page_table[bi, jnp.clip(kpos // PAGE_SIZE, 0, page_table.shape[1] - 1)]
    old = pool[page, kpos % PAGE_SIZE, gi]
    fresh = new[bi, jnp.clip(kpos - PAST_LEN, 0, new.shape[1] - 1), gi]
    return jnp.where((kpos < PAST_LEN)[..., None], old, fresh)

def nsa_combine(zgate, o_cmp, o_slc, o_win):
    B, T = zgate.shape[:2]
    g = jax.nn.sigmoid(zgate.astype(jnp.float32)).reshape(B, T, NSA_HEADS, 3, 1)
    o = g[:, :, :, 0] * o_cmp + g[:, :, :, 1] * o_slc + g[:, :, :, 2] * o_win
    return o.reshape(B, T, NSA_WIDTH)

def mem_attend(x, mem_k, mem_v, w_q, w_o):
    B, T, _ = x.shape
    q = (x @ w_q).reshape(B, T, MEM_HEADS, MEM_HD)
    s = jnp.einsum('bthd,bmhd->bhtm', q, mem_k).astype(jnp.float32) * MEM_HD ** -0.5
    p = jax.nn.softmax(s, axis=-1).astype(mem_v.dtype)
    o = jnp.einsum('bhtm,bmhd->bthd', p, mem_v).reshape(B, T, D_MODEL)
    return o @ w_o

def peer_block(x, w_q, sub_keys, u_tab, v_tab):
    n = x.shape[0]
    qh = (x @ w_q).reshape(n, PEER_HEADS, 2, PEER_KEY_DIM)
    s = jnp.einsum('nhcd,hckd->nhck', qh, sub_keys).astype(jnp.float32)
    s1, i1 = lax.top_k(s[:, :, 0], PEER_TOPK)
    s2, i2 = lax.top_k(s[:, :, 1], PEER_TOPK)
    cand = (s1[..., :, None] + s2[..., None, :]).reshape(n, PEER_HEADS, PEER_TOPK * PEER_TOPK)
    cidx = (i1[..., :, None] * PEER_NKEYS + i2[..., None, :]).reshape(n, PEER_HEADS, PEER_TOPK * PEER_TOPK)
    top_s, j = lax.top_k(cand, PEER_TOPK)
    e = jnp.take_along_axis(cidx, j, axis=-1)
    gate = jax.nn.softmax(top_s, axis=-1)
    h = jax.nn.gelu(jnp.einsum('nd,nhkd->nhk', x, u_tab[e]).astype(jnp.float32))
    return jnp.einsum('nhk,nhkd->nd', (gate * h).astype(x.dtype), v_tab[e])

def peer(x, w_q, sub_keys, u_tab, v_tab):
    B, T, D = x.shape
    n = B * T
    nb = -(-n // PEER_TOKEN_BLOCK)
    xb = jnp.pad(x.reshape(n, D), ((0, nb * PEER_TOKEN_BLOCK - n), (0, 0))).reshape(nb, PEER_TOKEN_BLOCK, D)
    y = lax.map(lambda xx: peer_block(xx, w_q, sub_keys, u_tab, v_tab), xb)
    return y.reshape(nb * PEER_TOKEN_BLOCK, D)[:n].reshape(B, T, D)

def trunk_tail(x, o_h, o_n, mem_k, mem_v, p):
    mix = jnp.concatenate([o_h, o_n], axis=-1).astype(x.dtype) @ p['w_out']
    x = layer_norm(DN_ALPHA * x + mix, p['ln1_g'], p['ln1_b'])
    x = layer_norm(DN_ALPHA * x + mem_attend(x, mem_k, mem_v, p['w_mem_q'], p['w_mem_o']), p['ln2_g'], p['ln2_b'])
    x = layer_norm(DN_ALPHA * x + peer(x, p['peer_w_q'], p['peer_sub_keys'], p['peer_u'], p['peer_v']),
                   p['ln3_g'], p['ln3_b'])
    return x

def prompt_layer(x, mem, lb, slopes, p):
    B, T, _ = x.shape
    hq, hf, hi, hg, nq, kc, vc, ks, vs, kw, vw, ng = jnp.split(x @ p['w_in'], IN_OFFSETS, axis=-1)
    q_h, k_h, v_h, lf_h = hgrn_features(hq, hf, hi, lb)
    s0 = jnp.zeros((B, HG_HEADS, HG_DK, HG_DV), jnp.float32)
    o_h, s_h = hgrn_recurrence(q_h, k_h, v_h, lf_h, s0, HG_CHUNK)
    o_h = hgrn_readout(o_h, hg, p['hgrn_norm_g'])
    q = nq.reshape(B, T, NSA_HEADS, NSA_HD)
    kc, vc, ks, vs, kw, vw = (a.reshape(B, T, NSA_KV_HEADS, NSA_HD) for a in (kc, vc, ks, vs, kw, vw))
    pos = jnp.arange(T)
    kc_blk = cmp_finish(cmp_partials(kc, p['cmp_k_w1']), p['cmp_k_b1'], p['cmp_k_w2'], p['cmp_k_b2'])
    vc_blk = cmp_finish(cmp_partials(vc, p['cmp_v_w1']), p['cmp_v_b1'], p['cmp_v_w2'], p['cmp_v_b2'])
    o_c, p_c = nsa_cmp_attend(q, pos, kc_blk, vc_blk, slopes)
    idx = nsa_select(p_c, pos, -(-T // SEL_BLOCK))
    o_s = prompt_slc(q, pos, idx, ks, vs, slopes)
    o_w = prompt_win(q, kw, vw, slopes)
    o_n = nsa_combine(ng, o_c, o_s, o_w)
    mem_k = (mem @ p['w_mem_k']).reshape(B, N_MEM, MEM_HEADS, MEM_HD)
    mem_v = (mem @ p['w_mem_v']).reshape(B, N_MEM, MEM_HEADS, MEM_HD)
    y = trunk_tail(x, o_h, o_n, mem_k, mem_v, p)
    n_win = min(WINDOW, T)
    return y, (kc, vc, ks, vs, kw[:, T - n_win:], vw[:, T - n_win:], s_h, mem_k, mem_v)

def sample_layer(x, pool_kc, pool_vc, pool_ks, pool_vs, win_k, win_v, s_prev, mem_k, mem_v,
                 page_table, lb, slopes, p):
    B, T, _ = x.shape
    hq, hf, hi, hg, nq, kc, vc, ks, vs, kw, vw, ng = jnp.split(x @ p['w_in'], IN_OFFSETS, axis=-1)
    q_h, k_h, v_h, lf_h = hgrn_features(hq, hf, hi, lb)
    o_h, s_h = hgrn_recurrence(q_h, k_h, v_h, lf_h, s_prev.astype(jnp.float32), T)
    o_h = hgrn_readout(o_h, hg, p['hgrn_norm_g'])
    q = nq.reshape(B, T, NSA_HEADS, NSA_HD)
    kc, vc, ks, vs, kw, vw = (a.reshape(B, T, NSA_KV_HEADS, NSA_HD) for a in (kc, vc, ks, vs, kw, vw))
    pos = PAST_LEN + jnp.arange(T)
    n_pages = page_table.shape[1]

    def cmp_full(pool, new, w1, b1, w2, b2):
        past = pool[page_table].reshape(B, n_pages * PAGE_SIZE, NSA_KV_HEADS, NSA_HD)
        a = jnp.concatenate([cmp_partials(past, w1), cmp_partials(new, w1)], axis=2)
        return cmp_finish(a, b1, w2, b2)

    kc_blk = cmp_full(pool_kc, kc, p['cmp_k_w1'], p['cmp_k_b1'], p['cmp_k_w2'], p['cmp_k_b2'])
    vc_blk = cmp_full(pool_vc, vc, p['cmp_v_w1'], p['cmp_v_b1'], p['cmp_v_w2'], p['cmp_v_b2'])
    o_c, p_c = nsa_cmp_attend(q, pos, kc_blk, vc_blk, slopes)
    idx = nsa_select(p_c, pos, -(-(PAST_LEN + T) // SEL_BLOCK))
    kpos = idx[..., None] * SEL_BLOCK + jnp.arange(SEL_BLOCK)
    o_s = nsa_slc_attend(q, pos, kpos, gather_paged(pool_ks, page_table, ks, kpos),
                         gather_paged(pool_vs, page_table, vs, kpos), slopes)
    n_buf = win_k.shape[1]
    kpos_w = PAST_LEN - n_buf + jnp.arange(n_buf + T)
    o_w = nsa_win_attend(q, pos, jnp.concatenate([win_k, kw], axis=1),
                         jnp.concatenate([win_v, vw], axis=1), kpos_w, slopes)
    o_n = nsa_combine(ng, o_c, o_s, o_w)
    y = trunk_tail(x, o_h, o_n, mem_k, mem_v, p)
    return y, (kc, vc, ks, vs, kw, vw, s_h)

def setup_inputs(seed: int = 0) -> dict:
    key = jax.random.key(seed)
    ks = list(jax.random.split(key, 48))

    def nrm(shape, scale=1.0):
        return jax.random.normal(ks.pop(), shape, jnp.float32) * scale

    L = DEPTH
    n_pages = PAST_LEN // PAGE_SIZE
    n_phys = (5 * DEC_BATCH * n_pages) // 4
    win_buf = min(WINDOW, PAST_LEN)
    pool_shape = (L, n_phys, PAGE_SIZE, NSA_KV_HEADS, NSA_HD)
    win_shape = (L, DEC_BATCH, win_buf, NSA_KV_HEADS, NSA_HD)
    memc_shape = (L, DEC_BATCH, N_MEM, MEM_HEADS, MEM_HD)
    col_scale = jnp.concatenate([jnp.full((n,), DN_BETA if v else 1.0, jnp.float32)
                                 for n, v in zip(IN_SIZES, IN_IS_VALUE)])
    d_inv = D_MODEL ** -0.5
    inputs = {
        'x_prompt': nrm((BATCH, SEQ, D_MODEL)),
        'x_sample': nrm((DEC_BATCH, DEC_SEQ, D_MODEL)),
        'cache_k_cmp': nrm(pool_shape),
        'cache_v_cmp': nrm(pool_shape, DN_BETA),
        'cache_k_slc': nrm(pool_shape),
        'cache_v_slc': nrm(pool_shape, DN_BETA),
        'cache_k_win': nrm(win_shape),
        'cache_v_win': nrm(win_shape, DN_BETA),
        'state_hgrn': nrm((L, DEC_BATCH, HG_HEADS, HG_DK, HG_DV), 0.5),
        'cache_mem_k': nrm(memc_shape),
        'cache_mem_v': nrm(memc_shape, DN_BETA),
        'page_table': jax.random.permutation(ks.pop(), n_phys)[:DEC_BATCH * n_pages]
                         .reshape(DEC_BATCH, n_pages).astype(jnp.int32),
        'mem_prompt': nrm((BATCH, N_MEM, D_MODEL)),
        'w_in': nrm((L, D_MODEL, IN_COLS), d_inv) * col_scale,
        'hgrn_lb_logits': nrm((DEPTH + 1, HG_HEADS * HG_DK)),
        'hgrn_norm_g': 1.0 + nrm((L, HG_DV), 0.02),
        'cmp_k_w1': nrm((L, CMP_BLOCK, NSA_HD, CMP_HIDDEN), (CMP_BLOCK * NSA_HD) ** -0.5),
        'cmp_k_b1': nrm((L, CMP_HIDDEN), 0.02),
        'cmp_k_w2': nrm((L, CMP_HIDDEN, NSA_HD), CMP_HIDDEN ** -0.5),
        'cmp_k_b2': nrm((L, NSA_HD), 0.02),
        'cmp_v_w1': nrm((L, CMP_BLOCK, NSA_HD, CMP_HIDDEN), (CMP_BLOCK * NSA_HD) ** -0.5),
        'cmp_v_b1': nrm((L, CMP_HIDDEN), 0.02),
        'cmp_v_w2': nrm((L, CMP_HIDDEN, NSA_HD), CMP_HIDDEN ** -0.5),
        'cmp_v_b2': nrm((L, NSA_HD), 0.02),
        'w_out': nrm((L, MIX_WIDTH, D_MODEL), MIX_WIDTH ** -0.5 * DN_BETA),
        'ln1_g': 1.0 + nrm((L, D_MODEL), 0.02),
        'ln1_b': nrm((L, D_MODEL), 0.02),
        'w_mem_q': nrm((L, D_MODEL, D_MODEL), d_inv),
        'w_mem_k': nrm((L, D_MODEL, D_MODEL), d_inv),
        'w_mem_v': nrm((L, D_MODEL, D_MODEL), d_inv * DN_BETA),
        'w_mem_o': nrm((L, D_MODEL, D_MODEL), d_inv * DN_BETA),
        'ln2_g': 1.0 + nrm((L, D_MODEL), 0.02),
        'ln2_b': nrm((L, D_MODEL), 0.02),
        'peer_w_q': nrm((L, D_MODEL, PEER_HEADS * 2 * PEER_KEY_DIM), d_inv),
        'peer_sub_keys': nrm((L, PEER_HEADS, 2, PEER_NKEYS, PEER_KEY_DIM), PEER_KEY_DIM ** -0.5),
        'peer_u': nrm((L, PEER_EXPERTS, D_MODEL), d_inv),
        'peer_v': nrm((L, PEER_EXPERTS, D_MODEL), DN_BETA),
        'ln3_g': 1.0 + nrm((L, D_MODEL), 0.02),
        'ln3_b': nrm((L, D_MODEL), 0.02),
    }
    return inputs

def reference(x_prompt, x_sample, cache_k_cmp, cache_v_cmp, cache_k_slc, cache_v_slc, cache_k_win, cache_v_win,
              state_hgrn, cache_mem_k, cache_mem_v, page_table, mem_prompt, w_in, hgrn_lb_logits, hgrn_norm_g,
              cmp_k_w1, cmp_k_b1, cmp_k_w2, cmp_k_b2, cmp_v_w1, cmp_v_b1, cmp_v_w2, cmp_v_b2, w_out, ln1_g, ln1_b,
              w_mem_q, w_mem_k, w_mem_v, w_mem_o, ln2_g, ln2_b, peer_w_q, peer_sub_keys, peer_u, peer_v,
              ln3_g, ln3_b):
    slopes = alibi_slopes()
    lb_all = jnp.cumsum(jax.nn.softmax(hgrn_lb_logits.astype(jnp.float32), axis=0), axis=0)
    y_prompt, y_sample = x_prompt, x_sample
    new_p, new_s = [], []
    for layer in range(DEPTH):
        p = {'w_in': w_in[layer], 'hgrn_norm_g': hgrn_norm_g[layer],
             'cmp_k_w1': cmp_k_w1[layer], 'cmp_k_b1': cmp_k_b1[layer],
             'cmp_k_w2': cmp_k_w2[layer], 'cmp_k_b2': cmp_k_b2[layer],
             'cmp_v_w1': cmp_v_w1[layer], 'cmp_v_b1': cmp_v_b1[layer],
             'cmp_v_w2': cmp_v_w2[layer], 'cmp_v_b2': cmp_v_b2[layer],
             'w_out': w_out[layer], 'ln1_g': ln1_g[layer], 'ln1_b': ln1_b[layer],
             'w_mem_q': w_mem_q[layer], 'w_mem_k': w_mem_k[layer], 'w_mem_v': w_mem_v[layer],
             'w_mem_o': w_mem_o[layer], 'ln2_g': ln2_g[layer], 'ln2_b': ln2_b[layer],
             'peer_w_q': peer_w_q[layer], 'peer_sub_keys': peer_sub_keys[layer],
             'peer_u': peer_u[layer], 'peer_v': peer_v[layer], 'ln3_g': ln3_g[layer], 'ln3_b': ln3_b[layer]}
        y_prompt, st_p = prompt_layer(y_prompt, mem_prompt, lb_all[layer], slopes, p)
        y_sample, st_s = sample_layer(y_sample, cache_k_cmp[layer], cache_v_cmp[layer], cache_k_slc[layer],
                                      cache_v_slc[layer], cache_k_win[layer], cache_v_win[layer],
                                      state_hgrn[layer], cache_mem_k[layer], cache_mem_v[layer],
                                      page_table, lb_all[layer], slopes, p)
        new_p.append(st_p)
        new_s.append(st_s)
    (p_k_cmp, p_v_cmp, p_k_slc, p_v_slc, p_k_win, p_v_win, p_state_hgrn, p_mem_k, p_mem_v) = (
        jnp.stack(a) for a in zip(*new_p))
    (s_k_cmp, s_v_cmp, s_k_slc, s_v_slc, s_k_win, s_v_win, s_state_hgrn) = (
        jnp.stack(a) for a in zip(*new_s))
    return (y_prompt, y_sample, p_k_cmp, p_v_cmp, p_k_slc, p_v_slc, p_k_win, p_v_win, p_state_hgrn,
            p_mem_k, p_mem_v, s_k_cmp, s_v_cmp, s_k_slc, s_v_slc, s_k_win, s_v_win, s_state_hgrn)


_drawn_inputs = setup_inputs


def setup_inputs(seed=0):
    import zlib

    import numpy as np

    out = dict(_drawn_inputs(seed))
    spreads = {}
    factors = {'hgrn_norm_g': 3.241,
     'cmp_k_b1': 159.919,
     'cmp_k_b2': 200.0,
     'cmp_v_b1': 4.734,
     'cmp_v_b2': 2.827,
     'ln3_g': 24.806,
     'ln3_b': 24.272}
    for name, (base, spread) in spreads.items():
        noise = np.random.default_rng([zlib.crc32(name.encode()), seed]).standard_normal(out[name].shape)
        drawn = base * np.exp(spread * noise) if base else spread * noise
        out[name] = __import__('jax').numpy.asarray(drawn.astype(out[name].dtype))
    for name, factor in factors.items():
        out[name] = (out[name] * factor).astype(out[name].dtype)
    return out
```

```python
from contextlib import ExitStack

import numpy as np
import concourse.bass as bass
from concourse import mybir

ALU = mybir.AluOpType
ACT = mybir.ActivationFunctionType
F32 = mybir.dt.float32
I32 = mybir.dt.int32
U32 = mybir.dt.uint32
AX = mybir.AxisListType.X

P = 128
D = 1024
KC = D // P
T_PROMPT, N_SAMPLE, STEPS = 256, 8, 4
TOK = T_PROMPT + N_SAMPLE * STEPS
TILES = [(0, P), (P, P), (2 * P, TOK - 2 * P)]
ZC = 3352
HQ, HF, HI, HG, NQ, KCC, VCC, KSC, VSC, KWC, VWC, NG = (
    0, 512, 1024, 1536, 2048, 2560, 2688, 2816, 2944, 3072, 3200, 3328)
H = 4
CH = 32
NCH = T_PROMPT // CH
ALPHA = 2.0 ** 0.25
EPS = 1e-5
NEG = -1e30
BIG = -1e33
SLOPES = [2.0 ** -(h + 1) for h in range(8)]
PAST, PAGE = 1024, 128
WIN = 512
NCB = 63
NCP = 15
GW = 512
WG_IN = [(i * GW, min(GW, ZC - i * GW)) for i in range(7)]
NSUBS = 2
GRP = 16
NGRP = 18


def const_table():
    parts = {}
    p = np.arange(P)
    parts["ident"] = np.eye(P)
    s = np.arange(256)
    d = s[None, :] - 128 - p[:, None]
    parts["dist"] = np.where(d <= 0, d, BIG)
    c = np.arange(NCP)
    bias = np.zeros((P, 2, 8, NCP)); mask = np.zeros((P, 2, 8, NCP))
    for t in range(2):
        dd = 16 * c[None, :] + 31 - (p[:, None] + 128 * t)
        for h in range(8):
            bias[:, t, h] = np.where(dd <= 0, dd * SLOPES[h], NEG)
            mask[:, t, h] = dd <= 0
    parts["cbias"] = bias; parts["cmask"] = mask
    b4, g, j, t = p // 32, p // 16 % 2, p // 4 % 4, p % 4
    slope = np.array(SLOPES)[g * 4 + j][:, None]
    qpos = (PAST + t)[:, None]
    pos = 8 * s[None, :128] + np.arange(8)[:, None]
    parts["bsel"] = slope * (pos.reshape(1, -1) - qpos)
    posw = (PAST - WIN + 4 * s[None, :128] + np.arange(4)[:, None]).reshape(1, -1)
    dw = qpos - posw
    parts["bwin"] = np.where(dw < WIN, -slope * dw, NEG)
    fr = np.zeros((P, 2, 32))
    kb, kt = np.arange(32) // 4, np.arange(32) % 4
    for u in range(2):
        ok = (kb[None] == (4 * u + b4)[:, None]) & (kt[None] <= t[:, None])
        fr[:, u] = np.where(ok, slope * (kt[None] - t[:, None]), NEG)
    parts["bnew"] = fr
    parts["bcmp"] = slope * (16 * np.arange(NCB)[None] + 31 - qpos)
    parts["pblk"] = np.broadcast_to((s[:128] // 8)[None], (P, P))
    parts["blk"] = np.broadcast_to(np.arange(17)[None], (P, 17))
    cs, ss = np.arange(NCB)[:, None] * 16, np.arange(17)[None] * 64
    m = np.zeros((P, 17)); m[:NCB] = np.clip(np.minimum(cs + 32, ss + 64) - np.maximum(cs, ss), 0, None) / 16
    parts["cover"] = m
    parts["jsum"] = (b4[:, None] == b4[None]) & (g[:, None] == g[None]) & (t[:, None] == t[None])
    parts["hmask"] = (p[:, None] // CH == p[None] // CH) & (p[:, None] <= p[None])
    q = np.arange(32)
    hs = np.zeros((P, 32)); hs[:32] = (q[:, None] // 4 == q[None] // 4) & (q[:, None] <= q[None])
    parts["hmask_s"] = hs
    r = np.ones(TOK); r[0:T_PROMPT:CH] = 0; r[T_PROMPT::STEPS] = 0
    parts["keep"] = np.broadcast_to(r[None], (P, TOK))
    parts["bmask"] = np.broadcast_to((q[None] // 4 == np.arange(8)[:, None])[None], (P, 8, 32))
    bt = np.zeros((P, 8)); bt[:32] = q[:, None] // 4 == np.arange(8)[None]
    parts["brow"] = bt
    parts["fold"] = p[:, None] % 32 == q[None]
    toks = 4 * (4 * np.arange(2)[:, None] + b4[None]) + t[None]
    rs = np.zeros((P, 2, P)); rs[:32] = np.arange(32)[:, None, None] == toks[None]
    parts["rowsel"] = rs
    hc = np.arange(24) // 3
    parts["headsel"] = hc[None] == (g * 4 + j)[:, None]
    parts["iota16"] = np.broadcast_to(np.arange(16)[None], (P, 16))
    parts["mod8"] = (p % 8)[:, None]
    parts["mod16"] = (p % 16)[:, None]
    at, n = {}, 0
    cols = []
    for k, v in parts.items():
        v = np.asarray(v, np.float32).reshape(P, -1)
        at[k] = (n, v.shape[1]); n += v.shape[1]
        cols.append(v)
    return np.ascontiguousarray(np.concatenate(cols, 1)), at


CONST_AT = const_table()[1]
NCONST = sum(n for _, n in CONST_AT.values())


def pe_jobs():
    jobs = [("xT", t, c) for t in range(3) for c in range(2)]
    jobs += [("z", g, t) for g in range(len(WG_IN)) for t in range(3)]
    for kv in range(2):
        jobs += [("subT", kv, i, q) for i in range(4) for q in range(4)] + [("subT", kv, 4, 0)]
        jobs += [("hid", kv, 0), ("hid", kv, 1), ("hidp", kv)]
        jobs += [("vc", 0), ("vc", 1), ("vcp",)] if kv else [("kcT",), ("kcTp",)]
    for t in range(3):
        jobs += [("hqT", t), ("hfT", t)]
    jobs += [("att", t) for t in range(3)] + [("kE", t) for t in range(3)] + [("oin", t) for t in range(3)]
    jobs += [("U", c) for c in range(NCH)] + [("ost", t) for t in range(3)] + [("US", b) for b in range(N_SAMPLE)]
    jobs += [("gs", u) for u in range(2)] + [("nqT", t) for t in range(3)] + [("nkT", t) for t in range(3)]
    for t in range(2):
        jobs += [("sc", t, g) for g in range(2)] + [("s", t, br, k) for br in range(2) for k in range(2 * (t + 1))]
        if t == 0:
            jobs += [("oT", k) for k in range(3)]
        jobs += [("pT", t, k) for k in range(4 * (t + 1))] + [("pcT", t, k) for k in range(2)] + [("pv", t)]
    for u in range(2):
        jobs += [("sc4", u)]
        for b in range(4):
            jobs += [("skT", u, b, k) for k in range(3)]
        jobs += [("spcT", u), ("imp", u), ("impj", u)]
        jobs += [("ss", u, 0), ("ss", u, 1), ("sw", u), ("sn", u)]
        jobs += [("spT", u, k) for k in range(4)] + [("spv", u)]
    jobs += [("wo", c, t) for c in range(2) for t in range(3)]
    jobs += [("memT", t, c) for t in range(2) for c in range(2)]
    jobs += [("mk", c, t) for c in range(2) for t in range(2)] + [("mv", c, t) for c in range(2) for t in range(2)]
    jobs += [("x1T", t, c) for t in range(3) for c in range(2)]
    jobs += [("mq", c) for c in range(KC)]
    jobs += [("mkT", 0, q) for q in range(4)]
    for t in range(2):
        jobs += [("ms", t, 0), ("ms", t, 1), ("mpT", t, 0), ("mpT", t, 1), ("mo", t, 0), ("mo", t, 1)]
    for u in range(2):
        for b in range(4):
            jobs += [("mkT", 1 + 4 * u + b, q) for q in range(4)] + [("sms", u, b)]
        jobs += [("smpT", u), ("smo", u)]
    jobs += [("mw", c, t) for c in range(2) for t in range(3)]
    jobs += [("skeyT", q) for q in range(4)] + [("x2T", t, c) for t in range(3) for c in range(2)]
    jobs += [("pq", c) for c in range(16)] + [("ps", t, q) for t in range(3) for q in range(4)]
    jobs += [("yfold", c) for c in range(2)]
    return jobs


JOBS = pe_jobs()
JOB = {k: n for n, k in enumerate(JOBS)}

W_GROUPS = [("w_in", o, n, ("z", i, 2)) for i, (o, n) in enumerate(WG_IN)]
W_GROUPS += [("w_out", c * GW, GW, ("wo", c, 2)) for c in range(2)]
W_GROUPS += [("w_mem_k", c * GW, GW, ("mk", c, 1)) for c in range(2)] + [("w_mem_v", c * GW, GW, ("mv", c, 1)) for c in range(2)]
W_GROUPS += [("w_mem_q", c * GW, GW, ("mq", 4 * c + 3)) for c in range(2)]
W_GROUPS += [("w_mem_o", c * GW, GW, ("mw", c, 2)) for c in range(2)]
W_GROUPS += [("peer_w_q", c * GW, GW, ("pq", 4 * c + 3)) for c in range(4)]
WG = {(name, o // GW): n for n, (name, o, _, _) in enumerate(W_GROUPS)}
W_DMAS = [3 if name == "w_out" else 1 for name, *_ in W_GROUPS]


def w_value(n):
    return 16 * sum(W_DMAS[i] for i in range(n % 2, n + 1, 2))


class Lane:

    def __init__(self, eng, step):
        self.eng, self.step, self.n = eng, step, {}

    def __call__(self, ins, signal=None, wait=True):
        s = signal or self.step
        ins.then_inc(s, 1)
        self.n[id(s)] = self.n.get(id(s), 0) + 1
        if wait:
            self.eng.wait_ge(s, self.n[id(s)])


def layer_kernel(nc, A, O):
    ctx = ExitStack()

    def sem(name):
        return ctx.enter_context(nc.semaphore(name))

    def sb(stack, name, shape, dt=F32):
        return stack.enter_context(nc.sbuf_tensor(name, shape, dt))

    bank_full = [sem(f"bank_full{b}") for b in range(8)]
    bank_free = [sem(f"bank_free{b}") for b in range(8)]
    dve_step, act_step, pool_step = sem("dve_step"), sem("act_step"), sem("pool_step")
    s_const, s_x, s_par = sem("s_const"), sem("s_x"), sem("s_par")
    s_w = [sem(f"s_w{i}") for i in range(2)]
    s_pt, s_idx = sem("s_pt"), sem("s_idx")
    s_sub = [sem(f"s_sub{i}") for i in range(NSUBS)]
    s_sorted = sem("s_sorted")
    s_cw, s_subp, s_stin = sem("s_cw"), sem("s_subp"), sem("s_stin")
    s_kvout, s_mkout, s_out = sem("s_kvout"), sem("s_mkout"), sem("s_out")
    s_lb, s_f, s_lnf, s_g, s_hexp, s_ke, s_ktok, s_vm = (sem("s_" + n) for n in "lb f lnf g hexp ke ktok vm".split())
    s_ms, s_rs, s_sgate, s_otok, s_gates = (sem("s_" + n) for n in "ms rs sgate otok gates".split())
    s_mx, s_exp, s_pn, s_qpad = (sem("s_" + n) for n in "mx exp pn qpad".split())
    s_slk = [sem(f"s_slk{i}") for i in range(2)]
    s_slv = [sem(f"s_slv{i}") for i in range(4)]
    s_cmx, s_cexp, s_cpn, s_smx, s_sexp, s_spn = (sem("s_" + n) for n in "cmx cexp cpn smx sexp spn".split())
    s_end = {k: (sem(f"s_dve_end_{k}"), sem(f"s_act_end_{k}")) for k in ("cmp", "hgrn", "nsa", "mem", "peer")}
    s_lnp, s_ln, s_lnv, s_lnr = (sem("s_" + n) for n in "lnp ln lnv lnr".split())
    s_mem = sem("s_mem")
    s_mck = [sem(f"s_mck{i}") for i in range(2)]
    s_mcv = [sem(f"s_mcv{i}") for i in range(4)]
    s_mpad, s_mmx, s_mexp, s_mpn = (sem("s_" + n) for n in "mpad mmx mexp mpn".split())
    s_skey, s_tmx, s_texp, s_route, s_fold, s_y = (sem("s_" + n) for n in "skey tmx texp route fold y".split())
    s_u = [sem(f"s_u{i}") for i in range(8)]
    s_v = [sem(f"s_v{i}") for i in range(GRP)]
    u_free, v_free, h_done, gelu_done, w_done, diag_done, y_free = (
        sem(n) for n in "u_free v_free h_done gelu_done w_done diag_done y_free".split())

    psum = ctx.enter_context(nc.psum_tensor("banks", [P, 8, 512], F32))
    cst = sb(ctx, "cst", [P, NCONST])
    xt = sb(ctx, "xt", [P, 3, D])
    xT = sb(ctx, "xT", [P, KC, TOK])
    mixT = sb(ctx, "mixT", [P, KC, TOK])
    wbuf = sb(ctx, "wbuf", [P, 2, KC, GW])
    par = sb(ctx, "par", [P, 320])
    small = sb(ctx, "small", [P, 192])

    def C(name, *inner):
        o, n = CONST_AT[name]
        v = cst[:, o:o + n]
        if len(inner) == 1:
            return v.rearrange("p (a b) -> p a b", b=inner[0])
        if len(inner) == 2:
            return v.rearrange("p (a b c) -> p a b c", b=inner[0], c=inner[1])
        return v

    ident = C("ident")
    lbl = par[:, 0:8].rearrange("p (a h) -> p a h", h=H)
    lb, omlb, b1, b2k = par[:, 8:12], par[:, 12:16], par[:, 16:18], par[:, 18:19]
    b2v, hng = par[:, 20:148], par[:, 148:276]
    otok = xT[:, :, :].rearrange("p a b -> p (a b)")[:, 0:1536].rearrange("p (t h e) -> p t h e", t=3, h=H)
    PTs = xT[:, :, :].rearrange("p a b -> p (a b)")[:, 0:15 * P].rearrange("p (n r) -> p n r", r=P)
    memT = mixT[:, :, :].rearrange("p a b -> p (a b)")[:, 0:KC * 256].rearrange("p (c m) -> p c m", m=256)

    zs = ExitStack()
    z = sb(zs, "z", [P, 3, ZC])
    kcT = sb(zs, "kcT", [P, N_SAMPLE * NCB + NCP])
    vcS = sb(zs, "vcS", [64, N_SAMPLE, P])
    vcP = sb(zs, "vcP", [16, P])

    st = ExitStack()
    sub = sb(st, "sub", [P, NSUBS, 2048])
    subg = sb(st, "subg", [P, 2048])
    subp = sb(st, "subp", [16, 2048])
    subT = sb(st, "subT", [P, 16, 528])
    w1 = sb(st, "w1", [P, 16, P])
    w2 = sb(st, "w2", [P, 2, 64])
    hid = sb(st, "hid", [P, 2, N_SAMPLE * NCB + NCP])
    pt = sb(st, "pt", [P, 4], I32)
    idx = sb(st, "idx", [P, 4], I32)
    st.close()

    st = ExitStack()
    qT, kT = sb(st, "qT", [P, H, TOK]), sb(st, "kT", [P, H, TOK])
    decay = sb(st, "decay", [P, 4, H, TOK])
    G, e1, e2, e3 = (decay[:, i] for i in range(4))
    vm = decay[:, :, :, :].rearrange("p a h t -> p (a h t)")[:, 0:4096].rearrange("p (b e) -> p b e", e=512)
    dec = sb(st, "dec", [P, H, NCH + N_SAMPLE])
    ktok = sb(st, "ktok", [P, 3, H, P])
    attS = sb(st, "attS", [P, 3, H, P])
    state = sb(st, "state", [P, NCH + 1, H, P])
    sstate = sb(st, "sstate", [P, N_SAMPLE, H, P])
    qGm = sb(st, "qGm", [P, H, N_SAMPLE, 32])
    st.close()

    st = ExitStack()
    qn = sb(st, "qn", [P, 4, TOK])
    kn = sb(st, "kn", [P, 2, TOK])
    qpad = sb(st, "qpad", [P, N_SAMPLE, 32])
    gsm = sb(st, "gsm", [P, 2, 3])
    ptab, sidx = sb(st, "ptab", [P, 8], I32), sb(st, "sidx", [P, 8], I32)
    slk, wk = sb(st, "slk", [P, 2, D]), sb(st, "wk", [P, 2, WIN])
    slv, wv = sb(st, "slv", [P, 4, D]), sb(st, "wv", [P, 4, WIN])
    st2 = ExitStack()
    PS = sb(st2, "PS", [P, 2, 8, 256])
    PTp = sb(st2, "PTp", [P, 32, P])
    PCp = sb(st2, "PCp", [P, 8, NCP])
    PCT = sb(st2, "PCT", [16, 8, P])
    st2.close()
    KT = sb(st, "KT", [P, 4, D + WIN])
    L = sb(st, "L", [P, 1600])
    LC = sb(st, "LC", [P, 2, NCB])
    pcs = sb(st, "pcs", [64, 2, P])
    pen = sb(st, "pen", [P, P])
    st.close()
    zs.close()

    st = ExitStack()
    lnp = sb(st, "lnp", [P, 2, D])
    memp = sb(st, "memp", [P, 2, D])
    mkt, mvt = sb(st, "mkt", [P, 2, D]), sb(st, "mvt", [P, 2, D])
    mqT = sb(st, "mqT", [P, KC, TOK])
    KTm = sb(st, "KTm", [P, 2, KC, 256])
    mck, mcv = sb(st, "mck", [P, 2, 2, D]), sb(st, "mcv", [P, 4, 2, D])
    qpm = sb(st, "qpm", [P, N_SAMPLE, KC, 32])
    Pm = sb(st, "Pm", [P, 4, 256])
    PTm = sb(st, "PTm", [P, 8, P])
    st.close()

    st = ExitStack()
    lnp3 = sb(st, "lnp3", [P, 2, D])
    E_all, W_all = sb(st, "E_all", [P, NGRP, GRP], I32), sb(st, "W_all", [P, NGRP, GRP])
    E_cur, h_cur, g_cur, w_cur = sb(st, "E_cur", [P, 2, GRP], I32), sb(st, "h_cur", [P, GRP]), sb(st, "g_cur", [P, GRP]), sb(st, "w_cur", [P, GRP])
    Y = sb(st, "Y", [P, 3, D])
    x_cur = sb(st, "x_cur", [P, D])
    diag = sb(st, "diag", [P, GRP, P])
    es, ws = sb(st, "es", [32, P], I32), sb(st, "ws", [32, P])
    st2 = ExitStack()
    skey, skT = sb(st2, "skey", [P, 16, P]), sb(st2, "skT", [P, 16, P])
    pqT = sb(st2, "pqT", [P, 16, TOK])
    sc = sb(st2, "sc", [P, 3, 16, P])
    tv, ti, tif = sb(st2, "tv", [P, 16, 16]), sb(st2, "ti", [P, 16, 16], U32), sb(st2, "tif", [P, 16, 16])
    cand = sb(st2, "cand", [P, 8, 256])
    cv, cj = sb(st2, "cv", [P, 8, 16]), sb(st2, "cj", [P, 8, 16], U32)
    ja, jaf, ef = sb(st2, "ja", [P, 2, P], U32), sb(st2, "jaf", [P, 2, P]), sb(st2, "ef", [P, 2, P])
    eqm = sb(st2, "eqm", [P, P, 16])
    texp, tsum = sb(st2, "texp", [P, 8, 16]), sb(st2, "tsum", [P, 16])
    st2.close()
    vbuf = sb(st, "vbuf", [P, GRP, D])
    ubuf = wbuf[:, :, :, :].rearrange("p a b c -> p (a b c)").rearrange("p (s d) -> p s d", d=D)
    st.close()

    block = ctx.enter_context(nc.Block())

    def bank(key):
        return psum[:, JOB[key] % 8, :]

    def filled(eng, key):
        eng.wait_ge(bank_full[JOB[key] % 8], JOB[key] // 8 + 1)

    def evacuated(eng, key):
        eng.wait_ge(bank_free[JOB[key] % 8], JOB[key] // 8 + 1)

    def release(eng, ins, key, wait=False):
        ins.then_inc(bank_free[JOB[key] % 8], 1)
        if wait:
            evacuated(eng, key)

    def copy_out(eng, key, dst, src, scale=None):
        on_act = JOB[key] % 2 == 1
        if (eng is nc.scalar) != on_act:
            return
        filled(eng, key)
        if on_act:
            ins = nc.scalar.activation(dst, src, ACT.Copy, scale=1.0 if scale is None else scale)
        elif scale is None:
            ins = nc.vector.tensor_copy(dst, src)
        else:
            ins = nc.vector.tensor_scalar(dst, src, scale, None, ALU.mult)
        release(eng, ins, key)

    def bc(ap, axis, n):
        v = ap.unsqueeze(axis)
        shape = list(v.shape)
        shape[axis] = n
        return v.to_broadcast(shape)

    def split(ap, n):
        return ap.rearrange("p (a b) -> p a b", b=n)

    def toks(t):
        return TILES[t][0], TILES[t][1]

    def copy_xT(eng, name, ntile=3, dst=None):
        for t in range(ntile):
            t0, n = toks(t)
            for c in range(2):
                d = (xT if dst is None else dst)[:, 4 * c:4 * c + 4, t0:t0 + n]
                copy_out(eng, (name, t, c), d, split(bank((name, t, c)), P)[:, :, 0:n])

    def copy_z(eng):
        for g, (o, w) in enumerate(WG_IN):
            for t in range(3):
                n = toks(t)[1]
                dst, src = z[0:n, t, o:o + w], bank(("z", g, t))[0:n, 0:w]
                if o == NQ:
                    dst, src = dst.rearrange("p (j g d) -> p g j d", j=4, g=2), src.rearrange("p (g j d) -> p g j d", j=4, g=2)
                copy_out(eng, ("z", g, t), dst, src)

    def copy_subT(eng, kv):
        if kv == 1:
            filled(eng, ("hidp", 0))
        for i in range(4):
            for q in range(4):
                copy_out(eng, ("subT", kv, i, q), subT[:, 4 * q:4 * q + 4, i * P:(i + 1) * P], split(bank(("subT", kv, i, q)), P))
        copy_out(eng, ("subT", kv, 4, 0), subT[:, :, 512:528], split(bank(("subT", kv, 4, 0))[:, 0:256], 16))

    def copy_pT(eng, t):
        if t == 1:
            filled(eng, ("pv", 0))
        for k in range(4 * (t + 1)):
            copy_out(eng, ("pT", t, k), PTp[:, 4 * k:4 * k + 4, :], split(bank(("pT", t, k)), P))
        for k in range(2):
            copy_out(eng, ("pcT", t, k), PCT[0:NCP, 4 * k:4 * k + 4, :], split(bank(("pcT", t, k))[0:NCP], P))

    def copy_skT(eng, u):
        if u == 1:
            filled(eng, ("sn", 0))
        for b in range(4):
            for k in range(3):
                copy_out(eng, ("skT", u, b, k), KT[:, b, 512 * k:512 * k + 512], bank(("skT", u, b, k)))

    def copy_spT(eng, u):
        if u == 1:
            filled(eng, ("spv", 0))
        for k in range(3):
            copy_out(eng, ("spT", u, k), PTs[:, 4 * k:4 * k + 4, :], split(bank(("spT", u, k)), P))
        copy_out(eng, ("spT", u, 3), PTs[0:32, 12:14, :], split(bank(("spT", u, 3))[0:32, 0:256], P))

    def copy_mkT(eng, seq):
        if seq >= 2:
            filled(eng, ("ms", 1, 1) if seq == 2 else ("sms", (seq - 3) // 4, (seq - 3) % 4))
        for q in range(4):
            copy_out(eng, ("mkT", seq, q), KTm[:, seq % 2, 2 * q:2 * q + 2, :], split(bank(("mkT", seq, q)), 256))

    def copy_oT(eng, k):
        t0, n = toks(k)
        copy_out(eng, ("oT", k), mixT[:, 0:4, t0:t0 + n], split(bank(("oT", k)), P)[:, :, 0:n])

    def copy_mkv(eng):
        for name, dst in (("mk", mkt), ("mv", mvt)):
            for c in range(2):
                for t in range(2):
                    copy_out(eng, (name, c, t), dst[:, t, GW * c:GW * c + GW], bank((name, c, t)))

    def copy_mq(eng):
        for c in range(KC):
            copy_out(eng, ("mq", c), mqT[:, c, :], bank(("mq", c))[:, 0:TOK], 1.0 / 16)

    def copy_mp(eng, t):
        for k in range(2):
            copy_out(eng, ("mpT", t, k), PTm[:, 4 * k:4 * k + 4, :], split(bank(("mpT", t, k)), P))
        for k in range(2):
            copy_out(eng, ("mo", t, k), mixT[:, 4 * k:4 * k + 4, P * t:P * t + P], split(bank(("mo", t, k)), P))

    def copy_sms(eng, u, b):
        if b == 0:
            filled(eng, ("mpT", 1, 1) if u == 0 else ("smpT", 0))
        copy_out(eng, ("sms", u, b), Pm[32 * b:32 * b + 32, 0, :], bank(("sms", u, b))[32 * b:32 * b + 32, 0:256])

    def copy_smpT(eng, u):
        filled(eng, ("mo", 1, 1) if u == 0 else ("smo", 0))
        copy_out(eng, ("smpT", u), PTm[:, 0:2, :], split(bank(("smpT", u))[:, 0:256], P))

    def copy_skeyT(eng):
        for q in range(4):
            copy_out(eng, ("skeyT", q), skT[:, 4 * q:4 * q + 4, :], split(bank(("skeyT", q)), P))

    def copy_pq(eng):
        for c in range(16):
            copy_out(eng, ("pq", c), pqT[:, c, :], bank(("pq", c))[:, 0:TOK])

    def copy_ps(eng, t):
        n = toks(t)[1]
        for q in range(4):
            copy_out(eng, ("ps", t, q), sc[0:n, t, 4 * q:4 * q + 4, :], split(bank(("ps", t, q)), P)[0:n])

    @block.sync
    def _(sp):
        def weights(n):
            name, o, w, _ = W_GROUPS[n]
            if n >= 2:
                filled(sp, W_GROUPS[n - 2][3])
            dst, src, done = wbuf[:, n % 2], A[name][0], s_w[n % 2]
            if name == "w_out":
                sp.dma_start(dst[:, 0:4, 0:w], src[0:512, o:o + w].rearrange("(c p) n -> p c n", p=P)).then_inc(done, 16)
                for g in range(2):
                    rows = src[512 + 256 * g:768 + 256 * g, o:o + w].rearrange("(j d) n -> d j n", d=64)
                    sp.dma_start(dst[64 * g:64 * g + 64, 4:8, 0:w], rows).then_inc(done, 16)
            else:
                sp.dma_start(dst[:, :, 0:w], src[:, o:o + w].rearrange("(c p) n -> p c n", p=P)).then_inc(done, 16)

        sp.dma_start(cst[:, :], A["consts"]).then_inc(s_const, 16)
        sp.dma_start(xt[:, 0:2, :], A["x_prompt"][0].rearrange("(t p) d -> p t d", p=P)).then_inc(s_x, 16)
        sp.dma_start(xt[0:32, 2, :], A["x_sample"].rearrange("b s d -> (b s) d")).then_inc(s_x, 16)
        weights(0)
        weights(1)
        sp.dma_start(lbl, A["hgrn_lb_logits"].rearrange("a (h p) -> p a h", p=P), allow_slow_non_contiguous=True).then_inc(s_par, 16)
        sp.dma_start(b1[:, 0:1], A["cmp_k_b1"].rearrange("a h -> h a"), allow_slow_non_contiguous=True).then_inc(s_par, 16)
        sp.dma_start(b1[:, 1:2], A["cmp_v_b1"].rearrange("a h -> h a"), allow_slow_non_contiguous=True).then_inc(s_par, 16)
        for g in range(2):
            sp.dma_start(b2k[64 * g:64 * g + 64, :], A["cmp_k_b2"].rearrange("a h -> h a"), allow_slow_non_contiguous=True).then_inc(s_par, 16)
            sp.dma_start(b2v[:, 64 * g:64 * g + 64], A["cmp_v_b2"].to_broadcast([P, 64])).then_inc(s_par, 16)
        sp.dma_start(hng, A["hgrn_norm_g"].to_broadcast([P, P])).then_inc(s_par, 16)
        w1_dram = [A[n][0].rearrange("a d h -> (a d) h").rearrange("(c k) h -> k c h", k=P) for n in ("cmp_k_w1", "cmp_v_w1")]
        sp.dma_start(w2[:, 0, :], A["cmp_k_w2"][0]).then_inc(s_cw, 16)
        sp.dma_start(w2[:, 1, :], A["cmp_v_w2"][0]).then_inc(s_cw, 16)
        sp.dma_start(w1[:, :, :], w1_dram[0]).then_inc(s_cw, 16)
        for n in range(2, 9):
            weights(n)
        evacuated(sp, ("z", 6, 0)); evacuated(sp, ("z", 6, 1)); evacuated(sp, ("z", 6, 2))
        for i, c in enumerate((KCC, VCC, KSC, VSC, KWC, VWC)):
            sp.dma_start(O[2 + i][0, 0].rearrange("(t p) g d -> p t (g d)", p=P), z[:, 0:2, c:c + P]).then_inc(s_kvout, 16)
            sp.dma_start(O[11 + i][0].rearrange("b s g d -> (b s) (g d)"), z[0:32, 2, c:c + P]).then_inc(s_kvout, 16)
            if i < 2:
                sp.wait_ge(s_kvout, 32 * (i + 1))
                if i == 1:
                    filled(sp, ("subT", 0, 4, 0))
                for g in range(2):
                    sp.dma_start(subp[:, 1024 * g:1024 * g + 1024], O[2 + i][0, 0].rearrange("(n s) g d -> n g s d", s=16)[:, g]).then_inc(s_subp, 16)
        filled(sp, ("hidp", 0))
        sp.dma_start(w1[:, :, :], w1_dram[1]).then_inc(s_cw, 16)
        for s in s_end["cmp"]:
            sp.wait_ge(s, 1)
        sp.dma_start(sstate[:, :, :, :], A["state_hgrn"][0].rearrange("b h d e -> d b h e")).then_inc(s_stin, 16)
        evacuated(sp, ("U", NCH - 1))
        sp.dma_start(O[8][0, 0].rearrange("h d e -> d h e"), state[:, NCH]).then_inc(s_out, 16)
        evacuated(sp, ("US", N_SAMPLE - 1))
        sp.dma_start(O[17][0].rearrange("b h d e -> d b h e"), sstate[:, :, :, :]).then_inc(s_out, 16)
        for s in s_end["nsa"]:
            sp.wait_ge(s, 1)
        sp.dma_start(memp[:, :, :], A["mem_prompt"][0].rearrange("(t p) d -> p t d", p=P)).then_inc(s_mem, 16)
        sp.dma_start(lnp[:, 0, :], A["ln1_g"].to_broadcast([P, D])).then_inc(s_lnp, 16)
        sp.dma_start(lnp[:, 1, :], A["ln1_b"].to_broadcast([P, D])).then_inc(s_lnp, 16)
        for n in range(9, 13):
            weights(n)
        for i, (buf, key) in enumerate(((mkt, "mk"), (mvt, "mv"))):
            for c in range(2):
                for t in range(2):
                    evacuated(sp, (key, c, t))
            sp.dma_start(O[9 + i][0, 0].rearrange("(t p) h d -> p t (h d)", p=P), buf[:, :, :]).then_inc(s_mkout, 16)
        weights(13)
        sp.wait_ge(s_ln, 3)
        sp.dma_start(lnp[:, 0, :], A["ln2_g"].to_broadcast([P, D])).then_inc(s_lnp, 16)
        sp.dma_start(lnp[:, 1, :], A["ln2_b"].to_broadcast([P, D])).then_inc(s_lnp, 16)
        for n in range(14, 19):
            weights(n)
        sp.wait_ge(s_ln, 6)
        sp.wait_ge(s_mkout, 32)
        for s in s_end["mem"]:
            sp.wait_ge(s, 1)
        sp.dma_start(skey[:, :, :], A["peer_sub_keys"][0].rearrange("h c k d -> k (h c) d")).then_inc(s_skey, 16)
        sp.dma_start(lnp3[:, 0, :], A["ln3_g"].to_broadcast([P, D])).then_inc(s_lnp, 16)
        sp.dma_start(lnp3[:, 1, :], A["ln3_b"].to_broadcast([P, D])).then_inc(s_lnp, 16)
        weights(19)
        weights(20)
        for q in range(1, 4):
            sp.dma_start(xt[32 * q:32 * q + 32, 2, :], xt[0:32, 2, :]).then_inc(s_fold, 16)
        sp.wait_ge(s_route, 3)
        for q in range(4):
            sp.dma_start(E_all[32 * q:32 * q + 32, 16:18, :], split(es[:, 32 * q:32 * q + 32], GRP)).then_inc(s_fold, 16)
            sp.dma_start(W_all[32 * q:32 * q + 32, 16:18, :], split(ws[:, 32 * q:32 * q + 32], GRP)).then_inc(s_fold, 16)
        sp.wait_ge(s_ln, 9)
        sp.dma_start(O[0][0].rearrange("(t p) d -> p t d", p=P), xt[:, 0:2, :]).then_inc(s_out, 16)
        sp.dma_start(O[1].rearrange("b s d -> (b s) d"), xt[0:32, 2, :]).then_inc(s_out, 16)
        sp.wait_ge(s_out, 64)
        sp.wait_ge(s_kvout, 192)

    @block.gpsimd
    def _(pool):
        def gather(dst, table, index, done):
            return nc.gpsimd.indirect_dma_start(out=dst, out_offset=None, in_=table,
                                                in_offset=bass.IndirectOffsetOnAxis(ap=index, axis=0)).then_inc(done, 16)

        pages = A["page_table"].rearrange("b j -> (b j)").rearrange("(i q) -> q i", q=16)
        for q in range(16):
            nc.gpsimd.dma_start(pt[8 * q:8 * q + 8, :], pages[q:q + 1, :].to_broadcast([8, 4]), allow_slow_non_contiguous=True).then_inc(s_pt, 16)
        pool.wait_ge(s_idx, 1)
        fetches = []
        for kv, cache in enumerate((A["cache_k_cmp"], A["cache_v_cmp"])):
            rows = cache[0].rearrange("n (r s) g d -> (n r) (s g d)", s=16)
            for i in range(4):
                fetches.append((rows, i))
        gather(sub[:, 0, :], fetches[0][0], idx[:, 0:1], s_sub[0])
        for n, (rows, i) in enumerate(fetches):
            if n + 1 < len(fetches):
                gather(sub[:, (n + 1) % NSUBS, :], fetches[n + 1][0], idx[:, fetches[n + 1][1]:fetches[n + 1][1] + 1], s_sub[(n + 1) % NSUBS])
            pool.wait_ge(s_sub[n % NSUBS], 16 * (n // NSUBS + 1))
            if n >= 1:
                filled(pool, ("subT", (n - 1) // 4, (n - 1) % 4, 3))
            nc.gpsimd.tensor_copy(subg[:, :].rearrange("p (g s d) -> p g s d", g=2, s=16),
                                  sub[:, n % NSUBS, :].rearrange("p (s g d) -> p g s d", g=2, s=16)).then_inc(s_sorted, 1)
            pool.wait_ge(s_sorted, n + 1)
        for s in s_end["hgrn"]:
            pool.wait_ge(s, 1)
        pool.wait_ge(s_out, 32)
        pages = A["page_table"].rearrange("b j -> j b")
        for q in range(8):
            nc.gpsimd.dma_start(ptab[16 * q:16 * q + 16, :], pages[q:q + 1, :].to_broadcast([16, 8]), allow_slow_non_contiguous=True).then_inc(s_pt, 16)
        pool.wait_ge(s_idx, 2)
        rk, rv = (A[n][0].rearrange("n (r s) g d -> (n r) (s g d)", s=8) for n in ("cache_k_slc", "cache_v_slc"))
        for b in range(N_SAMPLE):
            u, b4 = b // 4, b % 4
            if b >= 2:
                filled(pool, ("skT", (b - 2) // 4, (b - 2) % 4, 2))
            gather(slk[:, b % 2, :], rk, sidx[:, b:b + 1], s_slk[b % 2])
            nc.gpsimd.dma_start(wk[:, b % 2, :], A["cache_k_win"][0, b].rearrange("(p s) g d -> p (s g d)", s=4)).then_inc(s_slk[b % 2], 16)
            if b == 4:
                filled(pool, ("spv", 0))
            gather(slv[:, b4, :], rv, sidx[:, b:b + 1], s_slv[b4])
            nc.gpsimd.dma_start(wv[:, b4, :], A["cache_v_win"][0, b].rearrange("(p s) g d -> p (s g d)", s=4)).then_inc(s_slv[b4], 16)
        for s in s_end["nsa"]:
            pool.wait_ge(s, 1)
        for b in range(N_SAMPLE):
            if b >= 2:
                filled(pool, ("mkT", b - 1, 3))
            nc.gpsimd.dma_start(mck[:, b % 2, :, :], A["cache_mem_k"][0, b].rearrange("(p i) h d -> p i (h d)", i=2)).then_inc(s_mck[b % 2], 16)
            if b == 4:
                filled(pool, ("smo", 0))
            nc.gpsimd.dma_start(mcv[:, b % 4, :, :], A["cache_mem_v"][0, b].rearrange("(p i) h d -> p i (h d)", i=2)).then_inc(s_mcv[b % 4], 16)
        pool.wait_ge(s_route, 3)
        pool.wait_ge(s_fold, 16 * 11)
        for s in s_end["peer"]:
            pool.wait_ge(s, 1)
        waited, u_count, v_count = (pool.alloc_register(n) for n in ("waited", "u_count", "v_count"))
        pool.reg_mov(waited, 0)
        pool.reg_mov(u_count, 1)
        pool.reg_mov(v_count, 1)
        with pool.Fori(0, NGRP // 2) as pair:
            for odd in range(2):
                g = pair * 2 + odd
                nc.gpsimd.tensor_copy(E_cur[:, odd, :], E_all[:, bass.ds(g, 1), :].rearrange("p a k -> p (a k)")).then_inc(pool_step, 1)
                pool.wait_ge(pool_step, g + 1)
                for k in range(GRP):
                    pool.wait_ge(u_free, u_count)
                    pool.reg_add(waited, waited, 1)
                    pool.reg_add(u_count, u_count, 1)
                    gather(ubuf[:, k % 8, :], A["peer_u"][0], E_cur[:, odd, k:k + 1], s_u[k % 8])
                for k in range(GRP):
                    pool.wait_ge(v_free, v_count)
                    pool.reg_add(waited, waited, 1)
                    pool.reg_add(v_count, v_count, 1)
                    gather(vbuf[:, k, :], A["peer_v"][0], E_cur[:, odd, k:k + 1], s_v[k])

    @block.scalar
    def _(act):
        S = Lane(act, act_step)
        copy_xT(act, "xT")
        copy_z(act)
        act.wait_ge(s_lb, 1)
        S(nc.scalar.activation(lb, small[:, 0:4], ACT.Sigmoid), s_lb)
        act.wait_ge(s_par, 16 * 8)
        for kv in range(2):
            copy_subT(act, kv)
            if kv == 1:
                filled(act, ("kcTp",))
            for g in range(2):
                filled(act, ("hid", kv, g))
                release(act, nc.scalar.activation(hid[:, g, 0:504], bank(("hid", kv, g))[:, 0:504], ACT.Gelu_apprx_tanh,
                                                  bias=b1[:, kv:kv + 1]), ("hid", kv, g))
            filled(act, ("hidp", kv))
            release(act, nc.scalar.activation(hid[:, :, 504:519], split(bank(("hidp", kv))[:, 0:30], 15), ACT.Gelu_apprx_tanh,
                                              bias=b1[:, kv:kv + 1]), ("hidp", kv), wait=True)
        filled(act, ("vcp",))
        act.sem_inc(s_end["cmp"][1], 1)
        for s in s_end["cmp"]:
            act.wait_ge(s, 1)
        for t in range(3):
            t0, n = toks(t)
            filled(act, ("hfT", t))
            S(nc.scalar.activation(e1[:, :, t0:t0 + n], split(bank(("hfT", t)), P)[:, :, 0:n], ACT.Sigmoid))
            release(act, nc.scalar.activation(kT[:, :, t0:t0 + n], split(bank(("hfT", t)), P)[:, :, 0:n], ACT.Sigmoid, scale=-1.0),
                    ("hfT", t))
        for t, rows in ((slice(0, 2), P), (slice(2, 3), 32)):
            S(nc.scalar.activation(z[0:rows, t, HG:HG + 512], z[0:rows, t, HG:HG + 512], ACT.Sigmoid), s_sgate)
            S(nc.scalar.activation(z[0:rows, t, NG:NG + 24], z[0:rows, t, NG:NG + 24], ACT.Sigmoid), s_gates)
        act.wait_ge(s_f, 1)
        S(nc.scalar.activation(e2, e1, ACT.Ln), s_lnf)
        act.wait_ge(s_g, 1)
        S(nc.scalar.activation(e2, e1, ACT.Exp), wait=False)
        S(nc.scalar.activation(e3, e1, ACT.Exp, scale=-1.0), s_hexp)
        act.wait_ge(s_g, 2)
        S(nc.scalar.activation(G, G, ACT.Exp), wait=False)
        S(nc.scalar.activation(dec[:, :, :], dec[:, :, :], ACT.Exp), wait=False)
        S(nc.scalar.activation(e1, e1, ACT.Exp), s_hexp)
        for t in range(3):
            n = toks(t)[1]
            filled(act, ("kE", t))
            release(act, nc.scalar.copy(ktok[0:n, t], split(bank(("kE", t)), P)[0:n]), ("kE", t))
        evacuated(act, ("xT", 2, 1))
        filled(act, ("z", 6, 2))
        for t in range(3):
            n = toks(t)[1]
            filled(act, ("oin", t))
            release(act, nc.scalar.copy(otok[0:n, t], split(bank(("oin", t)), P)[0:n]), ("oin", t), wait=True)
        act.wait_ge(s_ms, 1)
        S(nc.scalar.activation(small[:, 16:28], small[:, 0:12], ACT.Sqrt), s_rs)
        act.sem_inc(s_end["hgrn"][1], 1)
        for s in s_end["hgrn"]:
            act.wait_ge(s, 1)
        for t in range(3):
            t0, n = toks(t)
            filled(act, ("nqT", t))
            release(act, nc.scalar.mul(qn[:, :, t0:t0 + n], split(bank(("nqT", t)), P)[:, :, 0:n], 0.125), ("nqT", t))
        for t in range(2):
            K = P * (t + 1)
            act.wait_ge(s_mx, 2 * t + 1)
            S(nc.scalar.activation(PCp[:, :, :], PCp[:, :, :], ACT.Exp), s_exp)
            act.wait_ge(s_mx, 2 * t + 2)
            for br in range(2):
                for h in range(8):
                    i = 8 * br + h
                    S(nc.scalar.activation(PS[:, br, h, 0:K], PS[:, br, h, 0:K], ACT.Exp, bias=small[:, i:i + 1],
                                           accum_out=small[:, 16 + i:17 + i]), s_exp if i == 15 else None, wait=(i == 15))
            if t == 0:
                for k in range(3):
                    copy_oT(act, k)
            copy_pT(act, t)
        evacuated(act, ("pv", 1))
        for u in range(2):
            copy_skT(act, u)
            act.wait_ge(s_cmx, u + 1)
            S(nc.scalar.activation(LC[:, 0, :], LC[:, 0, :], ACT.Exp, bias=small[:, 64:65], accum_out=small[:, 65:66]), s_cexp)
            act.wait_ge(s_smx, u + 1)
            S(nc.scalar.activation(L[:, 0:1056], L[:, 0:1056], ACT.Exp, bias=small[:, 72:73], accum_out=small[:, 74:75]), wait=False)
            S(nc.scalar.activation(L[:, 1056:1600], L[:, 1056:1600], ACT.Exp, bias=small[:, 73:74], accum_out=small[:, 75:76]), s_sexp)
            copy_spT(act, u)
        evacuated(act, ("spv", 1))
        act.sem_inc(s_end["nsa"][1], 1)
        for s in s_end["nsa"]:
            act.wait_ge(s, 1)

        def root(k):
            act.wait_ge(s_lnv, k + 1)
            S(nc.scalar.activation(small[:, 104:107], small[:, 100:103], ACT.Sqrt), s_lnr)

        root(0)
        copy_xT(act, "memT", 2, memT)
        copy_mkv(act)
        copy_xT(act, "x1T")
        copy_mq(act)
        copy_mkT(act, 0)
        for t in range(2):
            act.wait_ge(s_mmx, t + 1)
            for h in range(H):
                ins = nc.scalar.activation(Pm[:, h, :], bank(("ms", t, h // 2))[:, 256 * (h % 2):256 * (h % 2) + 256], ACT.Exp,
                                           bias=small[:, 80 + h:81 + h], accum_out=small[:, 84 + h:85 + h])
                if h % 2:
                    release(act, ins, ("ms", t, h // 2))
                else:
                    S(ins, wait=False)
            copy_mp(act, t)
        for u in range(2):
            for b in range(4):
                copy_mkT(act, 1 + 4 * u + b)
                copy_sms(act, u, b)
            act.wait_ge(s_mmx, 3 + u)
            S(nc.scalar.activation(Pm[:, 0, :], Pm[:, 0, :], ACT.Exp, bias=small[:, 80:81], accum_out=small[:, 84:85]), s_mexp)
            copy_smpT(act, u)
        evacuated(act, ("smo", 1))
        act.sem_inc(s_end["mem"][1], 1)
        for s in s_end["mem"]:
            act.wait_ge(s, 1)
        root(1)
        copy_skeyT(act)
        copy_xT(act, "x2T")
        copy_pq(act)
        for t in range(3):
            copy_ps(act, t)
            n = toks(t)[1]
            act.wait_ge(s_tmx, t + 1)
            S(nc.scalar.activation(texp[0:n], texp[0:n], ACT.Exp), s_texp)
        act.sem_inc(s_end["peer"][1], 1)
        with act.Fori(0, NGRP) as g:
            act.wait_ge(h_done, g + 1)
            nc.scalar.activation(g_cur[:, :], h_cur[:, :], ACT.Gelu_apprx_tanh).then_inc(gelu_done, 1)
            act.wait_ge(w_done, g + 1)
            for k in range(GRP):
                act.wait_ge(v_free, GRP * g + k + 1)
                nc.scalar.activation(diag[:, k, :], ident, ACT.Copy, scale=w_cur[:, k:k + 1]).then_inc(diag_done, 1)
        root(2)

    @block.vector
    def _(dve):
        V = Lane(dve, dve_step)
        v = nc.vector

        dve.wait_ge(s_const, 16)
        dve.wait_ge(s_pt, 16 * 16)
        V(v.tensor_scalar(idx[:, :], pt[:, :], 8.0, C("mod8"), ALU.mult, ALU.add), s_idx)
        dve.wait_ge(s_par, 16 * 8)
        V(v.tensor_tensor(small[:, 0:4], lbl[:, 0, :], lbl[:, 1, :], ALU.subtract), s_lb)
        copy_xT(dve, "xT")
        copy_z(dve)
        dve.wait_ge(s_lb, 2)
        V(v.tensor_scalar(omlb, lb, -1.0, 1.0, ALU.mult, ALU.add))
        copy_subT(dve, 0)
        for key, o, w in ((("kcT",), 0, 504), (("kcTp",), 504, NCP)):
            filled(dve, key)
            release(dve, v.tensor_scalar(kcT[:, o:o + w], bank(key)[:, 0:w], b2k, None, ALU.add), key)
        copy_subT(dve, 1)
        for k in range(2):
            filled(dve, ("vc", k))
            release(dve, v.tensor_tensor(vcS[0:NCB, 4 * k:4 * k + 4, :], split(bank(("vc", k))[0:NCB], P), bc(b2v[0:NCB], 1, 4), ALU.add), ("vc", k))
        filled(dve, ("vcp",))
        release(dve, v.tensor_tensor(vcP[0:NCP, :], bank(("vcp",))[0:NCP, 0:P], b2v[0:NCP], ALU.add), ("vcp",), wait=True)
        dve.sem_inc(s_end["cmp"][0], 1)
        for s in s_end["cmp"]:
            dve.wait_ge(s, 1)

        V(v.memset(state[:, 0], 0.0), wait=False)
        for t in range(3):
            t0, n = toks(t)
            filled(dve, ("hqT", t))
            release(dve, v.tensor_copy(qT[:, :, t0:t0 + n], split(bank(("hqT", t)), P)[:, :, 0:n]), ("hqT", t))
        evacuated(dve, ("hfT", 2))
        for h in range(H):
            V(v.tensor_scalar(e1[:, h, :], e1[:, h, :], omlb[:, h:h + 1], lb[:, h:h + 1], ALU.mult, ALU.add), wait=False)
        for h in range(H):
            V(v.tensor_scalar(kT[:, h, :], kT[:, h, :], omlb[:, h:h + 1], None, ALU.mult), s_f if h == 3 else None, wait=(h == 3))
        dve.wait_ge(s_lnf, 1)
        for h in range(H):
            V(v.tensor_tensor_scan(G[:, h, :], C("keep"), e2[:, h, :], 0.0, ALU.mult, ALU.add), wait=(h == 3))
        Gp = G[:, :, 0:T_PROMPT].rearrange("p h (c s) -> p h c s", s=CH)
        Gs = G[:, :, T_PROMPT:TOK].rearrange("p h (b s) -> p h b s", s=STEPS)
        Ep = e1[:, :, 0:T_PROMPT].rearrange("p h (c s) -> p h c s", s=CH)
        Es = e1[:, :, T_PROMPT:TOK].rearrange("p h (b s) -> p h b s", s=STEPS)
        for h in range(H):
            V(v.tensor_tensor(Ep[:, h], Gp[:, h], Gp[:, h, :, CH // 2 - 1:CH // 2].to_broadcast([P, NCH, CH]), ALU.subtract), wait=False)
        V(v.tensor_copy(e1[:, :, T_PROMPT:TOK], G[:, :, T_PROMPT:TOK]), s_g)
        dve.wait_ge(s_hexp, 1)
        V(v.tensor_tensor(e2, qT[:, :, :], e2, ALU.mult), wait=False)
        V(v.tensor_tensor(e3, kT[:, :, :], e3, ALU.mult), s_ke)
        for h in range(H):
            V(v.tensor_tensor(Ep[:, h], Gp[:, h, :, CH - 1:CH].to_broadcast([P, NCH, CH]), Gp[:, h], ALU.subtract), wait=False)
            V(v.tensor_tensor(Es[:, h], Gs[:, h, :, STEPS - 1:STEPS].to_broadcast([P, N_SAMPLE, STEPS]), Gs[:, h], ALU.subtract), wait=False)
        V(v.tensor_copy(dec[:, :, 0:NCH], Gp[:, :, :, CH - 1]), wait=False)
        V(v.tensor_copy(dec[:, :, NCH:], Gs[:, :, :, STEPS - 1]), s_g)
        dve.wait_ge(s_hexp, 2)
        V(v.tensor_tensor(qT[:, :, :], qT[:, :, :], G, ALU.mult), wait=False)
        V(v.tensor_tensor(kT[:, :, :], kT[:, :, :], e1, ALU.mult), s_ke)
        for h in range(H):
            V(v.tensor_tensor(qGm[:, h], C("bmask", 32), bc(qT[:, h, T_PROMPT:TOK], 1, N_SAMPLE), ALU.mult), s_ke if h == 3 else None, wait=(h == 3))
        for t in range(3):
            n = toks(t)[1]
            filled(dve, ("att", t))
            m = C("hmask") if t < 2 else C("hmask_s")[0:32]
            release(dve, v.tensor_tensor(attS[0:n, t, :, 0:n], split(bank(("att", t)), P)[0:n, :, 0:n], bc(m, 1, H), ALU.mult), ("att", t), wait=True)
        for b in range(N_SAMPLE):
            V(v.tensor_scalar(vm[0:32, b, :], z[0:32, 2, HI:HI + 512], C("brow")[0:32, b:b + 1], None, ALU.mult), s_vm, wait=False)
        for c in range(NCH):
            key = ("U", c)
            filled(dve, key)
            for h in range(H):
                ins = v.scalar_tensor_tensor(out=state[:, c + 1, h, :], in0=state[:, c, h, :], scalar=dec[:, h, c:c + 1],
                                             in1=bank(key)[:, P * h:P * h + P], op0=ALU.mult, op1=ALU.add)
                if h < 3:
                    V(ins, wait=False)
                else:
                    release(dve, ins, key, wait=True)
        for t in range(3):
            n = toks(t)[1]
            filled(dve, ("ost", t))
            evacuated(dve, ("oin", t))
            release(dve, v.tensor_tensor(otok[0:n, t], split(bank(("ost", t)), P)[0:n], otok[0:n, t], ALU.add), ("ost", t), wait=True)
        for b in range(N_SAMPLE):
            key = ("US", b)
            filled(dve, key)
            for h in range(H):
                ins = v.scalar_tensor_tensor(out=sstate[:, b, h, :], in0=sstate[:, b, h, :], scalar=dec[:, h, NCH + b:NCH + b + 1],
                                             in1=bank(key)[:, P * h:P * h + P], op0=ALU.mult, op1=ALU.add)
                if h < 3:
                    V(ins, wait=False)
                else:
                    release(dve, ins, key)
        V(v.memset(small[:, 0:12], 1.0))
        parts = ((slice(0, 2), P, 8), (slice(2, 3), 32, 4))

        def heads(x, ts, rows):
            return x[0:rows, ts].rearrange("p t h e -> p (t h) e")

        for ts, rows, nh in parts:
            o, sq, s0 = heads(otok, ts, rows), heads(attS, ts, rows), 4 * ts.start
            V(v.tensor_tensor(sq, o, o, ALU.mult))
            V(v.tensor_reduce(small[0:rows, s0:s0 + nh], sq, AX, ALU.add))
        V(v.tensor_scalar(small[:, 0:12], small[:, 0:12], 1.0 / P, EPS, ALU.mult, ALU.add), s_ms)
        dve.wait_ge(s_rs, 1)
        V(v.reciprocal(small[:, 32:44], small[:, 16:28]))
        dve.wait_ge(s_sgate, 2)
        for ts, rows, nh in parts:
            o, s0 = heads(otok, ts, rows), 4 * ts.start
            V(v.tensor_tensor(o, o, bc(small[0:rows, 32 + s0:32 + s0 + nh], 2, P), ALU.mult))
            V(v.tensor_tensor(o, o, bc(hng[0:rows], 1, nh), ALU.mult))
            for t in range(ts.start, ts.stop):
                V(v.tensor_tensor(otok[0:rows, t].rearrange("p h e -> p (h e)"), otok[0:rows, t].rearrange("p h e -> p (h e)"),
                                  z[0:rows, t, HG:HG + 512], ALU.mult), s_otok)
        dve.sem_inc(s_end["hgrn"][0], 1)
        for s in s_end["hgrn"]:
            dve.wait_ge(s, 1)
        dve.wait_ge(s_out, 32)

        dve.wait_ge(s_pt, 16 * 24)
        V(v.tensor_scalar(sidx[:, :], ptab[:, :], 16.0, C("mod16"), ALU.mult, ALU.add), s_idx)
        V(v.memset(qpad[:, :, :], 0.0))
        for u in range(2):
            filled(dve, ("gs", u))
            release(dve, v.tensor_tensor(small[:, 32:56], bank(("gs", u))[:, 0:24], C("headsel"), ALU.mult), ("gs", u), wait=True)
            V(v.tensor_reduce(gsm[:, u, :], small[:, 32:56].rearrange("p (h c) -> p c h", c=3), AX, ALU.add))
        evacuated(dve, ("nqT", 2))
        for g in range(2):
            rows = slice(64 * g, 64 * g + 64)
            V(v.tensor_copy(qpad[rows].rearrange("p b (g j t) -> p b g j t", g=2, j=4)[:, :, g],
                            qn[rows, :, T_PROMPT:TOK].rearrange("p j (b t) -> p b j t", t=STEPS)), s_qpad)
        for t in range(3):
            t0, n = toks(t)
            filled(dve, ("nkT", t))
            release(dve, v.tensor_copy(kn[:, :, t0:t0 + n], split(bank(("nkT", t))[:, 0:256], P)[:, :, 0:n]), ("nkT", t))
        for t in range(2):
            K = P * (t + 1)
            if t == 1:
                filled(dve, ("pcT", 0, 1))
            for g in range(2):
                key, hs = ("sc", t, g), slice(4 * g, 4 * g + 4)
                filled(dve, key)
                release(dve, v.tensor_tensor(PCp[:, hs, :], split(bank(key)[:, 0:4 * NCP], NCP), C("cbias", 8, NCP)[:, t, hs], ALU.add), key, wait=True)
            V(v.tensor_reduce(small[:, 48:56], PCp[:, :, :], AX, ALU.max))
            V(v.tensor_tensor(PCp[:, :, :], PCp[:, :, :], bc(small[:, 48:56], 2, NCP), ALU.subtract), s_mx)
            dist = C("dist")[:, 256 - K:256] if t == 0 else C("dist")
            per = 4 // (t + 1)
            for br in range(2):
                for k in range(2 * (t + 1)):
                    key = ("s", t, br, k)
                    filled(dve, key)
                    for i in range(per):
                        h = per * k + i
                        ins = v.scalar_tensor_tensor(out=PS[:, br, h, 0:K], in0=dist, scalar=SLOPES[h], in1=bank(key)[:, K * i:K * i + K],
                                                     op0=ALU.mult, op1=ALU.add)
                        if i < per - 1:
                            V(ins, wait=False)
                        else:
                            release(dve, ins, key, wait=(k == 2 * t + 1))
            V(v.tensor_reduce(small[:, 0:16], PS[:, :, :, 0:K].rearrange("p b h k -> p (b h) k"), AX, ALU.max))
            V(v.tensor_scalar(small[:, 0:16], small[:, 0:16], -1.0, None, ALU.mult), s_mx)
            dve.wait_ge(s_exp, 2 * t + 1)
            gate = z[:, t, NG:NG + 24].rearrange("p (h c) -> p c h", c=3)
            dve.wait_ge(s_gates, 2)
            V(v.tensor_reduce(small[:, 48:56], PCp[:, :, :], AX, ALU.add))
            V(v.reciprocal(small[:, 56:64], small[:, 48:56]))
            V(v.tensor_tensor(small[:, 56:64], small[:, 56:64], gate[:, 0], ALU.mult))
            V(v.tensor_tensor(PCp[:, :, :], PCp[:, :, :], C("cmask", 8, NCP)[:, t], ALU.mult))
            V(v.tensor_tensor(PCp[:, :, :], PCp[:, :, :], bc(small[:, 56:64], 2, NCP), ALU.mult))
            dve.wait_ge(s_exp, 2 * t + 2)
            V(v.reciprocal(small[:, 32:48], small[:, 16:32]))
            V(v.tensor_tensor(split(small[:, 32:48], 8), split(small[:, 32:48], 8), gate[:, 1:3], ALU.mult))
            pv_ = PS[:, :, :, 0:K].rearrange("p b h k -> p (b h) k")
            V(v.tensor_tensor(pv_, pv_, bc(small[:, 32:48], 2, K), ALU.mult), s_pn)
            if t == 0:
                for k in range(3):
                    copy_oT(dve, k)
            copy_pT(dve, t)
            filled(dve, ("pv", t))
            release(dve, v.tensor_copy(mixT[:, 4:8, P * t:P * t + P], split(bank(("pv", t)), P)), ("pv", t), wait=True)
        evacuated(dve, ("pT", 1, 7))
        evacuated(dve, ("pcT", 1, 1))
        for u in range(2):
            if u == 1:
                evacuated(dve, ("spT", 0, 3))
            filled(dve, ("sc4", u))
            release(dve, v.tensor_tensor(LC[:, 0, :], bank(("sc4", u))[:, 0:NCB], C("bcmp"), ALU.add), ("sc4", u), wait=True)
            V(v.tensor_reduce(small[:, 64:65], LC[:, 0, :], AX, ALU.max))
            V(v.tensor_scalar(small[:, 64:65], small[:, 64:65], -1.0, None, ALU.mult), s_cmx)
            copy_skT(dve, u)
            dve.wait_ge(s_cexp, u + 1)
            V(v.reciprocal(small[:, 66:67], small[:, 65:66]))
            V(v.tensor_scalar(LC[:, 0, :], LC[:, 0, :], small[:, 66:67], None, ALU.mult))
            V(v.tensor_scalar(LC[:, 1, :], LC[:, 0, :], gsm[:, u, 0:1], None, ALU.mult), s_cpn)
            filled(dve, ("spcT", u))
            release(dve, v.tensor_copy(pcs[0:NCB, :, :], split(bank(("spcT", u))[0:NCB, 0:256], P)), ("spcT", u))
            filled(dve, ("imp", u))
            release(dve, v.tensor_copy(small[:, 108:125], bank(("imp", u))[:, 0:17]), ("imp", u))
            filled(dve, ("impj", u))
            release(dve, v.tensor_copy(small[:, 128:145], bank(("impj", u))[:, 0:17]), ("impj", u), wait=True)
            V(v.tensor_reduce(small[:, 68:69], small[:, 129:144], AX, ALU.min))
            V(v.tensor_scalar(small[:, 108:123], small[:, 129:144], small[:, 68:69], None, ALU.is_equal))
            V(v.tensor_tensor(small[:, 108:123], small[:, 108:123], C("blk")[:, 1:16], ALU.mult))
            V(v.tensor_reduce(small[:, 69:70], small[:, 108:123], AX, ALU.max))
            for k in range(2):
                filled(dve, ("ss", u, k))
                release(dve, v.tensor_tensor(L[:, 512 * k:512 * k + 512], bank(("ss", u, k)), C("bsel")[:, 512 * k:512 * k + 512], ALU.add), ("ss", u, k))
            filled(dve, ("sw", u))
            release(dve, v.tensor_tensor(L[:, 1056:1568], bank(("sw", u)), C("bwin"), ALU.add), ("sw", u))
            filled(dve, ("sn", u))
            V(v.tensor_tensor(L[:, 1024:1056], bank(("sn", u))[:, 0:32], C("bnew", 32)[:, u], ALU.add), wait=False)
            release(dve, v.tensor_tensor(L[:, 1568:1600], bank(("sn", u))[:, 32:64], C("bnew", 32)[:, u], ALU.add), ("sn", u), wait=True)
            V(v.tensor_scalar(pen[:, :], C("pblk"), small[:, 69:70], NEG, ALU.is_equal, ALU.mult))
            V(v.tensor_tensor(split(L[:, 0:1024], P), split(L[:, 0:1024], P), bc(pen[:, :], 1, 8), ALU.add))
            V(v.tensor_reduce(small[:, 70:71], L[:, 0:1056], AX, ALU.max), wait=False)
            V(v.tensor_reduce(small[:, 71:72], L[:, 1056:1600], AX, ALU.max))
            V(v.tensor_scalar(small[:, 72:74], small[:, 70:72], -1.0, None, ALU.mult), s_smx)
            dve.wait_ge(s_sexp, u + 1)
            V(v.reciprocal(small[:, 76:78], small[:, 74:76]))
            V(v.tensor_tensor(small[:, 76:78], small[:, 76:78], gsm[:, u, 1:3], ALU.mult))
            V(v.tensor_scalar(L[:, 0:1056], L[:, 0:1056], small[:, 76:77], None, ALU.mult), wait=False)
            V(v.tensor_scalar(L[:, 1056:1600], L[:, 1056:1600], small[:, 77:78], None, ALU.mult), s_spn)
            copy_spT(dve, u)
            filled(dve, ("spv", u))
            for g in range(2):
                rows = slice(64 * g, 64 * g + 64)
                src = bank(("spv", u))[rows, 0:P].rearrange("p (b g j t) -> p g j b t", g=2, j=4, t=STEPS)[:, g]
                dst = mixT[rows, 4:8, T_PROMPT + 16 * u:T_PROMPT + 16 * u + 16].rearrange("p j (b t) -> p j b t", t=STEPS)
                if g == 0:
                    V(v.tensor_copy(dst, src), wait=False)
                else:
                    release(dve, v.tensor_copy(dst, src), ("spv", u), wait=True)
        dve.sem_inc(s_end["nsa"][0], 1)
        for s in s_end["nsa"]:
            dve.wait_ge(s, 1)

        def residual(name):
            for c in range(2):
                for t in range(3):
                    n = toks(t)[1]
                    x = xt[0:n, t, GW * c:GW * c + GW]
                    filled(dve, (name, c, t))
                    release(dve, v.scalar_tensor_tensor(out=x, in0=x, scalar=ALPHA, in1=bank((name, c, t))[0:n], op0=ALU.mult, op1=ALU.add),
                            (name, c, t), wait=True)

        def norm(k, lnp):
            V(v.memset(small[:, 100:103], 1.0))
            for t in range(3):
                n = toks(t)[1]
                for c in range(2):
                    V(v.bn_stats(small[0:n, 150 + 6 * c:156 + 6 * c], xt[0:n, t, 512 * c:512 * c + 512]), wait=(c == 1))
                V(v.bn_aggr(small[0:n, 162 + 2 * t:164 + 2 * t], small[0:n, 150:162]))
                V(v.tensor_scalar(small[0:n, 100 + t:101 + t], small[0:n, 163 + 2 * t:164 + 2 * t], EPS, None, ALU.add), s_lnv if t == 2 else None)
            dve.wait_ge(s_lnr, k + 1)
            V(v.reciprocal(small[:, 96:99], small[:, 104:107]))
            dve.wait_ge(s_lnp, 32 * (k + 1))
            for t in range(3):
                n = toks(t)[1]
                x = xt[0:n, t, :]
                V(v.tensor_scalar(x, x, small[0:n, 162 + 2 * t:163 + 2 * t], small[0:n, 96 + t:97 + t], ALU.subtract, ALU.mult))
                V(v.tensor_tensor(x, x, lnp[0:n, 0, :], ALU.mult))
                V(v.tensor_tensor(x, x, lnp[0:n, 1, :], ALU.add), s_ln)

        V(v.memset(qpm[:, :, :, :], 0.0))
        residual("wo")
        norm(0, lnp)
        copy_xT(dve, "memT", 2, memT)
        copy_mkv(dve)
        copy_xT(dve, "x1T")
        copy_mq(dve)
        evacuated(dve, ("mq", KC - 1))
        evacuated(dve, ("mq", KC - 2))
        for c in range(KC):
            o = 4 * (c // 2)
            V(v.tensor_copy(qpm[:, :, c, o:o + 4], mqT[:, c, T_PROMPT:TOK].rearrange("p (b t) -> p b t", t=STEPS)), s_mpad, wait=False)
        copy_mkT(dve, 0)
        for t in range(2):
            for k in range(2):
                filled(dve, ("ms", t, k))
                V(v.tensor_reduce(small[:, 88 + 2 * k:90 + 2 * k], split(bank(("ms", t, k)), 256), AX, ALU.max))
            if t == 1:
                filled(dve, ("mpT", 0, 1))
            V(v.tensor_scalar(small[:, 80:84], small[:, 88:92], -1.0, None, ALU.mult), s_mmx)
            evacuated(dve, ("ms", t, 1))
            V(v.reciprocal(small[:, 92:96], small[:, 84:88]))
            V(v.tensor_tensor(Pm[:, :, :], Pm[:, :, :], bc(small[:, 92:96], 2, 256), ALU.mult), s_mpn)
            copy_mp(dve, t)
        filled(dve, ("mpT", 1, 1))
        for u in range(2):
            for b in range(4):
                copy_mkT(dve, 1 + 4 * u + b)
                copy_sms(dve, u, b)
            evacuated(dve, ("sms", u, 3))
            evacuated(dve, ("sms", u, 2))
            V(v.tensor_reduce(small[:, 88:89], Pm[:, 0, :], AX, ALU.max))
            V(v.tensor_scalar(small[:, 80:81], small[:, 88:89], -1.0, None, ALU.mult), s_mmx)
            dve.wait_ge(s_mexp, u + 1)
            V(v.reciprocal(small[:, 92:93], small[:, 84:85]))
            V(v.tensor_scalar(Pm[:, 0, :], Pm[:, 0, :], small[:, 92:93], None, ALU.mult), s_mpn)
            copy_smpT(dve, u)
            filled(dve, ("smo", u))
            release(dve, v.tensor_copy(mixT[:, :, T_PROMPT + 16 * u:T_PROMPT + 16 * u + 16].rearrange("p c (b t) -> p b c t", t=STEPS),
                                       bank(("smo", u))[:, 0:P].rearrange("p (b c t) -> p b c t", b=4, c=KC)), ("smo", u), wait=True)
        residual("mw")
        dve.sem_inc(s_end["mem"][0], 1)
        norm(1, lnp)
        for s in s_end["mem"]:
            dve.wait_ge(s, 1)
        dve.wait_ge(s_mkout, 32)
        copy_skeyT(dve)
        copy_xT(dve, "x2T")
        copy_pq(dve)
        for t in range(3):
            n = toks(t)[1]
            copy_ps(dve, t)
            for q in range(4):
                evacuated(dve, ("ps", t, q))

            def best16(vals, inds, x):
                V(v.max(vals[:, 0:8], x))
                V(v.max_index(inds[:, 0:8], vals[:, 0:8], x))
                V(v.match_replace(x, vals[:, 0:8], x, NEG))
                V(v.max(vals[:, 8:16], x))
                V(v.max_index(inds[:, 8:16], vals[:, 8:16], x))

            for hc in range(16):
                best16(tv[0:n, hc], ti[0:n, hc], sc[0:n, t, hc])
            V(v.tensor_copy(tif[0:n], ti[0:n]))
            tvh, tih = tv[0:n].rearrange("p (h c) k -> p h c k", c=2), tif[0:n].rearrange("p (h c) k -> p h c k", c=2)
            for h in range(8):
                V(v.tensor_tensor(split(cand[0:n, h], 16), bc(tvh[:, h, 0], 2, 16), bc(tvh[:, h, 1], 1, 16), ALU.add), wait=(h == 7))
            for h in range(8):
                best16(cv[0:n, h], cj[0:n, h], cand[0:n, h])
            flat = cj[0:n].rearrange("p h k -> p (h k)")
            V(v.tensor_tensor(texp[0:n], cv[0:n], cv[0:n, :, 0:1].to_broadcast([n, 8, 16]), ALU.subtract), s_tmx)
            V(v.tensor_scalar(ja[0:n, 0], flat, 4, None, ALU.logical_shift_right), wait=False)
            V(v.tensor_scalar(ja[0:n, 1], flat, 15, None, ALU.bitwise_and))
            V(v.tensor_copy(jaf[0:n], ja[0:n]))
            for c in range(2):
                V(v.tensor_tensor(eqm[0:n], bc(jaf[0:n, c], 2, 16), bc(C("iota16")[0:n], 1, P), ALU.is_equal))
                for h in range(8):
                    V(v.tensor_tensor(eqm[0:n, 16 * h:16 * h + 16], eqm[0:n, 16 * h:16 * h + 16], bc(tih[:, h, c], 1, 16), ALU.mult), wait=(h == 7))
                V(v.tensor_reduce(ef[0:n, c], eqm[0:n], AX, ALU.add))
            e_out = E_all[:, 8 * t:8 * t + 8, :].rearrange("p a k -> p (a k)") if t < 2 else es[:, :]
            w_out = W_all[:, 8 * t:8 * t + 8, :] if t < 2 else split(ws[:, :], 16)
            V(v.scalar_tensor_tensor(out=e_out, in0=ef[0:n, 0], scalar=128.0, in1=ef[0:n, 1], op0=ALU.mult, op1=ALU.add))
            dve.wait_ge(s_texp, t + 1)
            V(v.tensor_reduce(tsum[0:n, 0:8], texp[0:n], AX, ALU.add))
            V(v.reciprocal(tsum[0:n, 8:16], tsum[0:n, 0:8]))
            V(v.tensor_tensor(w_out, texp[0:n], bc(tsum[0:n, 8:16], 2, 16), ALU.mult), s_route)
        dve.sem_inc(s_end["peer"][0], 1)
        for s in s_end["peer"]:
            dve.wait_ge(s, 1)
        V(v.memset(Y[:, :, :], 0.0))
        dve.sem_inc(u_free, 8)
        dve.sem_inc(v_free, GRP)
        dve.sem_inc(y_free, 1)
        dve.wait_ge(s_fold, 16 * 11)
        with dve.Fori(0, NGRP) as g:
            v.tensor_copy(x_cur[:, :], xt[:, bass.ds(g // 8, 1), :].rearrange("p a d -> p (a d)")).then_inc(dve_step, 1)
            dve.wait_ge(dve_step, g + (V.n[id(dve_step)] + 1))
            for k in range(GRP):
                dve.wait_ge(s_u[k % 8], 32 * g + 16 * (k // 8 + 1))
                v.tensor_tensor_reduce(out=ubuf[:, k % 8, :], in0=ubuf[:, k % 8, :], in1=x_cur[:, :], scale=1.0, scalar=0.0,
                                       op0=ALU.mult, op1=ALU.add, accum_out=h_cur[:, k:k + 1]).then_inc(u_free, 1)
            dve.wait_ge(u_free, GRP * g + GRP + 8)
            dve.sem_inc(h_done, 1)
            dve.wait_ge(gelu_done, g + 1)
            v.tensor_tensor(w_cur[:, :], g_cur[:, :], W_all[:, bass.ds(g, 1), :].rearrange("p a k -> p (a k)"), ALU.mult).then_inc(w_done, 1)
            dve.wait_ge(v_free, GRP * g + 2 * GRP)
            ysl = Y[:, bass.ds(g // 8, 1), :].rearrange("p a (c n) -> p (a c) n", n=512)
            v.tensor_tensor(ysl, psum[:, 0:2, :], ysl, ALU.add).then_inc(y_free, 1)
        V.n[id(dve_step)] += NGRP
        dve.wait_ge(y_free, NGRP + 1)
        dve.sem_inc(s_y, 1)
        for t in range(2):
            x = xt[:, t, :]
            V(v.scalar_tensor_tensor(out=x, in0=x, scalar=ALPHA, in1=Y[:, t, :], op0=ALU.mult, op1=ALU.add))
        for c in range(2):
            x = xt[0:32, 2, GW * c:GW * c + GW]
            filled(dve, ("yfold", c))
            release(dve, v.scalar_tensor_tensor(out=x, in0=x, scalar=ALPHA, in1=bank(("yfold", c))[0:32], op0=ALU.mult, op1=ALU.add), ("yfold", c), wait=True)
        norm(2, lnp3)

    @block.tensor
    def _(pe):
        def begin(key):
            if JOB[key] >= 8:
                pe.wait_ge(bank_free[JOB[key] % 8], JOB[key] // 8)
            return bank(key)

        def done(ins, key):
            ins.then_inc(bank_full[JOB[key] % 8], 1)

        mm, tr = nc.tensor.matmul, nc.tensor.transpose

        def landed(n):
            pe.wait_ge(s_w[n % 2], w_value(n))
            return wbuf[:, n % 2]

        def turn_tokens(name, src, ntile=3):
            for t in range(ntile):
                n = toks(t)[1]
                for c in range(2):
                    o = begin((name, t, c))
                    for i in range(4):
                        k = 4 * c + i
                        ins = tr(o[:, P * i:P * i + n], src[0:n, t, P * k:P * k + P], ident[0:n, 0:n])
                    done(ins, (name, t, c))

        def by_token(name, group, xs, c, ntile=3, w=GW):
            wt = landed(group)
            for t in range(ntile):
                t0, n = toks(t)
                o = begin((name, c, t))
                for k in range(KC):
                    ins = mm(o[0:n, 0:w], xs[:, k, t0:t0 + n], wt[:, k, 0:w], start=(k == 0), stop=(k == KC - 1))
                done(ins, (name, c, t))

        def by_feature(name, group, c, cols):
            wt = landed(group)
            o = begin((name, c))
            for k in range(KC):
                ins = mm(o[:, 0:TOK], wt[:, k, cols:cols + P], xT[:, k, :], start=(k == 0), stop=(k == KC - 1))
            done(ins, (name, c))

        def all_evacuated(keys):
            for key in keys:
                evacuated(pe, key)

        pe.wait_ge(s_const, 16)
        pe.wait_ge(s_x, 32)
        turn_tokens("xT", xt)
        all_evacuated([("xT", t, c) for t in range(3) for c in range(2)])
        for g, (o_, w_) in enumerate(WG_IN):
            by_token("z", WG["w_in", g], xT, g, 3, w_)

        for kv in range(2):
            for i in range(4):
                pe.wait_ge(s_sorted, 4 * kv + i + 1)
                src = subg[:, :].rearrange("p (g r n) -> p r g n", g=2, r=8)
                for q in range(4):
                    o = begin(("subT", kv, i, q))
                    for m in range(4):
                        r, g = (4 * q + m) // 2, m % 2
                        ins = tr(o[:, P * m:P * m + P], src[:, r, g], ident)
                    done(ins, ("subT", kv, i, q))
            pe.wait_ge(s_subp, 32 * (kv + 1))
            src = subp[:, :].rearrange("p (g r n) -> p r g n", g=2, r=8)
            o = begin(("subT", kv, 4, 0))
            for m in range(16):
                ins = tr(o[:, 16 * m:16 * m + 16], src[:, m // 2, m % 2], ident[0:16, 0:16])
            done(ins, ("subT", kv, 4, 0))
            all_evacuated([("subT", kv, i, q) for i in range(4) for q in range(4)] + [("subT", kv, 4, 0)])
            pe.wait_ge(s_cw, 16 * (3 + kv))
            for g in range(2):
                o = begin(("hid", kv, g))
                for n in range(16):
                    part = subT[:, 2 * (n % 8) + g, 0:512].rearrange("p (b s) -> p b s", s=64)[:, :, n // 8:n // 8 + NCB]
                    ins = mm(o[:, 0:504].rearrange("p (b s) -> p b s", s=NCB), w1[:, n, :], part, start=(n == 0), stop=(n == 15))
                done(ins, ("hid", kv, g))
            o = begin(("hidp", kv))
            for g in range(2):
                for n in range(16):
                    ins = mm(o[:, 15 * g:15 * g + 15], w1[:, n, :], subT[:, 2 * (n % 8) + g, 512 + n // 8:512 + n // 8 + NCP],
                             start=(n == 0), stop=(n == 15))
            done(ins, ("hidp", kv))
            all_evacuated([("hid", kv, 0), ("hid", kv, 1), ("hidp", kv)])
            if kv == 0:
                for key, o_, w_ in ((("kcT",), 0, 504), (("kcTp",), 504, NCP)):
                    o = begin(key)
                    for g in range(2):
                        ins = mm(o[64 * g:64 * g + 64, 0:w_], w2[:, 0, :], hid[:, g, o_:o_ + w_], start=True, stop=True)
                    done(ins, key)
            else:
                for c in range(2):
                    o = begin(("vc", c))
                    for b in range(4):
                        for g in range(2):
                            at = NCB * (4 * c + b)
                            ins = mm(o[0:NCB, P * b + 64 * g:P * b + 64 * g + 64], hid[:, g, at:at + NCB], w2[:, 1, :], start=True, stop=True)
                    done(ins, ("vc", c))
                o = begin(("vcp",))
                for g in range(2):
                    ins = mm(o[0:NCP, 64 * g:64 * g + 64], hid[:, g, 504:519], w2[:, 1, :], start=True, stop=True)
                done(ins, ("vcp",))

        for t in range(3):
            n = toks(t)[1]
            for key, c in ((("hqT", t), HQ), (("hfT", t), HF)):
                o = begin(key)
                for h in range(H):
                    ins = tr(o[:, P * h:P * h + n], z[0:n, t, c + P * h:c + P * h + P], ident[0:n, 0:n])
                done(ins, key)
        pe.wait_ge(s_ke, 1)
        for t in range(3):
            t0, n = toks(t)
            o = begin(("att", t))
            for h in range(H):
                ins = mm(o[0:n, P * h:P * h + n], e3[:, h, t0:t0 + n], e2[:, h, t0:t0 + n], start=True, stop=True)
            done(ins, ("att", t))
        pe.wait_ge(s_ke, 2)
        for t in range(3):
            t0, n = toks(t)
            o = begin(("kE", t))
            for h in range(H):
                ins = tr(o[0:n, P * h:P * h + P], kT[:, h, t0:t0 + n], ident)
            done(ins, ("kE", t))
        for t in range(3):
            n = toks(t)[1]
            evacuated(pe, ("att", t))
            o = begin(("oin", t))
            for h in range(H):
                ins = mm(o[0:n, P * h:P * h + P], attS[0:n, t, h, 0:n], z[0:n, t, HI + P * h:HI + P * h + P], start=True, stop=True)
            done(ins, ("oin", t))
        all_evacuated([("kE", t) for t in range(3)])
        for c in range(NCH):
            t, r = c // 4, slice(32 * (c % 4), 32 * (c % 4) + 32)
            o = begin(("U", c))
            for h in range(H):
                ins = mm(o[:, P * h:P * h + P], ktok[r, t, h, :], z[r, t, HI + P * h:HI + P * h + P], start=True, stop=True,
                         tile_position=(r.start, 0))
            done(ins, ("U", c))
        pe.wait_ge(s_ke, 3)
        pe.wait_ge(s_stin, 16)
        for t in range(3):
            if t < 2:
                evacuated(pe, ("U", 4 * t + 2))
            o = begin(("ost", t))
            for h in range(H):
                if t < 2:
                    for j in range(4):
                        c = 4 * t + j
                        ins = mm(o[32 * j:32 * j + 32, P * h:P * h + P], qT[:, h, CH * c:CH * c + CH], state[:, c, h, :], start=True, stop=True)
                else:
                    for b in range(N_SAMPLE):
                        ins = mm(o[0:32, P * h:P * h + P], qGm[:, h, b, :], sstate[:, b, h, :], start=(b == 0), stop=(b == N_SAMPLE - 1))
            done(ins, ("ost", t))
        pe.wait_ge(s_vm, N_SAMPLE)
        for b in range(N_SAMPLE):
            o = begin(("US", b))
            for h in range(H):
                ins = mm(o[:, P * h:P * h + P], ktok[0:32, 2, h, :], vm[0:32, b, P * h:P * h + P], start=True, stop=True)
            done(ins, ("US", b))

        pe.wait_ge(s_gates, 2)
        for u in range(2):
            o = begin(("gs", u))
            done(mm(o[:, 0:24], C("rowsel", P)[0:32, u, :], z[0:32, 2, NG:NG + 24], start=True, stop=True), ("gs", u))
        for t in range(3):
            n = toks(t)[1]
            o = begin(("nqT", t))
            q = split(z[0:n, t, NQ:NQ + 512], P)
            for j in range(4):
                ins = tr(o[:, P * j:P * j + n], q[:, j], ident[0:n, 0:n])
            done(ins, ("nqT", t))
        for t in range(3):
            n = toks(t)[1]
            o = begin(("nkT", t))
            for i, c in enumerate((KSC, KWC)):
                ins = tr(o[:, P * i:P * i + n], z[0:n, t, c:c + P], ident[0:n, 0:n])
            done(ins, ("nkT", t))
        all_evacuated([("nqT", t) for t in range(3)] + [("nkT", t) for t in range(3)])
        for t in range(2):
            K, t0, per = P * (t + 1), P * t, 4 // (t + 1)
            for g in range(2):
                o, r = begin(("sc", t, g)), slice(64 * g, 64 * g + 64)
                for j in range(4):
                    ins = mm(o[:, NCP * j:NCP * j + NCP], qn[r, j, t0:t0 + P], kcT[r, 504:519], start=True, stop=True)
                done(ins, ("sc", t, g))
            for br in range(2):
                for k in range(2 * (t + 1)):
                    o = begin(("s", t, br, k))
                    for i in range(per):
                        h = per * k + i
                        r = slice(64 * (h // 4), 64 * (h // 4) + 64)
                        ins = mm(o[:, K * i:K * i + K], qn[r, h % 4, t0:t0 + P], kn[r, br, 0:K], start=True, stop=True)
                    done(ins, ("s", t, br, k))
            if t == 0:
                pe.wait_ge(s_otok, 3)
                for k in range(3):
                    n = toks(k)[1]
                    o = begin(("oT", k))
                    for h in range(H):
                        ins = tr(o[:, P * h:P * h + n], otok[0:n, k, h, :], ident[0:n, 0:n])
                    done(ins, ("oT", k))
            pe.wait_ge(s_pn, t + 1)
            blocks = [(br, h, i) for br in range(2) for h in range(8) for i in range(t + 1)]
            for k in range(4 * (t + 1)):
                o = begin(("pT", t, k))
                for m in range(4):
                    br, h, i = blocks[4 * k + m]
                    ins = tr(o[:, P * m:P * m + P], PS[:, br, h, P * i:P * i + P], ident)
                done(ins, ("pT", t, k))
            for k in range(2):
                o = begin(("pcT", t, k))
                for m in range(4):
                    ins = tr(o[0:NCP, P * m:P * m + P], PCp[:, 4 * k + m, :], ident)
                done(ins, ("pcT", t, k))
            all_evacuated([("pT", t, k) for k in range(4 * (t + 1))] + [("pcT", t, k) for k in range(2)])
            o = begin(("pv", t))
            for h in range(8):
                g, j = h // 4, h % 4
                terms = [(z[:, i, (VSC, VWC)[br] + 64 * g:(VSC, VWC)[br] + 64 * g + 64], PTp[:, blocks.index((br, h, i)), :])
                         for br in range(2) for i in range(t + 1)]
                terms.append((vcP[0:NCP, 64 * g:64 * g + 64], PCT[0:NCP, h, :]))
                for n, (lhsT, rhs) in enumerate(terms):
                    ins = mm(o[64 * g:64 * g + 64, P * j:P * j + P], lhsT, rhs, start=(n == 0), stop=(n == len(terms) - 1))
            done(ins, ("pv", t))
        pe.wait_ge(s_qpad, 2)
        for u in range(2):
            o = begin(("sc4", u))
            for b in range(4):
                s = 4 * u + b
                ins = mm(o[32 * b:32 * b + 32, 0:NCB], qpad[:, s, :], kcT[:, NCB * s:NCB * s + NCB], start=True, stop=True)
            done(ins, ("sc4", u))
            for b in range(4):
                s = 4 * u + b
                pe.wait_ge(s_slk[s % 2], 32 * (s // 2 + 1))
                for k in range(3):
                    src = slk[:, s % 2, 512 * k:512 * k + 512] if k < 2 else wk[:, s % 2, :]
                    o = begin(("skT", u, b, k))
                    for i in range(4):
                        ins = tr(o[:, P * i:P * i + P], src[:, P * i:P * i + P], ident)
                    done(ins, ("skT", u, b, k))
            pe.wait_ge(s_cpn, u + 1)
            o = begin(("spcT", u))
            for i in range(2):
                ins = tr(o[0:NCB, P * i:P * i + P], LC[:, i, :], ident)
            done(ins, ("spcT", u))
            evacuated(pe, ("spcT", u))
            o = begin(("imp", u))
            done(mm(o[:, 0:17], pcs[0:NCB, 0, :], C("cover")[0:NCB], start=True, stop=True), ("imp", u))
            evacuated(pe, ("imp", u))
            o = begin(("impj", u))
            done(mm(o[:, 0:17], C("jsum"), small[:, 108:125], start=True, stop=True), ("impj", u))
            all_evacuated([("skT", u, b, k) for b in range(4) for k in range(3)])
            for key, c0 in ((("ss", u, 0), 0), (("ss", u, 1), 512), (("sw", u), 1024)):
                o = begin(key)
                for b in range(4):
                    ins = mm(o[32 * b:32 * b + 32, :], qpad[:, 4 * u + b, :], KT[:, b, c0:c0 + 512], start=True, stop=True)
                done(ins, key)
            o = begin(("sn", u))
            for b in range(4):
                for br in range(2):
                    ins = mm(o[32 * b:32 * b + 32, 32 * br:32 * br + 32], qpad[:, 4 * u + b, :], kn[:, br, T_PROMPT:TOK], start=True, stop=True)
            done(ins, ("sn", u))
            pe.wait_ge(s_spn, u + 1)
            for k in range(3):
                o = begin(("spT", u, k))
                c0 = 512 * k if k < 2 else 1056
                for i in range(4):
                    ins = tr(o[:, P * i:P * i + P], L[:, c0 + P * i:c0 + P * i + P], ident)
                done(ins, ("spT", u, k))
            o = begin(("spT", u, 3))
            for i, c0 in enumerate((1024, 1568)):
                ins = tr(o[0:32, P * i:P * i + P], L[:, c0:c0 + 32], ident)
            done(ins, ("spT", u, 3))
            all_evacuated([("spT", u, k) for k in range(4)])
            o = begin(("spv", u))
            for b in range(4):
                r = slice(32 * b, 32 * b + 32)
                pe.wait_ge(s_slv[b], 32 * (u + 1))
                terms = [(slv[:, b, P * i:P * i + P], PTs[:, i, r]) for i in range(8)]
                terms += [(wv[:, b, P * i:P * i + P], PTs[:, 8 + i, r]) for i in range(4)]
                terms += [(z[0:32, 2, VSC:VSC + P], PTs[0:32, 12, r]), (z[0:32, 2, VWC:VWC + P], PTs[0:32, 13, r]),
                          (vcS[0:NCB, 4 * u + b, :], pcs[0:NCB, 1, r])]
                for n, (lhsT, rhs) in enumerate(terms):
                    ins = mm(o[:, r], lhsT, rhs, start=(n == 0), stop=(n == len(terms) - 1))
            done(ins, ("spv", u))
        all_evacuated([("pv", 0), ("pv", 1), ("spv", 0), ("spv", 1), ("oT", 0), ("oT", 1), ("oT", 2)])
        for c in range(2):
            by_token("wo", WG["w_out", c], mixT, c)

        pe.wait_ge(s_mem, 16)
        turn_tokens("memT", memp, 2)
        all_evacuated([("memT", t, c) for t in range(2) for c in range(2)])
        for name, w in (("mk", "w_mem_k"), ("mv", "w_mem_v")):
            for c in range(2):
                by_token(name, WG[w, c], memT, c, 2)
        pe.wait_ge(s_ln, 3)
        turn_tokens("x1T", xt)
        all_evacuated([("x1T", t, c) for t in range(3) for c in range(2)])
        for c in range(KC):
            by_feature("mq", WG["w_mem_q", c // 4], c, P * (c % 4))
        all_evacuated([("mk", c, t) for c in range(2) for t in range(2)] + [("mv", c, t) for c in range(2) for t in range(2)])

        def turn_keys(seq, src):
            for q in range(4):
                o = begin(("mkT", seq, q))
                for m in range(4):
                    c, i = 2 * q + m // 2, m % 2
                    ins = tr(o[:, P * m:P * m + P], src[:, i, P * c:P * c + P], ident)
                done(ins, ("mkT", seq, q))

        turn_keys(0, mkt)
        all_evacuated([("mkT", 0, q) for q in range(4)] + [("mq", c) for c in range(KC)])
        for t in range(2):
            for k in range(2):
                o = begin(("ms", t, k))
                for m in range(2):
                    for i in range(2):
                        c = 2 * (2 * k + m) + i
                        ins = mm(o[:, 256 * m:256 * m + 256], mqT[:, c, P * t:P * t + P], KTm[:, 0, c, :], start=(i == 0), stop=(i == 1))
                done(ins, ("ms", t, k))
            pe.wait_ge(s_mpn, t + 1)
            for k in range(2):
                o = begin(("mpT", t, k))
                for m in range(4):
                    h, i = 2 * k + m // 2, m % 2
                    ins = tr(o[:, P * m:P * m + P], Pm[:, h, P * i:P * i + P], ident)
                done(ins, ("mpT", t, k))
            all_evacuated([("mpT", t, 0), ("mpT", t, 1)])
            for k in range(2):
                o = begin(("mo", t, k))
                for m in range(4):
                    c = 4 * k + m
                    for i in range(2):
                        ins = mm(o[:, P * m:P * m + P], mvt[:, i, P * c:P * c + P], PTm[:, 2 * (c // 2) + i, :], start=(i == 0), stop=(i == 1))
                done(ins, ("mo", t, k))
        pe.wait_ge(s_mpad, KC)
        for u in range(2):
            for b in range(4):
                s = 4 * u + b
                pe.wait_ge(s_mck[s % 2], 16 * (s // 2 + 1))
                turn_keys(1 + s, mck[:, s % 2])
                all_evacuated([("mkT", 1 + s, q) for q in range(4)])
                o = begin(("sms", u, b))
                for c in range(KC):
                    ins = mm(o[32 * b:32 * b + 32, 0:256], qpm[:, s, c, :], KTm[:, (1 + s) % 2, c, :], start=(c == 0), stop=(c == KC - 1))
                done(ins, ("sms", u, b))
            pe.wait_ge(s_mpn, 3 + u)
            o = begin(("smpT", u))
            for i in range(2):
                ins = tr(o[:, P * i:P * i + P], Pm[:, 0, P * i:P * i + P], ident)
            done(ins, ("smpT", u))
            evacuated(pe, ("smpT", u))
            o = begin(("smo", u))
            for b in range(4):
                pe.wait_ge(s_mcv[b], 16 * (u + 1))
                for c in range(KC):
                    at = 32 * b + 4 * c
                    for i in range(2):
                        ins = mm(o[:, at:at + 4], mcv[:, b, i, P * c:P * c + P], PTm[:, i, 32 * b + 4 * (c // 2):32 * b + 4 * (c // 2) + 4],
                                 start=(i == 0), stop=(i == 1))
            done(ins, ("smo", u))
        all_evacuated([("mo", t, k) for t in range(2) for k in range(2)] + [("smo", 0), ("smo", 1)])
        for c in range(2):
            by_token("mw", WG["w_mem_o", c], mixT, c)

        pe.wait_ge(s_skey, 16)
        for q in range(4):
            o = begin(("skeyT", q))
            for m in range(4):
                ins = tr(o[:, P * m:P * m + P], skey[:, 4 * q + m, :], ident)
            done(ins, ("skeyT", q))
        pe.wait_ge(s_ln, 6)
        turn_tokens("x2T", xt)
        all_evacuated([("x2T", t, c) for t in range(3) for c in range(2)])
        for c in range(16):
            by_feature("pq", WG["peer_w_q", c // 4], c, P * (c % 4))
        all_evacuated([("pq", c) for c in range(16)] + [("skeyT", q) for q in range(4)])
        for t in range(3):
            t0, n = toks(t)
            for q in range(4):
                o = begin(("ps", t, q))
                for m in range(4):
                    hc = 4 * q + m
                    ins = mm(o[0:n, P * m:P * m + P], pqT[:, hc, t0:t0 + n], skT[:, hc, :], start=True, stop=True)
                done(ins, ("ps", t, q))
        for s in s_end["peer"]:
            pe.wait_ge(s, 1)
        all_evacuated([("ps", 2, q) for q in range(4)])
        with pe.Fori(0, NGRP) as g:
            pe.wait_ge(y_free, g + 1)
            for k in range(GRP):
                pe.wait_ge(diag_done, GRP * g + k + 1)
                pe.wait_ge(s_v[k], 16 * g + 16)
                for c in range(2):
                    ins = mm(psum[:, c, :], diag[:, k, :], vbuf[:, k, GW * c:GW * c + GW], start=(k == 0), stop=(k == GRP - 1))
                ins.then_inc(v_free, 1)
        pe.wait_ge(s_y, 1)
        for c in range(2):
            o = begin(("yfold", c))
            done(mm(o[0:32, :], C("fold"), Y[:, 2, GW * c:GW * c + GW], start=True, stop=True), ("yfold", c))

    ctx.close()


_INS = ["x_prompt", "x_sample", "cache_k_cmp", "cache_v_cmp", "cache_k_slc", "cache_v_slc", "cache_k_win", "cache_v_win",
        "state_hgrn", "cache_mem_k", "cache_mem_v", "page_table", "mem_prompt", "w_in", "hgrn_lb_logits", "hgrn_norm_g",
        "cmp_k_w1", "cmp_k_b1", "cmp_k_w2", "cmp_k_b2", "cmp_v_w1", "cmp_v_b1", "cmp_v_w2", "cmp_v_b2", "w_out", "ln1_g",
        "ln1_b", "w_mem_q", "w_mem_k", "w_mem_v", "w_mem_o", "ln2_g", "ln2_b", "peer_w_q", "peer_sub_keys", "peer_u",
        "peer_v", "ln3_g", "ln3_b"]
_KV = (1, 1, 256, 2, 64)
_KVS = (1, 8, 4, 2, 64)
_OUTS = [(1, 256, 1024), (8, 4, 1024)] + [_KV] * 6 + [(1, 1, 4, 128, 128)] + [(1, 1, 256, 4, 256)] * 2 + [_KVS] * 6 + [(1, 8, 4, 128, 128)]


def kernel(**inputs):
    import numpy as _np
    import concourse.bacc as _bacc
    from concourse import mybir as _mybir
    from concourse.bass_utils import run_bass_kernel_spmd as _run

    nc = _bacc.Bacc("TRN2", target_bir_lowering=False, num_devices=1)
    arrays, args = {}, {}
    for name in _INS:
        a = _np.ascontiguousarray(inputs[name])
        arrays[f"in_{name}"] = a
        args[name] = nc.dram_tensor(f"in_{name}", a.shape, _mybir.dt.from_np(a.dtype), kind="ExternalInput").ap()
    arrays["consts"] = const_table()[0]
    args["consts"] = nc.dram_tensor("consts", arrays["consts"].shape, _mybir.dt.float32, kind="ExternalInput").ap()
    outs = [nc.dram_tensor(f"out_{i}", s, _mybir.dt.float32, kind="ExternalOutput").ap() for i, s in enumerate(_OUTS)]
    layer_kernel(nc, args, outs)
    r = _run(nc, [arrays], core_ids=[0])
    return tuple(r.results[0][f"out_{i}"] for i in range(len(_OUTS)))
```

```python
from contextlib import ExitStack

import numpy as np
import concourse.bass as bass
from concourse import mybir

ALU = mybir.AluOpType
ACT = mybir.ActivationFunctionType
F32 = mybir.dt.float32
I32 = mybir.dt.int32
U32 = mybir.dt.uint32
AX = mybir.AxisListType.X

P = 128
D = 1024
KC = D // P
T_PROMPT, N_SAMPLE, STEPS = 256, 8, 4
TOK = T_PROMPT + N_SAMPLE * STEPS
TILES = [(0, P), (P, P), (2 * P, TOK - 2 * P)]
ZC = 3352
HQ, HF, HI, HG, NQ, KCC, VCC, KSC, VSC, KWC, VWC, NG = (
    0, 512, 1024, 1536, 2048, 2560, 2688, 2816, 2944, 3072, 3200, 3328)
H = 4
CH = 32
NCH = T_PROMPT // CH
ALPHA = 2.0 ** 0.25
EPS = 1e-5
NEG = -1e30
BIG = -1e33
SLOPES = [2.0 ** -(h + 1) for h in range(8)]
PAST, PAGE = 1024, 128
WIN = 512
NCB = 63
NCP = 15
GW = 512
WG_IN = [(i * GW, min(GW, ZC - i * GW)) for i in range(7)]
NSUBS = 2
GRP = 16
NGRP = 18


def const_table():
    parts = {}
    p = np.arange(P)
    parts["ident"] = np.eye(P)
    s = np.arange(256)
    d = s[None, :] - 128 - p[:, None]
    parts["dist"] = np.where(d <= 0, d, BIG)
    c = np.arange(NCP)
    bias = np.zeros((P, 2, 8, NCP)); mask = np.zeros((P, 2, 8, NCP))
    for t in range(2):
        dd = 16 * c[None, :] + 31 - (p[:, None] + 128 * t)
        for h in range(8):
            bias[:, t, h] = np.where(dd <= 0, dd * SLOPES[h], NEG)
            mask[:, t, h] = dd <= 0
    parts["cbias"] = bias; parts["cmask"] = mask
    b4, g, j, t = p // 32, p // 16 % 2, p // 4 % 4, p % 4
    slope = np.array(SLOPES)[g * 4 + j][:, None]
    qpos = (PAST + t)[:, None]
    pos = 8 * s[None, :128] + np.arange(8)[:, None]
    parts["bsel"] = slope * (pos.reshape(1, -1) - qpos)
    posw = (PAST - WIN + 4 * s[None, :128] + np.arange(4)[:, None]).reshape(1, -1)
    dw = qpos - posw
    parts["bwin"] = np.where(dw < WIN, -slope * dw, NEG)
    fr = np.zeros((P, 2, 32))
    kb, kt = np.arange(32) // 4, np.arange(32) % 4
    for u in range(2):
        ok = (kb[None] == (4 * u + b4)[:, None]) & (kt[None] <= t[:, None])
        fr[:, u] = np.where(ok, slope * (kt[None] - t[:, None]), NEG)
    parts["bnew"] = fr
    parts["bcmp"] = slope * (16 * np.arange(NCB)[None] + 31 - qpos)
    parts["pblk"] = np.broadcast_to((s[:128] // 8)[None], (P, P))
    parts["blk"] = np.broadcast_to(np.arange(17)[None], (P, 17))
    cs, ss = np.arange(NCB)[:, None] * 16, np.arange(17)[None] * 64
    m = np.zeros((P, 17)); m[:NCB] = np.clip(np.minimum(cs + 32, ss + 64) - np.maximum(cs, ss), 0, None) / 16
    parts["cover"] = m
    parts["jsum"] = (b4[:, None] == b4[None]) & (g[:, None] == g[None]) & (t[:, None] == t[None])
    parts["hmask"] = (p[:, None] // CH == p[None] // CH) & (p[:, None] <= p[None])
    q = np.arange(32)
    hs = np.zeros((P, 32)); hs[:32] = (q[:, None] // 4 == q[None] // 4) & (q[:, None] <= q[None])
    parts["hmask_s"] = hs
    r = np.ones(TOK); r[0:T_PROMPT:CH] = 0; r[T_PROMPT::STEPS] = 0
    parts["keep"] = np.broadcast_to(r[None], (P, TOK))
    parts["bmask"] = np.broadcast_to((q[None] // 4 == np.arange(8)[:, None])[None], (P, 8, 32))
    bt = np.zeros((P, 8)); bt[:32] = q[:, None] // 4 == np.arange(8)[None]
    parts["brow"] = bt
    parts["fold"] = p[:, None] % 32 == q[None]
    toks = 4 * (4 * np.arange(2)[:, None] + b4[None]) + t[None]
    rs = np.zeros((P, 2, P)); rs[:32] = np.arange(32)[:, None, None] == toks[None]
    parts["rowsel"] = rs
    hc = np.arange(24) // 3
    parts["headsel"] = hc[None] == (g * 4 + j)[:, None]
    parts["iota16"] = np.broadcast_to(np.arange(16)[None], (P, 16))
    parts["mod8"] = (p % 8)[:, None]
    parts["mod16"] = (p % 16)[:, None]
    at, n = {}, 0
    cols = []
    for k, v in parts.items():
        v = np.asarray(v, np.float32).reshape(P, -1)
        at[k] = (n, v.shape[1]); n += v.shape[1]
        cols.append(v)
    return np.ascontiguousarray(np.concatenate(cols, 1)), at


CONST_AT = const_table()[1]
NCONST = sum(n for _, n in CONST_AT.values())


def pe_jobs():
    jobs = [("xT", t, c) for t in range(3) for c in range(2)]
    jobs += [("z", g, t) for g in range(len(WG_IN)) for t in range(3)]
    for kv in range(2):
        jobs += [("subT", kv, i, q) for i in range(4) for q in range(4)] + [("subT", kv, 4, 0)]
        jobs += [("hid", kv, 0), ("hid", kv, 1), ("hidp", kv)]
        jobs += [("vc", 0), ("vc", 1), ("vcp",)] if kv else [("kcT",), ("kcTp",)]
    for t in range(3):
        jobs += [("hqT", t), ("hfT", t)]
    jobs += [("att", t) for t in range(3)] + [("kE", t) for t in range(3)] + [("oin", t) for t in range(3)]
    jobs += [("U", c) for c in range(NCH)] + [("ost", t) for t in range(3)] + [("US", b) for b in range(N_SAMPLE)]
    jobs += [("gs", u) for u in range(2)] + [("nqT", t) for t in range(3)] + [("nkT", t) for t in range(3)]
    for t in range(2):
        jobs += [("sc", t, g) for g in range(2)] + [("s", t, br, k) for br in range(2) for k in range(2 * (t + 1))]
        if t == 0:
            jobs += [("oT", k) for k in range(3)]
        jobs += [("pT", t, k) for k in range(4 * (t + 1))] + [("pcT", t, k) for k in range(2)] + [("pv", t)]
    for u in range(2):
        jobs += [("sc4", u)]
        for b in range(4):
            jobs += [("skT", u, b, k) for k in range(3)]
        jobs += [("spcT", u), ("imp", u), ("impj", u)]
        jobs += [("ss", u, 0), ("ss", u, 1), ("sw", u), ("sn", u)]
        jobs += [("spT", u, k) for k in range(4)] + [("spv", u), ("spvT", u)]
    jobs += [("wo", c, t) for t in range(3) for c in range(2)]
    jobs += [("memT", t, c) for t in range(2) for c in range(2)]
    jobs += [("mk", c, t) for c in range(2) for t in range(2)] + [("mv", c, t) for c in range(2) for t in range(2)]
    jobs += [("x1T", t, c) for t in range(3) for c in range(2)]
    jobs += [("mq", c) for c in range(KC)]
    jobs += [("mkT", 0, q) for q in range(4)]
    for t in range(2):
        jobs += [("ms", t, 0), ("ms", t, 1), ("mpT", t, 0), ("mpT", t, 1), ("mo", t, 0), ("mo", t, 1)]
    for u in range(2):
        for b in range(4):
            jobs += [("mkT", 1 + 4 * u + b, q) for q in range(4)] + [("sms", u, b)]
        jobs += [("smpT", u), ("smo", u, 0), ("smo", u, 1), ("smoT", u, 0), ("smoT", u, 1)]
    jobs += [("mw", c, t) for t in range(3) for c in range(2)]
    jobs += [("skeyT", q) for q in range(4)] + [("x2T", t, c) for t in range(3) for c in range(2)]
    jobs += [("pq", c) for c in range(4)] + [("ps", 0, 0)] + [("pq", c) for c in range(4, 16)]
    jobs += [("ps", t, q) for t in range(3) for q in range(4) if (t, q) != (0, 0)]
    jobs += [("yfold", c) for c in range(2)]
    return jobs


JOBS = pe_jobs()
JOB = {k: n for n, k in enumerate(JOBS)}

W_GROUPS = [("w_in", o, n, ("z", i, 2)) for i, (o, n) in enumerate(WG_IN)]
W_GROUPS += [("w_out", c * GW, GW, ("wo", c, 2)) for c in range(2)]
W_GROUPS += [("w_mem_k", c * GW, GW, ("mk", c, 1)) for c in range(2)] + [("w_mem_v", c * GW, GW, ("mv", c, 1)) for c in range(2)]
W_GROUPS += [("w_mem_q", c * GW, GW, ("mq", 4 * c + 3)) for c in range(2)]
W_GROUPS += [("w_mem_o", c * GW, GW, ("mw", c, 2)) for c in range(2)]
W_GROUPS += [("peer_w_q", c * GW, GW, ("pq", 4 * c + 3)) for c in range(4)]
WG = {(name, o // GW): n for n, (name, o, _, _) in enumerate(W_GROUPS)}
W_DMAS = [3 if name == "w_out" else 1 for name, *_ in W_GROUPS]


def w_value(n):
    return 16 * sum(W_DMAS[i] for i in range(n % 2, n + 1, 2))


class Lane:

    def __init__(self, eng, step):
        self.eng, self.step, self.n = eng, step, {}

    def __call__(self, ins, signal=None, wait=True):
        s = signal or self.step
        ins.then_inc(s, 1)
        self.n[id(s)] = self.n.get(id(s), 0) + 1
        if wait:
            self.eng.wait_ge(s, self.n[id(s)])


def layer_kernel(nc, A, O):
    ctx = ExitStack()

    def sem(name):
        return ctx.enter_context(nc.semaphore(name))

    def sb(stack, name, shape, dt=F32):
        return stack.enter_context(nc.sbuf_tensor(name, shape, dt))

    bank_full = [sem(f"bank_full{b}") for b in range(8)]
    bank_free = [sem(f"bank_free{b}") for b in range(8)]
    dve_step, act_step, pool_step = sem("dve_step"), sem("act_step"), sem("pool_step")
    s_const, s_x, s_par = sem("s_const"), sem("s_x"), sem("s_par")
    s_w = [sem(f"s_w{i}") for i in range(2)]
    s_pt, s_idx = sem("s_pt"), sem("s_idx")
    s_sub = [sem(f"s_sub{i}") for i in range(NSUBS)]
    s_sorted = sem("s_sorted")
    s_cw, s_subp, s_stin = sem("s_cw"), sem("s_subp"), sem("s_stin")
    s_kvout, s_mkout, s_out = sem("s_kvout"), sem("s_mkout"), sem("s_out")
    s_lb, s_f, s_lnf, s_g, s_hexp, s_ke, s_ktok, s_vm = (sem("s_" + n) for n in "lb f lnf g hexp ke ktok vm".split())
    s_ms, s_rs, s_sgate, s_gz, s_otok, s_gates = (sem("s_" + n) for n in "ms rs sgate gz otok gates".split())
    s_mx, s_exp, s_pn, s_qpad = (sem("s_" + n) for n in "mx exp pn qpad".split())
    s_slk = [sem(f"s_slk{i}") for i in range(2)]
    s_slv = [sem(f"s_slv{i}") for i in range(4)]
    s_cmx, s_cexp, s_cpn, s_smx, s_sexp, s_spn = (sem("s_" + n) for n in "cmx cexp cpn smx sexp spn".split())
    s_end = {k: (sem(f"s_dve_end_{k}"), sem(f"s_act_end_{k}")) for k in ("cmp", "hgrn", "nsa", "mem")}
    s_lnp, s_ln, s_lnv, s_lnr = (sem("s_" + n) for n in "lnp ln lnv lnr".split())
    s_mem = sem("s_mem")
    s_mck = [sem(f"s_mck{i}") for i in range(2)]
    s_mcv = [sem(f"s_mcv{i}") for i in range(4)]
    s_mpad, s_mmx, s_mexp, s_mpn = (sem("s_" + n) for n in "mpad mmx mexp mpn".split())
    s_skey, s_tmx, s_texp, s_route, s_fold, s_y = (sem("s_" + n) for n in "skey tmx texp route fold y".split())
    route_step, x_ready = sem("route_step"), sem("x_ready")
    s_u = [sem(f"s_u{i}") for i in range(8)]
    s_v = [sem(f"s_v{i}") for i in range(GRP)]
    u_free, v_free, h_done, gelu_done, w_done, diag_done, y_free = (
        sem(n) for n in "u_free v_free h_done gelu_done w_done diag_done y_free".split())

    psum = ctx.enter_context(nc.psum_tensor("banks", [P, 8, 512], F32))
    cst = sb(ctx, "cst", [P, NCONST])
    xt = sb(ctx, "xt", [P, 3, D])
    feat = sb(ctx, "feat", [P, 2, KC, TOK])
    xT, mixT = feat[:, 0], feat[:, 1]
    wbuf = sb(ctx, "wbuf", [P, 2, KC, GW])
    par = sb(ctx, "par", [P, 320])
    small = sb(ctx, "small", [P, 192])

    def C(name, *inner):
        o, n = CONST_AT[name]
        v = cst[:, o:o + n]
        if len(inner) == 1:
            return v.rearrange("p (a b) -> p a b", b=inner[0])
        if len(inner) == 2:
            return v.rearrange("p (a b c) -> p a b c", b=inner[0], c=inner[1])
        return v

    ident = C("ident")
    lbl = par[:, 0:8].rearrange("p (a h) -> p a h", h=H)
    lb, omlb, b1, b2k = par[:, 8:12], par[:, 12:16], par[:, 16:18], par[:, 18:19]
    b2v, hng = par[:, 20:148], par[:, 148:276]
    otok = xT[:, :, :].rearrange("p a b -> p (a b)")[:, 0:1536].rearrange("p (t h e) -> p t h e", t=3, h=H)
    PTs = xT[:, :, :].rearrange("p a b -> p (a b)")[:, 0:15 * P].rearrange("p (n r) -> p n r", r=P)
    memT = mixT[:, :, :].rearrange("p a b -> p (a b)")[:, 0:KC * 256].rearrange("p (c m) -> p c m", m=256)

    zs = ExitStack()
    z = sb(zs, "z", [P, 3, ZC])
    kcT = sb(zs, "kcT", [P, N_SAMPLE * NCB + NCP])
    vcS = sb(zs, "vcS", [64, N_SAMPLE, P])
    vcP = sb(zs, "vcP", [16, P])

    st = ExitStack()
    sub = sb(st, "sub", [P, NSUBS, 2048])
    subg = sb(st, "subg", [P, 2048])
    subp = sb(st, "subp", [16, 2048])
    subT = sb(st, "subT", [P, 16, 528])
    w1 = sb(st, "w1", [P, 16, P])
    w2 = sb(st, "w2", [P, 2, 64])
    hid = sb(st, "hid", [P, 2, N_SAMPLE * NCB + NCP])
    pt = sb(st, "pt", [P, 4], I32)
    idx = sb(st, "idx", [P, 4], I32)
    st.close()

    st = ExitStack()
    qT, kT = sb(st, "qT", [P, H, TOK]), sb(st, "kT", [P, H, TOK])
    decay = sb(st, "decay", [P, 4, H, TOK])
    G, e1, e2, e3 = (decay[:, i] for i in range(4))
    vm = decay[:, :, :, :].rearrange("p a h t -> p (a h t)")[:, 0:4096].rearrange("p (b e) -> p b e", e=512)
    dec = sb(st, "dec", [P, H, NCH + N_SAMPLE])
    ktok = sb(st, "ktok", [P, 3, H, P])
    attS = sb(st, "attS", [P, 3, H, P])
    state = sb(st, "state", [P, NCH + 1, H, P])
    sstate = sb(st, "sstate", [P, N_SAMPLE, H, P])
    qGm = sb(st, "qGm", [P, H, N_SAMPLE, 32])
    st.close()

    st = ExitStack()
    qn = sb(st, "qn", [P, 4, TOK])
    kn = sb(st, "kn", [P, 2, TOK])
    qpad = sb(st, "qpad", [P, N_SAMPLE, 32])
    gsm = sb(st, "gsm", [P, 2, 3])
    ptab, sidx = sb(st, "ptab", [P, 8], I32), sb(st, "sidx", [P, 8], I32)
    slk, wk = sb(st, "slk", [P, 2, D]), sb(st, "wk", [P, 2, WIN])
    slv, wv = sb(st, "slv", [P, 4, D]), sb(st, "wv", [P, 4, WIN])
    st2 = ExitStack()
    PS = sb(st2, "PS", [P, 2, 8, 256])
    PTp = sb(st2, "PTp", [P, 32, P])
    PCp = sb(st2, "PCp", [P, 8, NCP])
    PCT = sb(st2, "PCT", [16, 8, P])
    st2.close()
    KT = sb(st, "KT", [P, 4, D + WIN])
    L = sb(st, "L", [P, 1600])
    LC = sb(st, "LC", [P, 2, NCB])
    pcs = sb(st, "pcs", [64, 2, P])
    ov = sb(st, "ov", [P, P])
    pen = sb(st, "pen", [P, P])
    st.close()
    zs.close()

    st = ExitStack()
    lnp = sb(st, "lnp", [P, 2, D])
    memp = sb(st, "memp", [P, 2, D])
    mkt, mvt = sb(st, "mkt", [P, 2, D]), sb(st, "mvt", [P, 2, D])
    so = memp[:, 0, :]
    mqT = sb(st, "mqT", [P, KC, TOK])
    KTm = sb(st, "KTm", [P, 2, KC, 256])
    mck, mcv = sb(st, "mck", [P, 2, 2, D]), sb(st, "mcv", [P, 4, 2, D])
    qpm = sb(st, "qpm", [P, N_SAMPLE, KC, 32])
    Pm = sb(st, "Pm", [P, 4, 256])
    PTm = sb(st, "PTm", [P, 8, P])
    st.close()

    st = ExitStack()
    lnp3 = sb(st, "lnp3", [P, 2, D])
    E_all, W_all = sb(st, "E_all", [P, NGRP + 8, GRP], I32), sb(st, "W_all", [P, NGRP + 8, GRP])
    E_cur, h_cur, g_cur, w_cur = sb(st, "E_cur", [P, 2, GRP], I32), sb(st, "h_cur", [P, GRP]), sb(st, "g_cur", [P, GRP]), sb(st, "w_cur", [P, GRP])
    after_x2T = feat[:, :, :, :].rearrange("p a b c -> p (a b c)")
    Y = after_x2T[:, 0:3 * D].rearrange("p (t d) -> p t d", d=D)
    x_cur = after_x2T[:, 3 * D:4 * D]
    diag = sb(st, "diag", [P, GRP, P])
    sc = sb(st, "sc", [P, 24, 2, P])

    def route_memory(stack, name, R):
        return dict(R=R, tv=sb(stack, name + "_tv", [P, R, 2, 16]), ti=sb(stack, name + "_ti", [P, R, 2, 16], U32),
                    tif=sb(stack, name + "_tif", [P, R, 2, 16]), cand=sb(stack, name + "_cand", [P, R, 256]),
                    cv=sb(stack, name + "_cv", [P, R, 16]), cj=sb(stack, name + "_cj", [P, R, 16], U32),
                    ja=sb(stack, name + "_ja", [P, 2, R * 16], U32), jaf=sb(stack, name + "_jaf", [P, 2, R * 16]),
                    ef=sb(stack, name + "_ef", [P, 2, R * 16]), eqm=sb(stack, name + "_eqm", [P, R * 16, 16]),
                    texp=sb(stack, name + "_texp", [P, R, 16]), tsum=sb(stack, name + "_tsum", [P, 2, R]))

    R2 = route_memory(st, "two", 2)
    xs = sb(st, "xs", [P, 2, 2, P])
    e_two, w_two = sb(st, "e_two", [P, 2, 16], I32), sb(st, "w_two", [P, 2, 16])
    skey = sc[:, 0:8].rearrange("p h c k -> p (h c) k")
    st2 = ExitStack()
    skT = sb(st2, "skT", [P, 16, P])
    pqT = sb(st2, "pqT", [P, 16, TOK])
    st2.close()
    rows_ = sb(st, "rows", [P, 16, D])
    wrows = wbuf[:, :, :, :].rearrange("p a b c -> p (a b c)").rearrange("p (s d) -> p s d", d=D)
    uslot = [rows_[:, 8 + k % 8, :] for k in range(GRP)]
    vslot = [wrows[:, k, :] if k < 8 else rows_[:, k - 8, :] for k in range(GRP)]
    st.close()

    block = ctx.enter_context(nc.Block())

    def bank(key):
        return psum[:, JOB[key] % 8, :]

    def filled(eng, key):
        eng.wait_ge(bank_full[JOB[key] % 8], JOB[key] // 8 + 1)

    def evacuated(eng, key):
        eng.wait_ge(bank_free[JOB[key] % 8], JOB[key] // 8 + 1)

    def release(eng, ins, key, wait=False):
        ins.then_inc(bank_free[JOB[key] % 8], 1)
        if wait:
            evacuated(eng, key)

    def copy_out(eng, key, dst, src, scale=None):
        on_act = JOB[key] % 2 == 1
        if (eng is nc.scalar) != on_act:
            return
        filled(eng, key)
        if on_act:
            ins = nc.scalar.activation(dst, src, ACT.Copy, scale=1.0 if scale is None else scale)
        elif scale is None:
            ins = nc.vector.tensor_copy(dst, src)
        else:
            ins = nc.vector.tensor_scalar(dst, src, scale, None, ALU.mult)
        release(eng, ins, key)

    def bc(ap, axis, n):
        v = ap.unsqueeze(axis)
        shape = list(v.shape)
        shape[axis] = n
        return v.to_broadcast(shape)

    def split(ap, n):
        return ap.rearrange("p (a b) -> p a b", b=n)

    def toks(t):
        return TILES[t][0], TILES[t][1]

    def copy_xT(eng, name, ntile=3, dst=None):
        for t in range(ntile):
            t0, n = toks(t)
            for c in range(2):
                d = (xT if dst is None else dst)[:, 4 * c:4 * c + 4, t0:t0 + n]
                copy_out(eng, (name, t, c), d, split(bank((name, t, c)), P)[:, :, 0:n])

    def copy_z(eng):
        for g, (o, w) in enumerate(WG_IN):
            for t in range(3):
                n = toks(t)[1]
                dst, src = z[0:n, t, o:o + w], bank(("z", g, t))[0:n, 0:w]
                if o == NQ:
                    dst, src = dst.rearrange("p (j g d) -> p g j d", j=4, g=2), src.rearrange("p (g j d) -> p g j d", j=4, g=2)
                copy_out(eng, ("z", g, t), dst, src)

    def copy_subT(eng, kv):
        if kv == 1:
            filled(eng, ("hidp", 0))
        for i in range(4):
            for q in range(4):
                copy_out(eng, ("subT", kv, i, q), subT[:, 4 * q:4 * q + 4, i * P:(i + 1) * P], split(bank(("subT", kv, i, q)), P))
        copy_out(eng, ("subT", kv, 4, 0), subT[:, :, 512:528], split(bank(("subT", kv, 4, 0))[:, 0:256], 16))

    def copy_pT(eng, t):
        if t == 1:
            filled(eng, ("pv", 0))
        for k in range(4 * (t + 1)):
            copy_out(eng, ("pT", t, k), PTp[:, 4 * k:4 * k + 4, :], split(bank(("pT", t, k)), P))
        for k in range(2):
            copy_out(eng, ("pcT", t, k), PCT[0:NCP, 4 * k:4 * k + 4, :], split(bank(("pcT", t, k))[0:NCP], P))

    def copy_skT(eng, u):
        if u == 1:
            filled(eng, ("sn", 0))
        for b in range(4):
            for k in range(3):
                copy_out(eng, ("skT", u, b, k), KT[:, b, 512 * k:512 * k + 512], bank(("skT", u, b, k)))

    def copy_spT(eng, u):
        if u == 1:
            filled(eng, ("spv", 0))
        for k in range(3):
            copy_out(eng, ("spT", u, k), PTs[:, 4 * k:4 * k + 4, :], split(bank(("spT", u, k)), P))
        copy_out(eng, ("spT", u, 3), PTs[0:32, 12:14, :], split(bank(("spT", u, 3))[0:32, 0:256], P))

    def copy_mkT(eng, seq):
        if seq >= 2:
            filled(eng, ("ms", 1, 1) if seq == 2 else ("sms", (seq - 3) // 4, (seq - 3) % 4))
        for q in range(4):
            copy_out(eng, ("mkT", seq, q), KTm[:, seq % 2, 2 * q:2 * q + 2, :], split(bank(("mkT", seq, q)), 256))

    def copy_oT(eng, k):
        t0, n = toks(k)
        copy_out(eng, ("oT", k), mixT[:, 0:4, t0:t0 + n], split(bank(("oT", k)), P)[:, :, 0:n])

    def copy_mkv(eng):
        for name, dst in (("mk", mkt), ("mv", mvt)):
            for c in range(2):
                for t in range(2):
                    copy_out(eng, (name, c, t), dst[:, t, GW * c:GW * c + GW], bank((name, c, t)))

    def copy_mq(eng):
        for c in range(KC):
            copy_out(eng, ("mq", c), mqT[:, c, :], bank(("mq", c))[:, 0:TOK], 1.0 / 16)

    def copy_mp(eng, t):
        for k in range(2):
            copy_out(eng, ("mpT", t, k), PTm[:, 4 * k:4 * k + 4, :], split(bank(("mpT", t, k)), P))
        for k in range(2):
            copy_out(eng, ("mo", t, k), mixT[:, 4 * k:4 * k + 4, P * t:P * t + P], split(bank(("mo", t, k)), P))

    def copy_sms(eng, u, b):
        if b == 0:
            filled(eng, ("mpT", 1, 1) if u == 0 else ("smpT", 0))
        copy_out(eng, ("sms", u, b), Pm[32 * b:32 * b + 32, 0, :], bank(("sms", u, b))[32 * b:32 * b + 32, 0:256])

    def copy_smpT(eng, u):
        filled(eng, ("mo", 1, 1) if u == 0 else ("smo", 0, 1))
        copy_out(eng, ("smpT", u), PTm[:, 0:2, :], split(bank(("smpT", u))[:, 0:256], P))

    def copy_skeyT(eng):
        for q in range(4):
            copy_out(eng, ("skeyT", q), skT[:, 4 * q:4 * q + 4, :], split(bank(("skeyT", q)), P))

    def copy_pq(eng, first, last):
        for c in range(first, last):
            copy_out(eng, ("pq", c), pqT[:, c, :], bank(("pq", c))[:, 0:TOK])

    def copy_ps(eng, t, qs=range(4)):
        n = toks(t)[1]
        for q in qs:
            copy_out(eng, ("ps", t, q), sc[0:n, 8 * t + 2 * q:8 * t + 2 * q + 2].rearrange("p h c k -> p (h c) k"), split(bank(("ps", t, q)), P)[0:n])

    @block.sync
    def _(sp):
        def weights(n):
            name, o, w, _ = W_GROUPS[n]
            if n >= 2:
                filled(sp, W_GROUPS[n - 2][3])
            dst, src, done = wbuf[:, n % 2], A[name][0], s_w[n % 2]
            if name == "w_out":
                sp.dma_start(dst[:, 0:4, 0:w], src[0:512, o:o + w].rearrange("(c p) n -> p c n", p=P)).then_inc(done, 16)
                for g in range(2):
                    rows = src[512 + 256 * g:768 + 256 * g, o:o + w].rearrange("(j d) n -> d j n", d=64)
                    sp.dma_start(dst[64 * g:64 * g + 64, 4:8, 0:w], rows).then_inc(done, 16)
            else:
                sp.dma_start(dst[:, :, 0:w], src[:, o:o + w].rearrange("(c p) n -> p c n", p=P)).then_inc(done, 16)

        sp.dma_start(cst[:, 0:P], A["consts"][:, 0:P]).then_inc(s_const, 16)
        sp.dma_start(xt[:, 0:2, :], A["x_prompt"][0].rearrange("(t p) d -> p t d", p=P)).then_inc(s_x, 16)
        sp.dma_start(xt[0:32, 2, :], A["x_sample"].rearrange("b s d -> (b s) d")).then_inc(s_x, 16)
        weights(0)
        weights(1)
        sp.dma_start(cst[:, P:], A["consts"][:, P:]).then_inc(s_const, 16)
        sp.dma_start(lbl, A["hgrn_lb_logits"].rearrange("a (h p) -> p a h", p=P), allow_slow_non_contiguous=True).then_inc(s_par, 16)
        sp.dma_start(b1[:, 0:1], A["cmp_k_b1"].rearrange("a h -> h a"), allow_slow_non_contiguous=True).then_inc(s_par, 16)
        sp.dma_start(b1[:, 1:2], A["cmp_v_b1"].rearrange("a h -> h a"), allow_slow_non_contiguous=True).then_inc(s_par, 16)
        for g in range(2):
            sp.dma_start(b2k[64 * g:64 * g + 64, :], A["cmp_k_b2"].rearrange("a h -> h a"), allow_slow_non_contiguous=True).then_inc(s_par, 16)
            sp.dma_start(b2v[:, 64 * g:64 * g + 64], A["cmp_v_b2"].to_broadcast([P, 64])).then_inc(s_par, 16)
        sp.dma_start(hng, A["hgrn_norm_g"].to_broadcast([P, P])).then_inc(s_par, 16)
        w1_dram = [A[n][0].rearrange("a d h -> (a d) h").rearrange("(c k) h -> k c h", k=P) for n in ("cmp_k_w1", "cmp_v_w1")]
        sp.dma_start(w2[:, 0, :], A["cmp_k_w2"][0]).then_inc(s_cw, 16)
        sp.dma_start(w2[:, 1, :], A["cmp_v_w2"][0]).then_inc(s_cw, 16)
        sp.dma_start(w1[:, :, :], w1_dram[0]).then_inc(s_cw, 16)
        for n in range(2, 9):
            weights(n)
        evacuated(sp, ("z", 6, 0)); evacuated(sp, ("z", 6, 1)); evacuated(sp, ("z", 6, 2))
        for i, c in enumerate((KCC, VCC, KSC, VSC, KWC, VWC)):
            sp.dma_start(O[2 + i][0, 0].rearrange("(t p) g d -> p t (g d)", p=P), z[:, 0:2, c:c + P]).then_inc(s_kvout, 16)
            sp.dma_start(O[11 + i][0].rearrange("b s g d -> (b s) (g d)"), z[0:32, 2, c:c + P]).then_inc(s_kvout, 16)
            if i < 2:
                sp.wait_ge(s_kvout, 32 * (i + 1))
                if i == 1:
                    filled(sp, ("subT", 0, 4, 0))
                for g in range(2):
                    sp.dma_start(subp[:, 1024 * g:1024 * g + 1024], O[2 + i][0, 0].rearrange("(n s) g d -> n g s d", s=16)[:, g]).then_inc(s_subp, 16)
        filled(sp, ("hidp", 0))
        sp.dma_start(w1[:, :, :], w1_dram[1]).then_inc(s_cw, 16)
        for s in s_end["cmp"]:
            sp.wait_ge(s, 1)
        sp.dma_start(sstate[:, :, :, :], A["state_hgrn"][0].rearrange("b h d e -> d b h e")).then_inc(s_stin, 16)
        evacuated(sp, ("U", NCH - 1))
        sp.dma_start(O[8][0, 0].rearrange("h d e -> d h e"), state[:, NCH]).then_inc(s_out, 16)
        evacuated(sp, ("US", N_SAMPLE - 1))
        sp.dma_start(O[17][0].rearrange("b h d e -> d b h e"), sstate[:, :, :, :]).then_inc(s_out, 16)
        for s in s_end["nsa"]:
            sp.wait_ge(s, 1)
        sp.dma_start(memp[:, :, :], A["mem_prompt"][0].rearrange("(t p) d -> p t d", p=P)).then_inc(s_mem, 16)
        sp.dma_start(lnp[:, 0, :], A["ln1_g"].to_broadcast([P, D])).then_inc(s_lnp, 16)
        sp.dma_start(lnp[:, 1, :], A["ln1_b"].to_broadcast([P, D])).then_inc(s_lnp, 16)
        for n in range(9, 13):
            weights(n)
        for i, (buf, key) in enumerate(((mkt, "mk"), (mvt, "mv"))):
            for c in range(2):
                for t in range(2):
                    evacuated(sp, (key, c, t))
            sp.dma_start(O[9 + i][0, 0].rearrange("(t p) h d -> p t (h d)", p=P), buf[:, :, :]).then_inc(s_mkout, 16)
        weights(13)
        sp.wait_ge(s_ln, 3)
        sp.dma_start(lnp[:, 0, :], A["ln2_g"].to_broadcast([P, D])).then_inc(s_lnp, 16)
        sp.dma_start(lnp[:, 1, :], A["ln2_b"].to_broadcast([P, D])).then_inc(s_lnp, 16)
        for n in range(14, 19):
            weights(n)
        sp.wait_ge(s_ln, 6)
        sp.wait_ge(s_mkout, 32)
        for s in s_end["mem"]:
            sp.wait_ge(s, 1)
        sp.dma_start(skey[:, :, :], A["peer_sub_keys"][0].rearrange("h c k d -> k (h c) d")).then_inc(s_skey, 16)
        sp.dma_start(lnp3[:, 0, :], A["ln3_g"].to_broadcast([P, D])).then_inc(s_lnp, 16)
        sp.dma_start(lnp3[:, 1, :], A["ln3_b"].to_broadcast([P, D])).then_inc(s_lnp, 16)
        weights(19)
        weights(20)
        for q in range(1, 4):
            sp.dma_start(xt[32 * q:32 * q + 32, 2, :], xt[0:32, 2, :]).then_inc(s_fold, 16)
        sp.wait_ge(s_route, 12)
        for q in range(4):
            h0 = NGRP + 2 * q
            sp.dma_start(E_all[32 * q:32 * q + 32, 16:18, :], E_all[0:32, h0:h0 + 2, :]).then_inc(s_fold, 16)
            sp.dma_start(W_all[32 * q:32 * q + 32, 16:18, :], W_all[0:32, h0:h0 + 2, :]).then_inc(s_fold, 16)
        sp.wait_ge(s_ln, 8)
        sp.dma_start(O[0][0].rearrange("(t p) d -> p t d", p=P), xt[:, 0:2, :]).then_inc(s_out, 16)
        sp.wait_ge(s_ln, 9)
        sp.dma_start(O[1].rearrange("b s d -> (b s) d"), xt[0:32, 2, :]).then_inc(s_out, 16)
        sp.wait_ge(s_out, 64)
        sp.wait_ge(s_kvout, 192)

    @block.gpsimd
    def _(pool):
        def gather(dst, table, index, done):
            return nc.gpsimd.indirect_dma_start(out=dst, out_offset=None, in_=table,
                                                in_offset=bass.IndirectOffsetOnAxis(ap=index, axis=0)).then_inc(done, 16)

        pages = A["page_table"].rearrange("b j -> (b j)").rearrange("(i q) -> q i", q=16)
        for q in range(16):
            nc.gpsimd.dma_start(pt[8 * q:8 * q + 8, :], pages[q:q + 1, :].to_broadcast([8, 4]), allow_slow_non_contiguous=True).then_inc(s_pt, 16)
        pool.wait_ge(s_idx, 1)
        fetches = []
        for kv, cache in enumerate((A["cache_k_cmp"], A["cache_v_cmp"])):
            rows = cache[0].rearrange("n (r s) g d -> (n r) (s g d)", s=16)
            for i in range(4):
                fetches.append((rows, i))
        gather(sub[:, 0, :], fetches[0][0], idx[:, 0:1], s_sub[0])
        for n, (rows, i) in enumerate(fetches):
            if n + 1 < len(fetches):
                gather(sub[:, (n + 1) % NSUBS, :], fetches[n + 1][0], idx[:, fetches[n + 1][1]:fetches[n + 1][1] + 1], s_sub[(n + 1) % NSUBS])
            pool.wait_ge(s_sub[n % NSUBS], 16 * (n // NSUBS + 1))
            if n >= 1:
                filled(pool, ("subT", (n - 1) // 4, (n - 1) % 4, 3))
            nc.gpsimd.tensor_copy(subg[:, :].rearrange("p (g s d) -> p g s d", g=2, s=16),
                                  sub[:, n % NSUBS, :].rearrange("p (s g d) -> p g s d", g=2, s=16)).then_inc(s_sorted, 1)
            pool.wait_ge(s_sorted, n + 1)
        pool.wait_ge(s_sgate, 2)
        pool.wait_ge(s_par, 16 * 8)
        for ts, rows in ((slice(0, 2), P), (slice(2, 3), 32)):
            gate = z[0:rows, ts, HG:HG + 512].rearrange("p t (h e) -> p t h e", e=P)
            for t in range(ts.stop - ts.start):
                ins = nc.gpsimd.tensor_tensor(gate[:, t], gate[:, t], bc(hng[0:rows], 1, H), ALU.mult)
            ins.then_inc(s_gz, 1)
        for s in s_end["hgrn"]:
            pool.wait_ge(s, 1)
        pool.wait_ge(s_out, 32)
        pages = A["page_table"].rearrange("b j -> j b")
        for q in range(8):
            nc.gpsimd.dma_start(ptab[16 * q:16 * q + 16, :], pages[q:q + 1, :].to_broadcast([16, 8]), allow_slow_non_contiguous=True).then_inc(s_pt, 16)
        pool.wait_ge(s_idx, 2)
        rk, rv = (A[n][0].rearrange("n (r s) g d -> (n r) (s g d)", s=8) for n in ("cache_k_slc", "cache_v_slc"))
        for b in range(N_SAMPLE):
            u, b4 = b // 4, b % 4
            if b >= 2:
                filled(pool, ("skT", (b - 2) // 4, (b - 2) % 4, 2))
            gather(slk[:, b % 2, :], rk, sidx[:, b:b + 1], s_slk[b % 2])
            nc.gpsimd.dma_start(wk[:, b % 2, :], A["cache_k_win"][0, b].rearrange("(p s) g d -> p (s g d)", s=4)).then_inc(s_slk[b % 2], 16)
            if b == 4:
                filled(pool, ("spv", 0))
            gather(slv[:, b4, :], rv, sidx[:, b:b + 1], s_slv[b4])
            nc.gpsimd.dma_start(wv[:, b4, :], A["cache_v_win"][0, b].rearrange("(p s) g d -> p (s g d)", s=4)).then_inc(s_slv[b4], 16)
        for s in s_end["nsa"]:
            pool.wait_ge(s, 1)
        for b in range(N_SAMPLE):
            if b >= 2:
                filled(pool, ("mkT", b - 1, 3))
            nc.gpsimd.dma_start(mck[:, b % 2, :, :], A["cache_mem_k"][0, b].rearrange("(p i) h d -> p i (h d)", i=2)).then_inc(s_mck[b % 2], 16)
            if b == 4:
                filled(pool, ("smo", 0, 1))
            nc.gpsimd.dma_start(mcv[:, b % 4, :, :], A["cache_mem_v"][0, b].rearrange("(p i) h d -> p i (h d)", i=2)).then_inc(s_mcv[b % 4], 16)
        u_count, v_count = (pool.alloc_register(n) for n in ("u_count", "v_count"))
        pool.reg_mov(u_count, 1)
        pool.reg_mov(v_count, 1)

        def slot_read(free, count, g, k):
            if isinstance(g, int):
                pool.wait_ge(free, GRP * g + k + 1)
            else:
                pool.wait_ge(free, count)
                pool.reg_add(count, count, 1)

        def two_turns(pair):
            for odd in range(2):
                g = pair * 2 + odd
                nc.gpsimd.tensor_copy(E_cur[:, odd, :], E_all[:, bass.ds(g, 1), :].rearrange("p a k -> p (a k)")).then_inc(pool_step, 1)
                pool.wait_ge(pool_step, g + 1)
                for k in range(GRP):
                    slot_read(u_free, u_count, g, k)
                    gather(uslot[k], A["peer_u"][0], E_cur[:, odd, k:k + 1], s_u[k % 8])
                for k in range(GRP):
                    slot_read(v_free, v_count, g, k)
                    gather(vslot[k], A["peer_v"][0], E_cur[:, odd, k:k + 1], s_v[k])

        with pool.Fori(0, 8) as pair:
            pool.wait_ge(s_route, pair + 1)
            two_turns(pair)
        pool.wait_ge(s_fold, 16 * 11)
        two_turns(8)

    @block.scalar
    def _(act):
        S = Lane(act, act_step)
        copy_xT(act, "xT")
        copy_z(act)
        act.wait_ge(s_lb, 1)
        S(nc.scalar.activation(lb, small[:, 0:4], ACT.Sigmoid), s_lb)
        act.wait_ge(s_par, 16 * 8)
        for kv in range(2):
            copy_subT(act, kv)
            if kv == 1:
                filled(act, ("kcTp",))
            for g in range(2):
                filled(act, ("hid", kv, g))
                release(act, nc.scalar.activation(hid[:, g, 0:504], bank(("hid", kv, g))[:, 0:504], ACT.Gelu_apprx_tanh,
                                                  bias=b1[:, kv:kv + 1]), ("hid", kv, g))
            filled(act, ("hidp", kv))
            release(act, nc.scalar.activation(hid[:, :, 504:519], split(bank(("hidp", kv))[:, 0:30], 15), ACT.Gelu_apprx_tanh,
                                              bias=b1[:, kv:kv + 1]), ("hidp", kv), wait=True)
        filled(act, ("vcp",))
        act.sem_inc(s_end["cmp"][1], 1)
        for s in s_end["cmp"]:
            act.wait_ge(s, 1)
        for t in range(3):
            t0, n = toks(t)
            filled(act, ("hfT", t))
            S(nc.scalar.activation(e1[:, :, t0:t0 + n], split(bank(("hfT", t)), P)[:, :, 0:n], ACT.Sigmoid))
            release(act, nc.scalar.activation(kT[:, :, t0:t0 + n], split(bank(("hfT", t)), P)[:, :, 0:n], ACT.Sigmoid, scale=-1.0),
                    ("hfT", t))
        for t, rows in ((slice(0, 2), P), (slice(2, 3), 32)):
            S(nc.scalar.activation(z[0:rows, t, HG:HG + 512], z[0:rows, t, HG:HG + 512], ACT.Sigmoid), s_sgate)
            S(nc.scalar.activation(z[0:rows, t, NG:NG + 24], z[0:rows, t, NG:NG + 24], ACT.Sigmoid), s_gates)
        act.wait_ge(s_f, 1)
        S(nc.scalar.activation(e2, e1, ACT.Ln), s_lnf)
        act.wait_ge(s_g, 1)
        S(nc.scalar.activation(e2, e1, ACT.Exp), wait=False)
        S(nc.scalar.activation(e3, e1, ACT.Exp, scale=-1.0), s_hexp)
        act.wait_ge(s_g, 2)
        S(nc.scalar.activation(G, G, ACT.Exp), wait=False)
        S(nc.scalar.activation(dec[:, :, :], dec[:, :, :], ACT.Exp), wait=False)
        S(nc.scalar.activation(e1, e1, ACT.Exp), s_hexp)
        for t in range(3):
            n = toks(t)[1]
            filled(act, ("kE", t))
            release(act, nc.scalar.copy(ktok[0:n, t], split(bank(("kE", t)), P)[0:n]), ("kE", t))
        evacuated(act, ("xT", 2, 1))
        filled(act, ("z", 6, 2))
        for t in range(3):
            n = toks(t)[1]
            filled(act, ("oin", t))
            release(act, nc.scalar.copy(otok[0:n, t], split(bank(("oin", t)), P)[0:n]), ("oin", t), wait=True)
        act.wait_ge(s_ms, 1)
        S(nc.scalar.activation(small[:, 16:28], small[:, 0:12], ACT.Sqrt), s_rs)
        act.sem_inc(s_end["hgrn"][1], 1)
        for s in s_end["hgrn"]:
            act.wait_ge(s, 1)
        for t in range(3):
            t0, n = toks(t)
            filled(act, ("nqT", t))
            release(act, nc.scalar.mul(qn[:, :, t0:t0 + n], split(bank(("nqT", t)), P)[:, :, 0:n], 0.125), ("nqT", t))
        for t in range(2):
            K = P * (t + 1)
            act.wait_ge(s_mx, 2 * t + 1)
            S(nc.scalar.activation(PCp[:, :, :], PCp[:, :, :], ACT.Exp), s_exp)
            act.wait_ge(s_mx, 2 * t + 2)
            for br in range(2):
                for h in range(8):
                    i = 8 * br + h
                    S(nc.scalar.activation(PS[:, br, h, 0:K], PS[:, br, h, 0:K], ACT.Exp, bias=small[:, i:i + 1],
                                           accum_out=small[:, 16 + i:17 + i]), s_exp if i == 15 else None, wait=(i == 15))
            if t == 0:
                for k in range(3):
                    copy_oT(act, k)
            copy_pT(act, t)
        evacuated(act, ("pv", 1))
        for u in range(2):
            copy_skT(act, u)
            act.wait_ge(s_cmx, u + 1)
            S(nc.scalar.activation(LC[:, 0, :], LC[:, 0, :], ACT.Exp, bias=small[:, 64:65], accum_out=small[:, 65:66]), s_cexp)
            act.wait_ge(s_smx, u + 1)
            S(nc.scalar.activation(L[:, 0:1056], L[:, 0:1056], ACT.Exp, bias=small[:, 72:73], accum_out=small[:, 74:75]), wait=False)
            S(nc.scalar.activation(L[:, 1056:1600], L[:, 1056:1600], ACT.Exp, bias=small[:, 73:74], accum_out=small[:, 75:76]), s_sexp)
            copy_spT(act, u)
        evacuated(act, ("spvT", 1))
        act.sem_inc(s_end["nsa"][1], 1)
        for s in s_end["nsa"]:
            act.wait_ge(s, 1)

        def roots(k, tiles=range(3)):
            for t in tiles:
                n = toks(t)[1]
                act.wait_ge(s_lnv, 3 * k + t + 1)
                S(nc.scalar.activation(small[0:n, 104 + t:105 + t], small[0:n, 100 + t:101 + t], ACT.Sqrt), s_lnr)

        roots(0, range(2))
        copy_xT(act, "memT", 2, memT)
        roots(0, range(2, 3))
        copy_mkv(act)
        copy_xT(act, "x1T")
        copy_mq(act)
        copy_mkT(act, 0)
        for t in range(2):
            act.wait_ge(s_mmx, t + 1)
            for h in range(H):
                ins = nc.scalar.activation(Pm[:, h, :], bank(("ms", t, h // 2))[:, 256 * (h % 2):256 * (h % 2) + 256], ACT.Exp,
                                           bias=small[:, 80 + h:81 + h], accum_out=small[:, 84 + h:85 + h])
                if h % 2:
                    release(act, ins, ("ms", t, h // 2))
                else:
                    S(ins, wait=False)
            copy_mp(act, t)
        for u in range(2):
            for b in range(4):
                copy_mkT(act, 1 + 4 * u + b)
                copy_sms(act, u, b)
            act.wait_ge(s_mmx, 3 + u)
            S(nc.scalar.activation(Pm[:, 0, :], Pm[:, 0, :], ACT.Exp, bias=small[:, 80:81], accum_out=small[:, 84:85]), s_mexp)
            copy_smpT(act, u)
        evacuated(act, ("smoT", 1, 1))
        act.sem_inc(s_end["mem"][1], 1)
        roots(1)
        for s in s_end["mem"]:
            act.wait_ge(s, 1)
        copy_skeyT(act)
        copy_xT(act, "x2T")
        copy_pq(act, 0, 4)
        copy_ps(act, 0, [0])
        copy_pq(act, 4, 8)
        act.wait_ge(s_tmx, 1)
        S(nc.scalar.activation(R2["texp"][:, :, :], R2["texp"][:, :, :], ACT.Exp), s_texp)
        copy_pq(act, 8, 16)
        for t in range(3):
            copy_ps(act, t, range(1 if t == 0 else 0, 4))

        def turn(g):
            act.wait_ge(h_done, g + 1)
            nc.scalar.activation(g_cur[:, :], h_cur[:, :], ACT.Gelu_apprx_tanh).then_inc(gelu_done, 1)
            act.wait_ge(w_done, g + 1)
            for k in range(GRP):
                act.wait_ge(v_free, GRP * g + k + 1)
                nc.scalar.activation(diag[:, k, :], ident, ACT.Copy, scale=w_cur[:, k:k + 1]).then_inc(diag_done, 1)

        with act.Fori(0, 11) as g:
            turn(g)
            act.wait_ge(s_tmx, g + 2)
            nc.scalar.activation(R2["texp"][:, :, :], R2["texp"][:, :, :], ACT.Exp).then_inc(s_texp, 1)
        with act.Fori(11, 16) as g:
            turn(g)
        roots(2, range(2))
        with act.Fori(16, NGRP) as g:
            turn(g)
        roots(2, range(2, 3))

    @block.vector
    def _(dve):
        V = Lane(dve, dve_step)
        v = nc.vector

        copy_xT(dve, "xT")
        dve.wait_ge(s_const, 32)
        dve.wait_ge(s_pt, 16 * 16)
        V(v.tensor_scalar(idx[:, :], pt[:, :], 8.0, C("mod8"), ALU.mult, ALU.add), s_idx)
        dve.wait_ge(s_par, 16 * 8)
        V(v.tensor_tensor(small[:, 0:4], lbl[:, 0, :], lbl[:, 1, :], ALU.subtract), s_lb)
        copy_z(dve)
        dve.wait_ge(s_lb, 2)
        V(v.tensor_scalar(omlb, lb, -1.0, 1.0, ALU.mult, ALU.add))
        copy_subT(dve, 0)
        for key, o, w in ((("kcT",), 0, 504), (("kcTp",), 504, NCP)):
            filled(dve, key)
            release(dve, v.tensor_scalar(kcT[:, o:o + w], bank(key)[:, 0:w], b2k, None, ALU.add), key)
        copy_subT(dve, 1)
        for k in range(2):
            filled(dve, ("vc", k))
            release(dve, v.tensor_tensor(vcS[0:NCB, 4 * k:4 * k + 4, :], split(bank(("vc", k))[0:NCB], P), bc(b2v[0:NCB], 1, 4), ALU.add), ("vc", k))
        filled(dve, ("vcp",))
        release(dve, v.tensor_tensor(vcP[0:NCP, :], bank(("vcp",))[0:NCP, 0:P], b2v[0:NCP], ALU.add), ("vcp",), wait=True)
        dve.sem_inc(s_end["cmp"][0], 1)
        for s in s_end["cmp"]:
            dve.wait_ge(s, 1)

        V(v.memset(state[:, 0], 0.0), wait=False)
        for t in range(3):
            t0, n = toks(t)
            filled(dve, ("hqT", t))
            release(dve, v.tensor_copy(qT[:, :, t0:t0 + n], split(bank(("hqT", t)), P)[:, :, 0:n]), ("hqT", t))
        evacuated(dve, ("hfT", 2))
        for h in range(H):
            V(v.tensor_scalar(e1[:, h, :], e1[:, h, :], omlb[:, h:h + 1], lb[:, h:h + 1], ALU.mult, ALU.add), wait=False)
        for h in range(H):
            V(v.tensor_scalar(kT[:, h, :], kT[:, h, :], omlb[:, h:h + 1], None, ALU.mult), s_f if h == 3 else None, wait=(h == 3))
        dve.wait_ge(s_lnf, 1)
        for h in range(H):
            V(v.tensor_tensor_scan(G[:, h, :], C("keep"), e2[:, h, :], 0.0, ALU.mult, ALU.add), wait=(h == 3))
        Gp = G[:, :, 0:T_PROMPT].rearrange("p h (c s) -> p h c s", s=CH)
        Gs = G[:, :, T_PROMPT:TOK].rearrange("p h (b s) -> p h b s", s=STEPS)
        Ep = e1[:, :, 0:T_PROMPT].rearrange("p h (c s) -> p h c s", s=CH)
        Es = e1[:, :, T_PROMPT:TOK].rearrange("p h (b s) -> p h b s", s=STEPS)
        for h in range(H):
            V(v.tensor_tensor(Ep[:, h], Gp[:, h], Gp[:, h, :, CH // 2 - 1:CH // 2].to_broadcast([P, NCH, CH]), ALU.subtract), wait=False)
        V(v.tensor_copy(e1[:, :, T_PROMPT:TOK], G[:, :, T_PROMPT:TOK]), s_g)
        dve.wait_ge(s_hexp, 1)
        V(v.tensor_tensor(e2, qT[:, :, :], e2, ALU.mult), wait=False)
        V(v.tensor_tensor(e3, kT[:, :, :], e3, ALU.mult), s_ke)
        for h in range(H):
            V(v.tensor_tensor(Ep[:, h], Gp[:, h, :, CH - 1:CH].to_broadcast([P, NCH, CH]), Gp[:, h], ALU.subtract), wait=False)
            V(v.tensor_tensor(Es[:, h], Gs[:, h, :, STEPS - 1:STEPS].to_broadcast([P, N_SAMPLE, STEPS]), Gs[:, h], ALU.subtract), wait=False)
        V(v.tensor_copy(dec[:, :, 0:NCH], Gp[:, :, :, CH - 1]), wait=False)
        V(v.tensor_copy(dec[:, :, NCH:], Gs[:, :, :, STEPS - 1]), s_g)
        dve.wait_ge(s_hexp, 2)
        V(v.tensor_tensor(qT[:, :, :], qT[:, :, :], G, ALU.mult), wait=False)
        V(v.tensor_tensor(kT[:, :, :], kT[:, :, :], e1, ALU.mult), s_ke)
        for h in range(H):
            V(v.tensor_tensor(qGm[:, h], C("bmask", 32), bc(qT[:, h, T_PROMPT:TOK], 1, N_SAMPLE), ALU.mult), s_ke if h == 3 else None, wait=(h == 3))
        for t in range(3):
            n = toks(t)[1]
            filled(dve, ("att", t))
            m = C("hmask") if t < 2 else C("hmask_s")[0:32]
            release(dve, v.tensor_tensor(attS[0:n, t, :, 0:n], split(bank(("att", t)), P)[0:n, :, 0:n], bc(m, 1, H), ALU.mult), ("att", t), wait=True)
        for b in range(N_SAMPLE):
            V(v.tensor_scalar(vm[0:32, b, :], z[0:32, 2, HI:HI + 512], C("brow")[0:32, b:b + 1], None, ALU.mult), s_vm, wait=False)
        for c in range(NCH):
            key = ("U", c)
            filled(dve, key)
            for h in range(H):
                ins = v.scalar_tensor_tensor(out=state[:, c + 1, h, :], in0=state[:, c, h, :], scalar=dec[:, h, c:c + 1],
                                             in1=bank(key)[:, P * h:P * h + P], op0=ALU.mult, op1=ALU.add)
                if h < 3:
                    V(ins, wait=False)
                else:
                    release(dve, ins, key, wait=True)
        for t in range(3):
            n = toks(t)[1]
            filled(dve, ("ost", t))
            evacuated(dve, ("oin", t))
            release(dve, v.tensor_tensor(otok[0:n, t], split(bank(("ost", t)), P)[0:n], otok[0:n, t], ALU.add), ("ost", t), wait=True)
        for b in range(N_SAMPLE):
            key = ("US", b)
            filled(dve, key)
            for h in range(H):
                ins = v.scalar_tensor_tensor(out=sstate[:, b, h, :], in0=sstate[:, b, h, :], scalar=dec[:, h, NCH + b:NCH + b + 1],
                                             in1=bank(key)[:, P * h:P * h + P], op0=ALU.mult, op1=ALU.add)
                if h < 3:
                    V(ins, wait=False)
                else:
                    release(dve, ins, key)
        V(v.memset(small[:, 0:12], 1.0))
        last = (2, H - 1)
        for t in range(3):
            n = toks(t)[1]
            for h in range(H):
                i, o = 4 * t + h, otok[0:n, t, h, :]
                V(v.tensor_tensor_reduce(out=attS[0:n, t, h, :], in0=o, in1=o, scale=1.0, scalar=0.0, op0=ALU.mult, op1=ALU.add,
                                         accum_out=small[0:n, i:i + 1]), wait=((t, h) == last))
        V(v.tensor_scalar(small[:, 0:12], small[:, 0:12], 1.0 / P, EPS, ALU.mult, ALU.add), s_ms)
        dve.wait_ge(s_rs, 1)
        V(v.reciprocal(small[:, 32:44], small[:, 16:28]))
        dve.wait_ge(s_gz, 2)
        for t in range(3):
            n = toks(t)[1]
            for h in range(H):
                i, o = 4 * t + h, otok[0:n, t, h, :]
                V(v.scalar_tensor_tensor(out=o, in0=o, scalar=small[0:n, 32 + i:33 + i], in1=z[0:n, t, HG + P * h:HG + P * h + P],
                                         op0=ALU.mult, op1=ALU.mult), s_otok if h == H - 1 else None, wait=((t, h) == last))
        dve.sem_inc(s_end["hgrn"][0], 1)
        for s in s_end["hgrn"]:
            dve.wait_ge(s, 1)
        dve.wait_ge(s_out, 32)

        dve.wait_ge(s_pt, 16 * 24)
        V(v.tensor_scalar(sidx[:, :], ptab[:, :], 16.0, C("mod16"), ALU.mult, ALU.add), s_idx)
        V(v.memset(qpad[:, :, :], 0.0))
        for u in range(2):
            filled(dve, ("gs", u))
            release(dve, v.tensor_tensor(small[:, 32:56], bank(("gs", u))[:, 0:24], C("headsel"), ALU.mult), ("gs", u), wait=True)
            V(v.tensor_reduce(gsm[:, u, :], small[:, 32:56].rearrange("p (h c) -> p c h", c=3), AX, ALU.add))
        evacuated(dve, ("nqT", 2))
        for g in range(2):
            rows = slice(64 * g, 64 * g + 64)
            V(v.tensor_copy(qpad[rows].rearrange("p b (g j t) -> p b g j t", g=2, j=4)[:, :, g],
                            qn[rows, :, T_PROMPT:TOK].rearrange("p j (b t) -> p b j t", t=STEPS)), s_qpad)
        for t in range(3):
            t0, n = toks(t)
            filled(dve, ("nkT", t))
            release(dve, v.tensor_copy(kn[:, :, t0:t0 + n], split(bank(("nkT", t))[:, 0:256], P)[:, :, 0:n]), ("nkT", t))
        for t in range(2):
            K = P * (t + 1)
            if t == 1:
                filled(dve, ("pcT", 0, 1))
            for g in range(2):
                key, hs = ("sc", t, g), slice(4 * g, 4 * g + 4)
                filled(dve, key)
                release(dve, v.tensor_tensor(PCp[:, hs, :], split(bank(key)[:, 0:4 * NCP], NCP), C("cbias", 8, NCP)[:, t, hs], ALU.add), key, wait=True)
            V(v.tensor_reduce(small[:, 48:56], PCp[:, :, :], AX, ALU.max))
            V(v.tensor_tensor(PCp[:, :, :], PCp[:, :, :], bc(small[:, 48:56], 2, NCP), ALU.subtract), s_mx)
            dist = C("dist")[:, 256 - K:256] if t == 0 else C("dist")
            per = 4 // (t + 1)
            for br in range(2):
                for k in range(2 * (t + 1)):
                    key = ("s", t, br, k)
                    filled(dve, key)
                    for i in range(per):
                        h = per * k + i
                        ins = v.scalar_tensor_tensor(out=PS[:, br, h, 0:K], in0=dist, scalar=SLOPES[h], in1=bank(key)[:, K * i:K * i + K],
                                                     op0=ALU.mult, op1=ALU.add)
                        if i < per - 1:
                            V(ins, wait=False)
                        else:
                            release(dve, ins, key, wait=(k == 2 * t + 1))
            V(v.tensor_reduce(small[:, 0:16], PS[:, :, :, 0:K].rearrange("p b h k -> p (b h) k"), AX, ALU.max))
            V(v.tensor_scalar(small[:, 0:16], small[:, 0:16], -1.0, None, ALU.mult), s_mx)
            dve.wait_ge(s_exp, 2 * t + 1)
            gate = z[:, t, NG:NG + 24].rearrange("p (h c) -> p c h", c=3)
            dve.wait_ge(s_gates, 2)
            V(v.tensor_reduce(small[:, 48:56], PCp[:, :, :], AX, ALU.add))
            V(v.reciprocal(small[:, 56:64], small[:, 48:56]))
            V(v.tensor_tensor(small[:, 56:64], small[:, 56:64], gate[:, 0], ALU.mult))
            V(v.tensor_tensor(PCp[:, :, :], PCp[:, :, :], C("cmask", 8, NCP)[:, t], ALU.mult))
            V(v.tensor_tensor(PCp[:, :, :], PCp[:, :, :], bc(small[:, 56:64], 2, NCP), ALU.mult))
            dve.wait_ge(s_exp, 2 * t + 2)
            V(v.reciprocal(small[:, 32:48], small[:, 16:32]))
            V(v.tensor_tensor(split(small[:, 32:48], 8), split(small[:, 32:48], 8), gate[:, 1:3], ALU.mult))
            pv_ = PS[:, :, :, 0:K].rearrange("p b h k -> p (b h) k")
            V(v.tensor_tensor(pv_, pv_, bc(small[:, 32:48], 2, K), ALU.mult), s_pn)
            if t == 0:
                for k in range(3):
                    copy_oT(dve, k)
            copy_pT(dve, t)
            filled(dve, ("pv", t))
            release(dve, v.tensor_copy(mixT[:, 4:8, P * t:P * t + P], split(bank(("pv", t)), P)), ("pv", t), wait=True)
        evacuated(dve, ("pT", 1, 7))
        evacuated(dve, ("pcT", 1, 1))
        for u in range(2):
            if u == 1:
                evacuated(dve, ("spT", 0, 3))
            filled(dve, ("sc4", u))
            release(dve, v.tensor_tensor(LC[:, 0, :], bank(("sc4", u))[:, 0:NCB], C("bcmp"), ALU.add), ("sc4", u), wait=True)
            V(v.tensor_reduce(small[:, 64:65], LC[:, 0, :], AX, ALU.max))
            V(v.tensor_scalar(small[:, 64:65], small[:, 64:65], -1.0, None, ALU.mult), s_cmx)
            copy_skT(dve, u)
            dve.wait_ge(s_cexp, u + 1)
            V(v.reciprocal(small[:, 66:67], small[:, 65:66]))
            V(v.tensor_scalar(LC[:, 0, :], LC[:, 0, :], small[:, 66:67], None, ALU.mult))
            V(v.tensor_scalar(LC[:, 1, :], LC[:, 0, :], gsm[:, u, 0:1], None, ALU.mult), s_cpn)
            filled(dve, ("spcT", u))
            release(dve, v.tensor_copy(pcs[0:NCB, :, :], split(bank(("spcT", u))[0:NCB, 0:256], P)), ("spcT", u))
            filled(dve, ("imp", u))
            release(dve, v.tensor_copy(small[:, 108:125], bank(("imp", u))[:, 0:17]), ("imp", u))
            filled(dve, ("impj", u))
            release(dve, v.tensor_copy(small[:, 128:145], bank(("impj", u))[:, 0:17]), ("impj", u), wait=True)
            V(v.tensor_reduce(small[:, 68:69], small[:, 129:144], AX, ALU.min))
            V(v.tensor_scalar(small[:, 108:123], small[:, 129:144], small[:, 68:69], None, ALU.is_equal))
            V(v.tensor_tensor(small[:, 108:123], small[:, 108:123], C("blk")[:, 1:16], ALU.mult))
            V(v.tensor_reduce(small[:, 69:70], small[:, 108:123], AX, ALU.max))
            for k in range(2):
                filled(dve, ("ss", u, k))
                release(dve, v.tensor_tensor(L[:, 512 * k:512 * k + 512], bank(("ss", u, k)), C("bsel")[:, 512 * k:512 * k + 512], ALU.add), ("ss", u, k))
            filled(dve, ("sw", u))
            release(dve, v.tensor_tensor(L[:, 1056:1568], bank(("sw", u)), C("bwin"), ALU.add), ("sw", u))
            filled(dve, ("sn", u))
            V(v.tensor_tensor(L[:, 1024:1056], bank(("sn", u))[:, 0:32], C("bnew", 32)[:, u], ALU.add), wait=False)
            release(dve, v.tensor_tensor(L[:, 1568:1600], bank(("sn", u))[:, 32:64], C("bnew", 32)[:, u], ALU.add), ("sn", u), wait=True)
            V(v.tensor_scalar(pen[:, :], C("pblk"), small[:, 69:70], NEG, ALU.is_equal, ALU.mult))
            V(v.tensor_tensor(split(L[:, 0:1024], P), split(L[:, 0:1024], P), bc(pen[:, :], 1, 8), ALU.add))
            V(v.tensor_reduce(small[:, 70:71], L[:, 0:1056], AX, ALU.max), wait=False)
            V(v.tensor_reduce(small[:, 71:72], L[:, 1056:1600], AX, ALU.max))
            V(v.tensor_scalar(small[:, 72:74], small[:, 70:72], -1.0, None, ALU.mult), s_smx)
            dve.wait_ge(s_sexp, u + 1)
            V(v.reciprocal(small[:, 76:78], small[:, 74:76]))
            V(v.tensor_tensor(small[:, 76:78], small[:, 76:78], gsm[:, u, 1:3], ALU.mult))
            V(v.tensor_scalar(L[:, 0:1056], L[:, 0:1056], small[:, 76:77], None, ALU.mult), wait=False)
            V(v.tensor_scalar(L[:, 1056:1600], L[:, 1056:1600], small[:, 77:78], None, ALU.mult), s_spn)
            copy_spT(dve, u)
            filled(dve, ("spv", u))
            release(dve, v.tensor_copy(ov[:, :], bank(("spv", u))[:, 0:P]), ("spv", u))
            filled(dve, ("spvT", u))
            for g in range(2):
                rows = slice(64 * g, 64 * g + 64)
                src = bank(("spvT", u))[rows, 0:P].rearrange("p (b g j t) -> p g j b t", g=2, j=4, t=STEPS)[:, g]
                dst = mixT[rows, 4:8, T_PROMPT + 16 * u:T_PROMPT + 16 * u + 16].rearrange("p j (b t) -> p j b t", t=STEPS)
                if g == 0:
                    V(v.tensor_copy(dst, src), wait=False)
                else:
                    release(dve, v.tensor_copy(dst, src), ("spvT", u), wait=True)
        dve.sem_inc(s_end["nsa"][0], 1)
        for s in s_end["nsa"]:
            dve.wait_ge(s, 1)

        def residual(name, t):
            for c in range(2):
                n = toks(t)[1]
                x = xt[0:n, t, GW * c:GW * c + GW]
                filled(dve, (name, c, t))
                release(dve, v.scalar_tensor_tensor(out=x, in0=x, scalar=ALPHA, in1=bank((name, c, t))[0:n], op0=ALU.mult, op1=ALU.add),
                        (name, c, t), wait=True)

        def norm(k, t, lnp):
            n = toks(t)[1]
            x = xt[0:n, t, :]
            for c in range(2):
                V(v.bn_stats(small[0:n, 150 + 6 * c:156 + 6 * c], x[:, 512 * c:512 * c + 512]), wait=(c == 1))
            V(v.bn_aggr(small[0:n, 162 + 2 * t:164 + 2 * t], small[0:n, 150:162]))
            V(v.tensor_scalar(small[0:n, 100 + t:101 + t], small[0:n, 163 + 2 * t:164 + 2 * t], EPS, None, ALU.add), s_lnv)
            dve.wait_ge(s_lnr, 3 * k + t + 1)
            V(v.reciprocal(small[0:n, 96 + t:97 + t], small[0:n, 104 + t:105 + t]))
            dve.wait_ge(s_lnp, 32 * (k + 1))
            V(v.tensor_scalar(x, x, small[0:n, 162 + 2 * t:163 + 2 * t], small[0:n, 96 + t:97 + t], ALU.subtract, ALU.mult))
            V(v.tensor_tensor(x, x, lnp[0:n, 0, :], ALU.mult))
            V(v.tensor_tensor(x, x, lnp[0:n, 1, :], ALU.add), s_ln)

        V(v.memset(qpm[:, :, :, :], 0.0))
        for t in range(3):
            residual("wo", t)
            if t == 2:
                copy_xT(dve, "memT", 2, memT)
            norm(0, t, lnp)
        copy_mkv(dve)
        copy_xT(dve, "x1T")
        copy_mq(dve)
        evacuated(dve, ("mq", KC - 1))
        evacuated(dve, ("mq", KC - 2))
        for c in range(KC):
            o = 4 * (c // 2)
            V(v.tensor_copy(qpm[:, :, c, o:o + 4], mqT[:, c, T_PROMPT:TOK].rearrange("p (b t) -> p b t", t=STEPS)), s_mpad, wait=False)
        copy_mkT(dve, 0)
        for t in range(2):
            for k in range(2):
                filled(dve, ("ms", t, k))
                V(v.tensor_reduce(small[:, 88 + 2 * k:90 + 2 * k], split(bank(("ms", t, k)), 256), AX, ALU.max))
            if t == 1:
                filled(dve, ("mpT", 0, 1))
            V(v.tensor_scalar(small[:, 80:84], small[:, 88:92], -1.0, None, ALU.mult), s_mmx)
            evacuated(dve, ("ms", t, 1))
            V(v.reciprocal(small[:, 92:96], small[:, 84:88]))
            V(v.tensor_tensor(Pm[:, :, :], Pm[:, :, :], bc(small[:, 92:96], 2, 256), ALU.mult), s_mpn)
            copy_mp(dve, t)
        filled(dve, ("mpT", 1, 1))
        for u in range(2):
            for b in range(4):
                copy_mkT(dve, 1 + 4 * u + b)
                copy_sms(dve, u, b)
            evacuated(dve, ("sms", u, 3))
            evacuated(dve, ("sms", u, 2))
            V(v.tensor_reduce(small[:, 88:89], Pm[:, 0, :], AX, ALU.max))
            V(v.tensor_scalar(small[:, 80:81], small[:, 88:89], -1.0, None, ALU.mult), s_mmx)
            dve.wait_ge(s_mexp, u + 1)
            V(v.reciprocal(small[:, 92:93], small[:, 84:85]))
            V(v.tensor_scalar(Pm[:, 0, :], Pm[:, 0, :], small[:, 92:93], None, ALU.mult), s_mpn)
            copy_smpT(dve, u)
            for k in range(2):
                filled(dve, ("smo", u, k))
                release(dve, v.tensor_copy(so[:, GW * k:GW * k + GW], bank(("smo", u, k))), ("smo", u, k))
            for k in range(2):
                key = ("smoT", u, k)
                filled(dve, key)
                for m in range(2):
                    h, c = 2 * k + m, 4 * k + 2 * m
                    dst = mixT[:, c:c + 2, T_PROMPT + 16 * u:T_PROMPT + 16 * u + 16].rearrange("p c (b t) -> p c b t", t=STEPS)
                    src = split(bank(key), P)[:, 2 * m:2 * m + 2].rearrange("p c (b r) -> p c b r", r=32)[:, :, :, 4 * h:4 * h + 4]
                    for i in range(2):
                        ins = v.tensor_copy(dst[:, i], src[:, i])
                        if (m, i) != (1, 1):
                            V(ins, wait=False)
                release(dve, ins, key, wait=True)
        for t in range(3):
            residual("mw", t)
            norm(1, t, lnp)
        dve.sem_inc(s_end["mem"][0], 1)
        for s in s_end["mem"]:
            dve.wait_ge(s, 1)
        dve.wait_ge(s_mkout, 32)
        V(v.memset(sc[:, 16:24], 0.0))
        copy_skeyT(dve)
        copy_xT(dve, "x2T")
        copy_pq(dve, 0, 4)
        copy_ps(dve, 0, [0])
        evacuated(dve, ("ps", 0, 0))

        def best16(step, items):
            for op in range(5):
                for i, (vals, inds, x) in enumerate(items):
                    h = slice(0, 8) if op < 3 else slice(8, 16)
                    if op in (0, 3):
                        ins = v.max(vals[:, h], x)
                    elif op in (1, 4):
                        ins = v.max_index(inds[:, h], vals[:, h], x)
                    else:
                        ins = v.match_replace(x, vals[:, 0:8], x, NEG)
                    step(ins, wait=(i == len(items) - 1))

        def experts(step, M, scores):
            R, tv, ti, tif, cand, cv, cj = (M[k] for k in ("R", "tv", "ti", "tif", "cand", "cv", "cj"))
            best16(step, [(tv[:, r, c], ti[:, r, c], scores(r, c)) for r in range(R) for c in range(2)])
            step(v.tensor_copy(tif[:, :, :, :], ti[:, :, :, :]), wait=False)
            for r in range(R):
                step(v.tensor_tensor(split(cand[:, r], 16), bc(tv[:, r, 0], 2, 16), bc(tv[:, r, 1], 1, 16), ALU.add), wait=(r == R - 1))
            best16(step, [(cv[:, r], cj[:, r], cand[:, r]) for r in range(R)])
            step(v.tensor_tensor(M["texp"][:, :, :], cv[:, :, :], cv[:, :, 0:1].to_broadcast([P, R, 16]), ALU.subtract), wait=False)
            flat, ja, jaf, eqm, ef = cj[:, :, :].rearrange("p h k -> p (h k)"), M["ja"], M["jaf"], M["eqm"], M["ef"]
            step(v.tensor_scalar(ja[:, 0], flat, 4, None, ALU.logical_shift_right), wait=False)
            step(v.tensor_scalar(ja[:, 1], flat, 15, None, ALU.bitwise_and))
            dve.sem_inc(s_tmx, 1)
            step(v.tensor_copy(jaf[:, :, :], ja[:, :, :]))
            for c in range(2):
                step(v.tensor_tensor(eqm[:, :, :], bc(jaf[:, c], 2, 16), bc(C("iota16"), 1, 16 * R), ALU.is_equal))
                for r in range(R):
                    rows = slice(16 * r, 16 * r + 16)
                    step(v.tensor_tensor(eqm[:, rows], eqm[:, rows], bc(tif[:, r, c], 1, 16), ALU.mult), wait=(r == R - 1))
                step(v.tensor_reduce(ef[:, c], eqm[:, :, :], AX, ALU.add))

        def gates(step, M, out):
            R, texp, tsum = M["R"], M["texp"], M["tsum"]
            step(v.tensor_reduce(tsum[:, 0], texp[:, :, :], AX, ALU.add))
            step(v.reciprocal(tsum[:, 1], tsum[:, 0]))
            step(v.tensor_tensor(out, texp[:, :, :], bc(tsum[:, 1], 2, 16), ALU.mult))

        V(v.tensor_copy(xs[:, :, :, :], sc[:, 0:2]))
        experts(V, R2, lambda r, c: xs[:, r, c])
        V(v.scalar_tensor_tensor(out=E_all[:, 0:2, :].rearrange("p a k -> p (a k)"), in0=R2["ef"][:, 0], scalar=128.0,
                                 in1=R2["ef"][:, 1], op0=ALU.mult, op1=ALU.add))
        dve.wait_ge(s_texp, 1)
        gates(V, R2, W_all[:, 0:2, :])
        dve.sem_inc(s_route, 1)
        dve.sem_inc(u_free, 8)
        copy_pq(dve, 4, 16)

        route_count = dve.alloc_register("route_count")
        dve.reg_mov(route_count, 1)

        def loop_step(ins, wait=True):
            if wait:
                ins.then_inc(route_step, 1)
                dve.wait_ge(route_step, route_count)
                dve.reg_add(route_count, route_count, 1)

        def route(g, skip=0):
            step = loop_step
            step(v.tensor_copy(xs[:, :, :, :], sc[:, bass.ds(g * 2 + 2, 2)]))
            experts(step, R2, lambda r, c: xs[:, r, c])
            step(v.scalar_tensor_tensor(out=e_two[:, :, :].rearrange("p r k -> p (r k)"), in0=R2["ef"][:, 0], scalar=128.0,
                                        in1=R2["ef"][:, 1], op0=ALU.mult, op1=ALU.add))
            dve.wait_ge(s_texp, g + 2)
            gates(step, R2, w_two[:, :, :])
            step(v.tensor_copy(E_all[:, bass.ds(g * 2 + (2 + skip), 2), :], e_two[:, :, :]), wait=False)
            step(v.tensor_copy(W_all[:, bass.ds(g * 2 + (2 + skip), 2), :], w_two[:, :, :]))
            dve.sem_inc(s_route, 1)

        def dots(g, half):
            if half == 0:
                v.tensor_copy(x_cur, xt[:, bass.ds(g // 8, 1), :].rearrange("p a d -> p (a d)")).then_inc(x_ready, 1)
                dve.wait_ge(x_ready, g + 1)
            for k in range(8 * half, 8 * half + 8):
                dve.wait_ge(s_u[k % 8], 32 * g + 16 * (half + 1))
                v.tensor_tensor_reduce(out=uslot[k], in0=uslot[k], in1=x_cur, scale=1.0, scalar=0.0,
                                       op0=ALU.mult, op1=ALU.add, accum_out=h_cur[:, k:k + 1]).then_inc(u_free, 1)

        def turn(g, between=None, last=False):
            dots(g, 1)
            dve.wait_ge(u_free, GRP * g + GRP + 8)
            dve.sem_inc(h_done, 1)
            dve.wait_ge(gelu_done, g + 1)
            v.tensor_tensor(w_cur[:, :], g_cur[:, :], W_all[:, bass.ds(g, 1), :].rearrange("p a k -> p (a k)"), ALU.mult).then_inc(w_done, 1)
            if between is not None:
                between(g)
            if not last:
                dots(g + 1, 0)
            dve.wait_ge(v_free, GRP * g + 2 * GRP)
            ysl = Y[:, bass.ds(g // 8, 1), :].rearrange("p a (c n) -> p (a c) n", n=512)
            v.tensor_tensor(ysl, psum[:, 0:2, :], ysl, ALU.add).then_inc(y_free, 1)

        dots(0, 0)
        for t in range(3):
            copy_ps(dve, t, range(1 if t == 0 else 0, 4))
        for t in range(3):
            for q in range(4):
                evacuated(dve, ("ps", t, q))
        dve.sem_inc(v_free, GRP)
        V(v.memset(Y[:, :, :], 0.0))
        dve.sem_inc(y_free, 1)
        with dve.Fori(0, 7) as g:
            turn(g, route)
        with dve.Fori(7, 11) as g:
            turn(g, lambda g: route(g, 2))
        with dve.Fori(11, 15) as g:
            turn(g)
        dve.wait_ge(s_fold, 16 * 11)
        turn(15)
        dve.wait_ge(y_free, 17)
        for t in range(2):
            x = xt[:, t, :]
            V(v.scalar_tensor_tensor(out=x, in0=x, scalar=ALPHA, in1=Y[:, t, :], op0=ALU.mult, op1=ALU.add))
            norm(2, t, lnp3)
        turn(16)
        turn(17, last=True)
        dve.wait_ge(y_free, NGRP + 1)
        dve.sem_inc(s_y, 1)
        for c in range(2):
            x = xt[0:32, 2, GW * c:GW * c + GW]
            filled(dve, ("yfold", c))
            release(dve, v.scalar_tensor_tensor(out=x, in0=x, scalar=ALPHA, in1=bank(("yfold", c))[0:32], op0=ALU.mult, op1=ALU.add), ("yfold", c), wait=True)
        norm(2, 2, lnp3)

    @block.tensor
    def _(pe):
        def begin(key):
            if JOB[key] >= 8:
                pe.wait_ge(bank_free[JOB[key] % 8], JOB[key] // 8)
            return bank(key)

        def done(ins, key):
            ins.then_inc(bank_full[JOB[key] % 8], 1)

        mm, tr = nc.tensor.matmul, nc.tensor.transpose

        def landed(n):
            pe.wait_ge(s_w[n % 2], w_value(n))
            return wbuf[:, n % 2]

        def turn_tokens(name, src, ntile=3, norms=None):
            for t in range(ntile):
                n = toks(t)[1]
                if norms is not None:
                    pe.wait_ge(s_ln, 3 * norms + t + 1)
                for c in range(2):
                    o = begin((name, t, c))
                    for i in range(4):
                        k = 4 * c + i
                        ins = tr(o[:, P * i:P * i + n], src[0:n, t, P * k:P * k + P], ident[0:n, 0:n])
                    done(ins, (name, t, c))

        def by_token(name, group, xs, c, ntile=3, w=GW):
            wt = landed(group)
            for t in range(ntile):
                t0, n = toks(t)
                o = begin((name, c, t))
                for k in range(KC):
                    ins = mm(o[0:n, 0:w], xs[:, k, t0:t0 + n], wt[:, k, 0:w], start=(k == 0), stop=(k == KC - 1))
                done(ins, (name, c, t))

        def by_tile(name, w):
            wt = [landed(WG[w, c]) for c in range(2)]
            for t in range(3):
                t0, n = toks(t)
                for c in range(2):
                    o = begin((name, c, t))
                    for k in range(KC):
                        ins = mm(o[0:n, :], mixT[:, k, t0:t0 + n], wt[c][:, k, :], start=(k == 0), stop=(k == KC - 1))
                    done(ins, (name, c, t))

        def by_feature(name, group, c, cols):
            wt = landed(group)
            o = begin((name, c))
            for k in range(KC):
                ins = mm(o[:, 0:TOK], wt[:, k, cols:cols + P], xT[:, k, :], start=(k == 0), stop=(k == KC - 1))
            done(ins, (name, c))

        def all_evacuated(keys):
            for key in keys:
                evacuated(pe, key)

        pe.wait_ge(s_const, 16)
        pe.wait_ge(s_x, 32)
        turn_tokens("xT", xt)
        all_evacuated([("xT", t, c) for t in range(3) for c in range(2)])
        for g, (o_, w_) in enumerate(WG_IN):
            by_token("z", WG["w_in", g], xT, g, 3, w_)

        for kv in range(2):
            for i in range(4):
                pe.wait_ge(s_sorted, 4 * kv + i + 1)
                src = subg[:, :].rearrange("p (g r n) -> p r g n", g=2, r=8)
                for q in range(4):
                    o = begin(("subT", kv, i, q))
                    for m in range(4):
                        r, g = (4 * q + m) // 2, m % 2
                        ins = tr(o[:, P * m:P * m + P], src[:, r, g], ident)
                    done(ins, ("subT", kv, i, q))
            pe.wait_ge(s_subp, 32 * (kv + 1))
            src = subp[:, :].rearrange("p (g r n) -> p r g n", g=2, r=8)
            o = begin(("subT", kv, 4, 0))
            for m in range(16):
                ins = tr(o[:, 16 * m:16 * m + 16], src[:, m // 2, m % 2], ident[0:16, 0:16])
            done(ins, ("subT", kv, 4, 0))
            all_evacuated([("subT", kv, i, q) for i in range(4) for q in range(4)] + [("subT", kv, 4, 0)])
            pe.wait_ge(s_cw, 16 * (3 + kv))
            for g in range(2):
                o = begin(("hid", kv, g))
                for n in range(16):
                    part = subT[:, 2 * (n % 8) + g, 0:512].rearrange("p (b s) -> p b s", s=64)[:, :, n // 8:n // 8 + NCB]
                    ins = mm(o[:, 0:504].rearrange("p (b s) -> p b s", s=NCB), w1[:, n, :], part, start=(n == 0), stop=(n == 15))
                done(ins, ("hid", kv, g))
            o = begin(("hidp", kv))
            for g in range(2):
                for n in range(16):
                    ins = mm(o[:, 15 * g:15 * g + 15], w1[:, n, :], subT[:, 2 * (n % 8) + g, 512 + n // 8:512 + n // 8 + NCP],
                             start=(n == 0), stop=(n == 15))
            done(ins, ("hidp", kv))
            all_evacuated([("hid", kv, 0), ("hid", kv, 1), ("hidp", kv)])
            if kv == 0:
                for key, o_, w_ in ((("kcT",), 0, 504), (("kcTp",), 504, NCP)):
                    o = begin(key)
                    for g in range(2):
                        ins = mm(o[64 * g:64 * g + 64, 0:w_], w2[:, 0, :], hid[:, g, o_:o_ + w_], start=True, stop=True)
                    done(ins, key)
            else:
                for c in range(2):
                    o = begin(("vc", c))
                    for b in range(4):
                        for g in range(2):
                            at = NCB * (4 * c + b)
                            ins = mm(o[0:NCB, P * b + 64 * g:P * b + 64 * g + 64], hid[:, g, at:at + NCB], w2[:, 1, :], start=True, stop=True)
                    done(ins, ("vc", c))
                o = begin(("vcp",))
                for g in range(2):
                    ins = mm(o[0:NCP, 64 * g:64 * g + 64], hid[:, g, 504:519], w2[:, 1, :], start=True, stop=True)
                done(ins, ("vcp",))

        for t in range(3):
            n = toks(t)[1]
            for key, c in ((("hqT", t), HQ), (("hfT", t), HF)):
                o = begin(key)
                for h in range(H):
                    ins = tr(o[:, P * h:P * h + n], z[0:n, t, c + P * h:c + P * h + P], ident[0:n, 0:n])
                done(ins, key)
        pe.wait_ge(s_ke, 1)
        for t in range(3):
            t0, n = toks(t)
            o = begin(("att", t))
            for h in range(H):
                ins = mm(o[0:n, P * h:P * h + n], e3[:, h, t0:t0 + n], e2[:, h, t0:t0 + n], start=True, stop=True)
            done(ins, ("att", t))
        pe.wait_ge(s_ke, 2)
        for t in range(3):
            t0, n = toks(t)
            o = begin(("kE", t))
            for h in range(H):
                ins = tr(o[0:n, P * h:P * h + P], kT[:, h, t0:t0 + n], ident)
            done(ins, ("kE", t))
        for t in range(3):
            n = toks(t)[1]
            evacuated(pe, ("att", t))
            o = begin(("oin", t))
            for h in range(H):
                ins = mm(o[0:n, P * h:P * h + P], attS[0:n, t, h, 0:n], z[0:n, t, HI + P * h:HI + P * h + P], start=True, stop=True)
            done(ins, ("oin", t))
        all_evacuated([("kE", t) for t in range(3)])
        for c in range(NCH):
            t, r = c // 4, slice(32 * (c % 4), 32 * (c % 4) + 32)
            o = begin(("U", c))
            for h in range(H):
                ins = mm(o[:, P * h:P * h + P], ktok[r, t, h, :], z[r, t, HI + P * h:HI + P * h + P], start=True, stop=True,
                         tile_position=(r.start, 0))
            done(ins, ("U", c))
        pe.wait_ge(s_ke, 3)
        pe.wait_ge(s_stin, 16)
        for t in range(3):
            if t < 2:
                evacuated(pe, ("U", 4 * t + 2))
            o = begin(("ost", t))
            for h in range(H):
                if t < 2:
                    for j in range(4):
                        c = 4 * t + j
                        ins = mm(o[32 * j:32 * j + 32, P * h:P * h + P], qT[:, h, CH * c:CH * c + CH], state[:, c, h, :], start=True, stop=True)
                else:
                    for b in range(N_SAMPLE):
                        ins = mm(o[0:32, P * h:P * h + P], qGm[:, h, b, :], sstate[:, b, h, :], start=(b == 0), stop=(b == N_SAMPLE - 1))
            done(ins, ("ost", t))
        pe.wait_ge(s_vm, N_SAMPLE)
        for b in range(N_SAMPLE):
            o = begin(("US", b))
            for h in range(H):
                ins = mm(o[:, P * h:P * h + P], ktok[0:32, 2, h, :], vm[0:32, b, P * h:P * h + P], start=True, stop=True)
            done(ins, ("US", b))

        pe.wait_ge(s_gates, 2)
        for u in range(2):
            o = begin(("gs", u))
            done(mm(o[:, 0:24], C("rowsel", P)[0:32, u, :], z[0:32, 2, NG:NG + 24], start=True, stop=True), ("gs", u))
        for t in range(3):
            n = toks(t)[1]
            o = begin(("nqT", t))
            q = split(z[0:n, t, NQ:NQ + 512], P)
            for j in range(4):
                ins = tr(o[:, P * j:P * j + n], q[:, j], ident[0:n, 0:n])
            done(ins, ("nqT", t))
        for t in range(3):
            n = toks(t)[1]
            o = begin(("nkT", t))
            for i, c in enumerate((KSC, KWC)):
                ins = tr(o[:, P * i:P * i + n], z[0:n, t, c:c + P], ident[0:n, 0:n])
            done(ins, ("nkT", t))
        all_evacuated([("nqT", t) for t in range(3)] + [("nkT", t) for t in range(3)])
        for t in range(2):
            K, t0, per = P * (t + 1), P * t, 4 // (t + 1)
            for g in range(2):
                o, r = begin(("sc", t, g)), slice(64 * g, 64 * g + 64)
                for j in range(4):
                    ins = mm(o[:, NCP * j:NCP * j + NCP], qn[r, j, t0:t0 + P], kcT[r, 504:519], start=True, stop=True)
                done(ins, ("sc", t, g))
            for br in range(2):
                for k in range(2 * (t + 1)):
                    o = begin(("s", t, br, k))
                    for i in range(per):
                        h = per * k + i
                        r = slice(64 * (h // 4), 64 * (h // 4) + 64)
                        ins = mm(o[:, K * i:K * i + K], qn[r, h % 4, t0:t0 + P], kn[r, br, 0:K], start=True, stop=True)
                    done(ins, ("s", t, br, k))
            if t == 0:
                pe.wait_ge(s_otok, 3)
                for k in range(3):
                    n = toks(k)[1]
                    o = begin(("oT", k))
                    for h in range(H):
                        ins = tr(o[:, P * h:P * h + n], otok[0:n, k, h, :], ident[0:n, 0:n])
                    done(ins, ("oT", k))
            pe.wait_ge(s_pn, t + 1)
            blocks = [(br, h, i) for br in range(2) for h in range(8) for i in range(t + 1)]
            for k in range(4 * (t + 1)):
                o = begin(("pT", t, k))
                for m in range(4):
                    br, h, i = blocks[4 * k + m]
                    ins = tr(o[:, P * m:P * m + P], PS[:, br, h, P * i:P * i + P], ident)
                done(ins, ("pT", t, k))
            for k in range(2):
                o = begin(("pcT", t, k))
                for m in range(4):
                    ins = tr(o[0:NCP, P * m:P * m + P], PCp[:, 4 * k + m, :], ident)
                done(ins, ("pcT", t, k))
            all_evacuated([("pT", t, k) for k in range(4 * (t + 1))] + [("pcT", t, k) for k in range(2)])
            o = begin(("pv", t))
            for h in range(8):
                g, j = h // 4, h % 4
                terms = [(z[:, i, (VSC, VWC)[br] + 64 * g:(VSC, VWC)[br] + 64 * g + 64], PTp[:, blocks.index((br, h, i)), :])
                         for br in range(2) for i in range(t + 1)]
                terms.append((vcP[0:NCP, 64 * g:64 * g + 64], PCT[0:NCP, h, :]))
                for n, (lhsT, rhs) in enumerate(terms):
                    ins = mm(o[64 * g:64 * g + 64, P * j:P * j + P], lhsT, rhs, start=(n == 0), stop=(n == len(terms) - 1))
            done(ins, ("pv", t))
        pe.wait_ge(s_qpad, 2)
        for u in range(2):
            o = begin(("sc4", u))
            for b in range(4):
                s = 4 * u + b
                ins = mm(o[32 * b:32 * b + 32, 0:NCB], qpad[:, s, :], kcT[:, NCB * s:NCB * s + NCB], start=True, stop=True)
            done(ins, ("sc4", u))
            for b in range(4):
                s = 4 * u + b
                pe.wait_ge(s_slk[s % 2], 32 * (s // 2 + 1))
                for k in range(3):
                    src = slk[:, s % 2, 512 * k:512 * k + 512] if k < 2 else wk[:, s % 2, :]
                    o = begin(("skT", u, b, k))
                    for i in range(4):
                        ins = tr(o[:, P * i:P * i + P], src[:, P * i:P * i + P], ident)
                    done(ins, ("skT", u, b, k))
            pe.wait_ge(s_cpn, u + 1)
            o = begin(("spcT", u))
            for i in range(2):
                ins = tr(o[0:NCB, P * i:P * i + P], LC[:, i, :], ident)
            done(ins, ("spcT", u))
            evacuated(pe, ("spcT", u))
            o = begin(("imp", u))
            done(mm(o[:, 0:17], pcs[0:NCB, 0, :], C("cover")[0:NCB], start=True, stop=True), ("imp", u))
            evacuated(pe, ("imp", u))
            o = begin(("impj", u))
            done(mm(o[:, 0:17], C("jsum"), small[:, 108:125], start=True, stop=True), ("impj", u))
            all_evacuated([("skT", u, b, k) for b in range(4) for k in range(3)])
            for key, c0 in ((("ss", u, 0), 0), (("ss", u, 1), 512), (("sw", u), 1024)):
                o = begin(key)
                for b in range(4):
                    ins = mm(o[32 * b:32 * b + 32, :], qpad[:, 4 * u + b, :], KT[:, b, c0:c0 + 512], start=True, stop=True)
                done(ins, key)
            o = begin(("sn", u))
            for b in range(4):
                for br in range(2):
                    ins = mm(o[32 * b:32 * b + 32, 32 * br:32 * br + 32], qpad[:, 4 * u + b, :], kn[:, br, T_PROMPT:TOK], start=True, stop=True)
            done(ins, ("sn", u))
            pe.wait_ge(s_spn, u + 1)
            for k in range(3):
                o = begin(("spT", u, k))
                c0 = 512 * k if k < 2 else 1056
                for i in range(4):
                    ins = tr(o[:, P * i:P * i + P], L[:, c0 + P * i:c0 + P * i + P], ident)
                done(ins, ("spT", u, k))
            o = begin(("spT", u, 3))
            for i, c0 in enumerate((1024, 1568)):
                ins = tr(o[0:32, P * i:P * i + P], L[:, c0:c0 + 32], ident)
            done(ins, ("spT", u, 3))
            all_evacuated([("spT", u, k) for k in range(4)])
            o = begin(("spv", u))
            for b in range(4):
                r = slice(32 * b, 32 * b + 32)
                pe.wait_ge(s_slv[b], 32 * (u + 1))
                terms = [(PTs[:, i, r], slv[:, b, P * i:P * i + P]) for i in range(8)]
                terms += [(PTs[:, 8 + i, r], wv[:, b, P * i:P * i + P]) for i in range(4)]
                terms += [(PTs[0:32, 12, r], z[0:32, 2, VSC:VSC + P]), (PTs[0:32, 13, r], z[0:32, 2, VWC:VWC + P]),
                          (pcs[0:NCB, 1, r], vcS[0:NCB, 4 * u + b, :])]
                for n, (lhsT, rhs) in enumerate(terms):
                    ins = mm(o[r, 0:P], lhsT, rhs, start=(n == 0), stop=(n == len(terms) - 1))
            done(ins, ("spv", u))
            evacuated(pe, ("spv", u))
            o = begin(("spvT", u))
            done(tr(o[:, 0:P], ov[:, :], ident), ("spvT", u))
        all_evacuated([("pv", 0), ("pv", 1), ("spvT", 0), ("spvT", 1), ("oT", 0), ("oT", 1), ("oT", 2)])
        by_tile("wo", "w_out")

        pe.wait_ge(s_mem, 16)
        turn_tokens("memT", memp, 2)
        all_evacuated([("memT", t, c) for t in range(2) for c in range(2)])
        for name, w in (("mk", "w_mem_k"), ("mv", "w_mem_v")):
            for c in range(2):
                by_token(name, WG[w, c], memT, c, 2)
        turn_tokens("x1T", xt, norms=0)
        all_evacuated([("x1T", t, c) for t in range(3) for c in range(2)])
        for c in range(KC):
            by_feature("mq", WG["w_mem_q", c // 4], c, P * (c % 4))
        all_evacuated([("mk", c, t) for c in range(2) for t in range(2)] + [("mv", c, t) for c in range(2) for t in range(2)])

        def turn_keys(seq, src):
            for q in range(4):
                o = begin(("mkT", seq, q))
                for m in range(4):
                    c, i = 2 * q + m // 2, m % 2
                    ins = tr(o[:, P * m:P * m + P], src[:, i, P * c:P * c + P], ident)
                done(ins, ("mkT", seq, q))

        turn_keys(0, mkt)
        all_evacuated([("mkT", 0, q) for q in range(4)] + [("mq", c) for c in range(KC)])
        for t in range(2):
            for k in range(2):
                o = begin(("ms", t, k))
                for m in range(2):
                    for i in range(2):
                        c = 2 * (2 * k + m) + i
                        ins = mm(o[:, 256 * m:256 * m + 256], mqT[:, c, P * t:P * t + P], KTm[:, 0, c, :], start=(i == 0), stop=(i == 1))
                done(ins, ("ms", t, k))
            pe.wait_ge(s_mpn, t + 1)
            for k in range(2):
                o = begin(("mpT", t, k))
                for m in range(4):
                    h, i = 2 * k + m // 2, m % 2
                    ins = tr(o[:, P * m:P * m + P], Pm[:, h, P * i:P * i + P], ident)
                done(ins, ("mpT", t, k))
            all_evacuated([("mpT", t, 0), ("mpT", t, 1)])
            for k in range(2):
                o = begin(("mo", t, k))
                for m in range(4):
                    c = 4 * k + m
                    for i in range(2):
                        ins = mm(o[:, P * m:P * m + P], mvt[:, i, P * c:P * c + P], PTm[:, 2 * (c // 2) + i, :], start=(i == 0), stop=(i == 1))
                done(ins, ("mo", t, k))
        pe.wait_ge(s_mpad, KC)
        for u in range(2):
            for b in range(4):
                s = 4 * u + b
                pe.wait_ge(s_mck[s % 2], 16 * (s // 2 + 1))
                turn_keys(1 + s, mck[:, s % 2])
                all_evacuated([("mkT", 1 + s, q) for q in range(4)])
                o = begin(("sms", u, b))
                for c in range(KC):
                    ins = mm(o[32 * b:32 * b + 32, 0:256], qpm[:, s, c, :], KTm[:, (1 + s) % 2, c, :], start=(c == 0), stop=(c == KC - 1))
                done(ins, ("sms", u, b))
            pe.wait_ge(s_mpn, 3 + u)
            o = begin(("smpT", u))
            for i in range(2):
                ins = tr(o[:, P * i:P * i + P], Pm[:, 0, P * i:P * i + P], ident)
            done(ins, ("smpT", u))
            evacuated(pe, ("smpT", u))
            for k in range(2):
                o = begin(("smo", u, k))
                for b in range(4):
                    if k == 0:
                        pe.wait_ge(s_mcv[b], 16 * (u + 1))
                    r = slice(32 * b, 32 * b + 32)
                    for i in range(2):
                        ins = mm(o[r, :], PTm[:, i, r], mcv[:, b, i, GW * k:GW * k + GW], start=(i == 0), stop=(i == 1))
                done(ins, ("smo", u, k))
            for k in range(2):
                evacuated(pe, ("smo", u, k))
                o = begin(("smoT", u, k))
                for m in range(4):
                    ins = tr(o[:, P * m:P * m + P], so[:, GW * k + P * m:GW * k + P * m + P], ident)
                done(ins, ("smoT", u, k))
        all_evacuated([("mo", t, k) for t in range(2) for k in range(2)] + [("smoT", u, k) for u in range(2) for k in range(2)])
        by_tile("mw", "w_mem_o")

        pe.wait_ge(s_skey, 16)
        for q in range(4):
            o = begin(("skeyT", q))
            for m in range(4):
                ins = tr(o[:, P * m:P * m + P], skey[:, 4 * q + m, :], ident)
            done(ins, ("skeyT", q))
        turn_tokens("x2T", xt, norms=1)
        all_evacuated([("x2T", t, c) for t in range(3) for c in range(2)])
        for c in range(4):
            by_feature("pq", WG["peer_w_q", c // 4], c, P * (c % 4))
        all_evacuated([("pq", c) for c in range(4)] + [("skeyT", q) for q in range(4)])

        def key_scores(t, q):
            t0, n = toks(t)
            o = begin(("ps", t, q))
            for m in range(4):
                hc = 4 * q + m
                ins = mm(o[0:n, P * m:P * m + P], pqT[:, hc, t0:t0 + n], skT[:, hc, :], start=True, stop=True)
            done(ins, ("ps", t, q))

        key_scores(0, 0)
        for c in range(4, 16):
            by_feature("pq", WG["peer_w_q", c // 4], c, P * (c % 4))
        all_evacuated([("pq", c) for c in range(4, 16)])
        for t in range(3):
            for q in range(1 if t == 0 else 0, 4):
                key_scores(t, q)
        all_evacuated([("ps", t, q) for t in range(3) for q in range(4)])
        with pe.Fori(0, NGRP) as g:
            pe.wait_ge(y_free, g + 1)
            for k in range(GRP):
                pe.wait_ge(diag_done, GRP * g + k + 1)
                pe.wait_ge(s_v[k], 16 * g + 16)
                for c in range(2):
                    ins = mm(psum[:, c, :], diag[:, k, :], vslot[k][:, GW * c:GW * c + GW], start=(k == 0), stop=(k == GRP - 1))
                ins.then_inc(v_free, 1)
        pe.wait_ge(s_y, 1)
        for c in range(2):
            o = begin(("yfold", c))
            done(mm(o[0:32, :], C("fold"), Y[:, 2, GW * c:GW * c + GW], start=True, stop=True), ("yfold", c))

    ctx.close()


_INS = ["x_prompt", "x_sample", "cache_k_cmp", "cache_v_cmp", "cache_k_slc", "cache_v_slc", "cache_k_win", "cache_v_win",
        "state_hgrn", "cache_mem_k", "cache_mem_v", "page_table", "mem_prompt", "w_in", "hgrn_lb_logits", "hgrn_norm_g",
        "cmp_k_w1", "cmp_k_b1", "cmp_k_w2", "cmp_k_b2", "cmp_v_w1", "cmp_v_b1", "cmp_v_w2", "cmp_v_b2", "w_out", "ln1_g",
        "ln1_b", "w_mem_q", "w_mem_k", "w_mem_v", "w_mem_o", "ln2_g", "ln2_b", "peer_w_q", "peer_sub_keys", "peer_u",
        "peer_v", "ln3_g", "ln3_b"]
_KV = (1, 1, 256, 2, 64)
_KVS = (1, 8, 4, 2, 64)
_OUTS = [(1, 256, 1024), (8, 4, 1024)] + [_KV] * 6 + [(1, 1, 4, 128, 128)] + [(1, 1, 256, 4, 256)] * 2 + [_KVS] * 6 + [(1, 8, 4, 128, 128)]


def kernel(**inputs):
    import numpy as _np
    import concourse.bacc as _bacc
    from concourse import mybir as _mybir
    from concourse.bass_utils import run_bass_kernel_spmd as _run

    nc = _bacc.Bacc("TRN2", target_bir_lowering=False, num_devices=1)
    arrays, args = {}, {}
    for name in _INS:
        a = _np.ascontiguousarray(inputs[name])
        arrays[f"in_{name}"] = a
        args[name] = nc.dram_tensor(f"in_{name}", a.shape, _mybir.dt.from_np(a.dtype), kind="ExternalInput").ap()
    arrays["consts"] = const_table()[0]
    args["consts"] = nc.dram_tensor("consts", arrays["consts"].shape, _mybir.dt.float32, kind="ExternalInput").ap()
    outs = [nc.dram_tensor(f"out_{i}", s, _mybir.dt.float32, kind="ExternalOutput").ap() for i, s in enumerate(_OUTS)]
    layer_kernel(nc, args, outs)
    r = _run(nc, [arrays], core_ids=[0])
    return tuple(r.results[0][f"out_{i}"] for i in range(len(_OUTS)))
```

```python
from contextlib import ExitStack

import numpy as np
import concourse.bass as bass
from concourse import mybir

ALU = mybir.AluOpType
ACT = mybir.ActivationFunctionType
F32 = mybir.dt.float32
I32 = mybir.dt.int32
U32 = mybir.dt.uint32
AX = mybir.AxisListType.X

P = 128
D = 1024
KC = D // P
T_PROMPT, N_SAMPLE, STEPS = 256, 8, 4
TOK = T_PROMPT + N_SAMPLE * STEPS
TILES = [(0, P), (P, P), (2 * P, TOK - 2 * P)]
HQ, HF, NQ = 0, 512, 2048
HI, HG, KCC, VCC, KSC, VSC, KWC, VWC, NG, ZC = (0, 512, 1024, 1152, 1280, 1408, 1536, 1664, 1792, 1816)
H = 4
CH = 32
NCH = T_PROMPT // CH
ALPHA = 2.0 ** 0.25
EPS = 1e-5
NEG = -1e30
BIG = -1e33
SLOPES = [2.0 ** -(h + 1) for h in range(8)]
PAST, PAGE = 1024, 128
WIN = 512
NCB = 63
NCP = 15
GW = 512
Z_GROUPS = [(1024, 0, GW), (1536, GW, GW), (2560, 2 * GW, GW), (3072, 3 * GW, ZC - 3 * GW)]
NSUBS = 2
GRP = 16
NGRP = 18


def const_table():
    parts = {}
    p = np.arange(P)
    parts["ident"] = np.eye(P)
    s = np.arange(256)
    d = s[None, :] - 128 - p[:, None]
    parts["dist"] = np.where(d <= 0, d, BIG)
    c = np.arange(NCP)
    bias = np.zeros((P, 2, 8, NCP)); mask = np.zeros((P, 2, 8, NCP))
    for t in range(2):
        dd = 16 * c[None, :] + 31 - (p[:, None] + 128 * t)
        for h in range(8):
            bias[:, t, h] = np.where(dd <= 0, dd * SLOPES[h], NEG)
            mask[:, t, h] = dd <= 0
    parts["cbias"] = bias; parts["cmask"] = mask
    b4, g, j, t = p // 32, p // 16 % 2, p // 4 % 4, p % 4
    slope = np.array(SLOPES)[g * 4 + j][:, None]
    qpos = (PAST + t)[:, None]
    pos = 8 * s[None, :128] + np.arange(8)[:, None]
    parts["bsel"] = slope * (pos.reshape(1, -1) - qpos)
    posw = (PAST - WIN + 4 * s[None, :128] + np.arange(4)[:, None]).reshape(1, -1)
    dw = qpos - posw
    parts["bwin"] = np.where(dw < WIN, -slope * dw, NEG)
    fr = np.zeros((P, 2, 32))
    kb, kt = np.arange(32) // 4, np.arange(32) % 4
    for u in range(2):
        ok = (kb[None] == (4 * u + b4)[:, None]) & (kt[None] <= t[:, None])
        fr[:, u] = np.where(ok, slope * (kt[None] - t[:, None]), NEG)
    parts["bnew"] = fr
    parts["bcmp"] = slope * (16 * np.arange(NCB)[None] + 31 - qpos)
    parts["pblk"] = np.broadcast_to((s[:128] // 8)[None], (P, P))
    parts["blk"] = np.broadcast_to(np.arange(17)[None], (P, 17))
    cs, ss = np.arange(NCB)[:, None] * 16, np.arange(17)[None] * 64
    m = np.zeros((P, 17)); m[:NCB] = np.clip(np.minimum(cs + 32, ss + 64) - np.maximum(cs, ss), 0, None) / 16
    parts["cover"] = m
    parts["jsum"] = (b4[:, None] == b4[None]) & (g[:, None] == g[None]) & (t[:, None] == t[None])
    parts["hmask"] = (p[:, None] // CH == p[None] // CH) & (p[:, None] <= p[None])
    q = np.arange(32)
    hs = np.zeros((P, 32)); hs[:32] = (q[:, None] // 4 == q[None] // 4) & (q[:, None] <= q[None])
    parts["hmask_s"] = hs
    r = np.ones(TOK); r[0:T_PROMPT:CH] = 0; r[T_PROMPT::STEPS] = 0
    parts["keep"] = np.broadcast_to(r[None], (P, TOK))
    parts["bmask"] = np.broadcast_to((q[None] // 4 == np.arange(8)[:, None])[None], (P, 8, 32))
    bt = np.zeros((P, 8)); bt[:32] = q[:, None] // 4 == np.arange(8)[None]
    parts["brow"] = bt
    parts["fold"] = p[:, None] % 32 == q[None]
    toks = 4 * (4 * np.arange(2)[:, None] + b4[None]) + t[None]
    rs = np.zeros((P, 2, P)); rs[:32] = np.arange(32)[:, None, None] == toks[None]
    parts["rowsel"] = rs
    hc = np.arange(24) // 3
    parts["headsel"] = hc[None] == (g * 4 + j)[:, None]
    parts["iota16"] = np.broadcast_to(np.arange(16)[None], (P, 16))
    parts["mod8"] = (p % 8)[:, None]
    parts["mod16"] = (p % 16)[:, None]
    at, n = {}, 0
    cols = []
    for k, v in parts.items():
        v = np.asarray(v, np.float32).reshape(P, -1)
        at[k] = (n, v.shape[1]); n += v.shape[1]
        cols.append(v)
    return np.ascontiguousarray(np.concatenate(cols, 1)), at


CONST_AT = const_table()[1]
NCONST = sum(n for _, n in CONST_AT.values())


def pe_jobs():
    jobs = [("xT", t, c) for t in range(3) for c in range(2)]
    jobs += [("zf", c) for c in range(8)]
    for g in range(4):
        jobs += [("z", g, t) for t in range(3)] + [("zq", j) for j in range(4) if g == 1]
    for kv in range(2):
        jobs += [("subT", kv, i, q) for i in range(4) for q in range(4)] + [("subT", kv, 4, 0)]
        jobs += [("hid", kv, 0), ("hid", kv, 1), ("hidp", kv)]
        jobs += [("vc", 0), ("vc", 1), ("vcp",)] if kv else [("kcT",), ("kcTp",)]
    jobs += [("nkT", t) for t in range(3)]
    jobs += [("att", t) for t in range(3)] + [("kE", t) for t in range(3)] + [("oin", t) for t in range(3)]
    jobs += [("U", c) for c in range(NCH)] + [("ost", t) for t in range(3)] + [("US", b) for b in range(N_SAMPLE)]
    for t in range(2):
        jobs += [("sc", t, g) for g in range(2)] + [("s", t, br, k) for br in range(2) for k in range(2 * (t + 1))]
        if t == 0:
            jobs += [("oT", k) for k in range(3)]
        jobs += [("pT", t, k) for k in range(4 * (t + 1))] + [("pcT", t, k) for k in range(2)] + [("pv", t)]
    jobs += [("gs", u) for u in range(2)]
    for u in range(2):
        jobs += [("sc4", u)]
        for b in range(4):
            jobs += [("skT", u, b, k) for k in range(3)]
        jobs += [("ss", u, 0), ("ss", u, 1), ("sw", u), ("sn", u)]
        jobs += [("spcT", u), ("imp", u), ("impj", u)]
        jobs += [("wo", u, c) for c in range(2)]
        jobs += [("spT", u, k) for k in range(4)] + [("spv", u), ("spvT", u)]
    jobs += [("wo", 2, c) for c in range(2)]
    jobs += [("memT", t, c) for t in range(2) for c in range(2)]
    jobs += [("mk", c, t) for c in range(2) for t in range(2)] + [("mv", c, t) for c in range(2) for t in range(2)]
    jobs += [("x1T", t, c) for t in range(3) for c in range(2)]
    jobs += [("mq", c) for c in range(KC)]
    jobs += [("mkT", 0, q) for q in range(4)]
    jobs += [("ms", t, k) for t in range(2) for k in range(2)] + [("mkT", 1, q) for q in range(4)]
    for t in range(2):
        jobs += [("mpT", t, 0), ("mpT", t, 1), ("mo", t, 0), ("mo", t, 1)]
    for u in range(2):
        for b in range(4):
            jobs += [("mkT", 1 + 4 * u + b, q) for q in range(4) if u + b > 0] + [("sms", u, b)]
        jobs += [("smpT", u), ("smo", u, 0), ("smo", u, 1), ("smoT", u, 0), ("smoT", u, 1)]
    jobs += [("mw", t, c) for t in range(2) for c in range(2)] + [("skeyT", q) for q in range(4)] + [("mw", 2, c) for c in range(2)]
    jobs += [("x2T", t, c) for t in range(3) for c in range(2)]
    jobs += [("pq", c) for c in range(4)] + [("ps", 0, 0)] + [("pq", c) for c in range(4, 8)] + [("ps", 0, 1)]
    jobs += [("pq", c) for c in range(8, 16)] + [("ps", t, q) for t in range(3) for q in range(4) if (t, q) > (0, 1)]
    jobs += [("yfold", c) for c in range(2)]
    return jobs


JOBS = pe_jobs()
JOB = {k: n for n, k in enumerate(JOBS)}

W_GROUPS = [("w_in", HF, GW, ("zf", 3)), ("w_in", HQ, GW, ("zf", 7))]
W_GROUPS += [("w_in", o, n, ("z", i, 2)) for i, (o, _, n) in enumerate(Z_GROUPS)]
W_GROUPS.insert(4, ("w_in", NQ, GW, ("zq", 3)))
W_GROUPS += [("w_out", c * GW, GW, ("wo", 2, c)) for c in range(2)]
W_GROUPS += [("w_mem_k", c * GW, GW, ("mk", c, 1)) for c in range(2)] + [("w_mem_v", c * GW, GW, ("mv", c, 1)) for c in range(2)]
W_GROUPS += [("w_mem_q", c * GW, GW, ("mq", 4 * c + 3)) for c in range(2)]
W_GROUPS += [("w_mem_o", c * GW, GW, ("mw", 2, c)) for c in range(2)]
W_GROUPS += [("peer_w_q", c * GW, GW, ("pq", 4 * c + 3)) for c in range(4)]
WG = {(name, o // GW): n for n, (name, o, _, _) in enumerate(W_GROUPS)}
W_DMAS = [3 if name == "w_out" else 8 if (name, o) == ("w_in", NQ) else 1 for name, o, *_ in W_GROUPS]


def w_value(n):
    return 16 * sum(W_DMAS[i] for i in range(n % 2, n + 1, 2))


class Lane:

    def __init__(self, eng, step):
        self.eng, self.step, self.n = eng, step, {}

    def __call__(self, ins, signal=None, wait=True):
        s = signal or self.step
        ins.then_inc(s, 1)
        self.n[id(s)] = self.n.get(id(s), 0) + 1
        if wait:
            self.eng.wait_ge(s, self.n[id(s)])


def layer_kernel(nc, A, O):
    ctx = ExitStack()

    def sem(name):
        return ctx.enter_context(nc.semaphore(name))

    def sb(stack, name, shape, dt=F32):
        return stack.enter_context(nc.sbuf_tensor(name, shape, dt))

    bank_full = [sem(f"bank_full{b}") for b in range(8)]
    bank_free = [sem(f"bank_free{b}") for b in range(8)]
    dve_step, act_step, pool_step = sem("dve_step"), sem("act_step"), sem("pool_step")
    s_const, s_x, s_par = sem("s_const"), sem("s_x"), sem("s_par")
    s_w = [sem(f"s_w{i}") for i in range(2)]
    s_pt, s_pts, s_idx = sem("s_pt"), sem("s_pts"), sem("s_idx")
    s_sub = [sem(f"s_sub{i}") for i in range(NSUBS)]
    s_sorted = [sem(f"s_sorted{g}") for g in range(2)]
    s_cw, s_subp, s_stin = sem("s_cw"), sem("s_subp"), sem("s_stin")
    s_stout, s_kvout, s_mkout, s_out = sem("s_stout"), sem("s_kvout"), sem("s_mkout"), sem("s_out")
    s_lb, s_f, s_lnf, s_g, s_hexp, s_ke, s_vm = (sem("s_" + n) for n in "lb f lnf g hexp ke vm".split())
    s_ms, s_rs, s_sgate, s_gz, s_otok, s_gates = (sem("s_" + n) for n in "ms rs sgate gz otok gates".split())
    s_mx, s_exp, s_pn, s_qpad = (sem("s_" + n) for n in "mx exp pn qpad".split())
    s_slk = [sem(f"s_slk{i}") for i in range(2)]
    s_slv = [sem(f"s_slv{i}") for i in range(4)]
    s_cmx, s_cexp, s_cpn, s_smx, s_sexp, s_spn = (sem("s_" + n) for n in "cmx cexp cpn smx sexp spn".split())
    s_end = {k: (sem(f"s_dve_end_{k}"), sem(f"s_act_end_{k}")) for k in ("cmp", "hgrn", "nsa", "mem")}
    s_lnp, s_ln, s_lnv, s_lnr = (sem("s_" + n) for n in "lnp ln lnv lnr".split())
    s_mem = sem("s_mem")
    s_mck = [sem(f"s_mck{i}") for i in range(2)]
    s_mcv = [sem(f"s_mcv{i}") for i in range(4)]
    s_mpad, s_mmx, s_mexp, s_mpn = (sem("s_" + n) for n in "mpad mmx mexp mpn".split())
    s_skey, s_tmx, s_texp, s_route, s_fold, s_y = (sem("s_" + n) for n in "skey tmx texp route fold y".split())
    route_step, x_ready = sem("route_step"), sem("x_ready")
    s_u = [sem(f"s_u{i}") for i in range(8)]
    s_v = [sem(f"s_v{i}") for i in range(GRP)]
    u_free, v_free, h_done, gelu_done, w_done, diag_done, y_free = (
        sem(n) for n in "u_free v_free h_done gelu_done w_done diag_done y_free".split())

    psum = ctx.enter_context(nc.psum_tensor("banks", [P, 8, 512], F32))
    cst = sb(ctx, "cst", [P, NCONST])
    xt = sb(ctx, "xt", [P, 3, D])
    feat = sb(ctx, "feat", [P, 2, KC, TOK])
    xT, mixT = feat[:, 0], feat[:, 1]
    wbuf = sb(ctx, "wbuf", [P, 2, KC, GW])
    par = sb(ctx, "par", [P, 320])
    small = sb(ctx, "small", [P, 192])
    ptab, sidx = sb(ctx, "ptab", [P, 8], I32), sb(ctx, "sidx", [P, 8], I32)

    def C(name, *inner):
        o, n = CONST_AT[name]
        v = cst[:, o:o + n]
        if len(inner) == 1:
            return v.rearrange("p (a b) -> p a b", b=inner[0])
        if len(inner) == 2:
            return v.rearrange("p (a b c) -> p a b c", b=inner[0], c=inner[1])
        return v

    ident = C("ident")
    lbl = par[:, 0:8].rearrange("p (a h) -> p a h", h=H)
    lb, omlb, b1, b2k = par[:, 8:12], par[:, 12:16], par[:, 16:18], par[:, 18:19]
    b2v, hng = par[:, 20:148], par[:, 148:276]
    otok = xT[:, :, :].rearrange("p a b -> p (a b)")[:, 0:1536].rearrange("p (t h e) -> p t h e", t=3, h=H)
    PTs = xT[:, :, :].rearrange("p a b -> p (a b)")[:, 0:15 * P].rearrange("p (n r) -> p n r", r=P)
    memT = mixT[:, :, :].rearrange("p a b -> p (a b)")[:, 0:KC * 256].rearrange("p (c m) -> p c m", m=256)

    zs = ExitStack()
    z = sb(zs, "z", [P, 3, ZC])
    qn = sb(zs, "qn", [P, 4, TOK])
    kn = sb(zs, "kn", [P, 2, TOK])
    kcT = sb(zs, "kcT", [P, N_SAMPLE * NCB + NCP])
    vcS = sb(zs, "vcS", [64, N_SAMPLE, P])
    vcP = sb(zs, "vcP", [16, P])

    early = ExitStack()
    qT, kT = sb(early, "qT", [P, H, TOK]), sb(early, "kT", [P, H, TOK])
    decay = sb(early, "decay", [P, 4, H, TOK])
    G, e1, e2, e3 = (decay[:, i] for i in range(4))
    vm = decay[:, :, :, :].rearrange("p a h t -> p (a h t)")[:, 0:4096].rearrange("p (b e) -> p b e", e=512)
    dec = sb(early, "dec", [P, H, NCH + N_SAMPLE])

    st = ExitStack()
    sub = [mixT[:, :, :].rearrange("p a b -> p (a b)")[:, 0:2048], sb(st, "sub", [P, 2048])[:, :]]
    subg = xT[:, :, :].rearrange("p a b -> p (a b)")[:, 0:2048]
    subp = sb(st, "subp", [16, 2048])
    subT = sb(st, "subT", [P, 16, 528])
    w1 = sb(st, "w1", [P, 16, P])
    w2 = sb(st, "w2", [P, 2, 64])
    hid = sb(st, "hid", [P, 2, N_SAMPLE * NCB + NCP])
    pt = sb(st, "pt", [P, 4], I32)
    idx = sb(st, "idx", [P, 4], I32)
    st.close()

    st = ExitStack()
    ktok = sb(st, "ktok", [P, 3, H, P])
    attS = sb(st, "attS", [P, 3, H, P])
    state = sb(st, "state", [P, NCH + 1, H, P])
    sstate = sb(st, "sstate", [P, N_SAMPLE, H, P])
    qGm = sb(st, "qGm", [P, H, N_SAMPLE, 32])
    st.close()
    early.close()

    st = ExitStack()
    qpad = sb(st, "qpad", [P, N_SAMPLE, 32])
    gsm = sb(st, "gsm", [P, 2, 3])
    slk, wk = sb(st, "slk", [P, 2, D]), sb(st, "wk", [P, 2, WIN])
    slv, wv = sb(st, "slv", [P, 4, D]), sb(st, "wv", [P, 4, WIN])
    st2 = ExitStack()
    PCp = sb(st2, "PCp", [P, 8, NCP])
    PS = sb(st2, "PS", [P, 2, 8, 256])
    PTp = sb(st2, "PTp", [P, 32, P])
    PCT = sb(st2, "PCT", [16, 8, P])
    st2.close()
    KT = sb(st, "KT", [P, 4, D + WIN])
    L = sb(st, "L", [P, 1600])
    LC = sb(st, "LC", [P, 2, NCB])
    pcs = sb(st, "pcs", [64, 2, P])
    ov = sb(st, "ov", [P, P])
    pen = sb(st, "pen", [P, P])
    st.close()
    zs.close()

    st = ExitStack()
    lnp = sb(st, "lnp", [P, 2, D])
    memp = sb(st, "memp", [P, 2, D])
    mkt, mvt = sb(st, "mkt", [P, 2, D]), sb(st, "mvt", [P, 2, D])
    so = memp[:, 0, :]
    mqT = sb(st, "mqT", [P, KC, TOK])
    KTm = sb(st, "KTm", [P, 2, KC, 256])
    mck, mcv = sb(st, "mck", [P, 2, 2, D]), sb(st, "mcv", [P, 4, 2, D])
    qpm = sb(st, "qpm", [P, N_SAMPLE, KC, 32])
    Pm = sb(st, "Pm", [P, 4, 256])
    PTm = sb(st, "PTm", [P, 8, P])
    Pmt = [Pm, memp[:, 1, :].rearrange("p (h m) -> p h m", m=256)]
    mst = [small[:, 80:96], small[:, 108:124]]
    st.close()

    st = ExitStack()
    lnp3 = sb(st, "lnp3", [P, 2, D])
    E_all, W_all = sb(st, "E_all", [P, NGRP + 8, GRP], I32), sb(st, "W_all", [P, NGRP + 8, GRP])
    E_cur, h_cur, g_cur, w_cur = sb(st, "E_cur", [P, 2, GRP], I32), sb(st, "h_cur", [P, GRP]), sb(st, "g_cur", [P, GRP]), sb(st, "w_cur", [P, GRP])
    after_x2T = feat[:, :, :, :].rearrange("p a b c -> p (a b c)")
    Y = after_x2T[:, 0:3 * D].rearrange("p (t d) -> p t d", d=D)
    x_cur = after_x2T[:, 3 * D:4 * D]
    diag = sb(st, "diag", [P, GRP, P])
    sc = sb(st, "sc", [P, 24, 2, P])

    def route_memory(stack, name, R):
        return dict(R=R, tv=sb(stack, name + "_tv", [P, R, 2, 16]), ti=sb(stack, name + "_ti", [P, R, 2, 16], U32),
                    tif=sb(stack, name + "_tif", [P, R, 2, 16]), cand=sb(stack, name + "_cand", [P, R, 256]),
                    cv=sb(stack, name + "_cv", [P, R, 16]), cj=sb(stack, name + "_cj", [P, R, 16], U32),
                    ja=sb(stack, name + "_ja", [P, 2, R * 16], U32), jaf=sb(stack, name + "_jaf", [P, 2, R * 16]),
                    ef=sb(stack, name + "_ef", [P, 2, R * 16]), eqm=sb(stack, name + "_eqm", [P, R * 16, 16]),
                    texp=sb(stack, name + "_texp", [P, R, 16]), tsum=sb(stack, name + "_tsum", [P, 2, R]))

    R2 = route_memory(st, "two", 2)
    xs = sb(st, "xs", [P, 2, 2, P])
    e_two, w_two = sb(st, "e_two", [P, 2, 16], I32), sb(st, "w_two", [P, 2, 16])
    skey = sc[:, 0:8].rearrange("p h c k -> p (h c) k")
    st2 = ExitStack()
    skT = sb(st2, "skT", [P, 16, P])
    pqT = sb(st2, "pqT", [P, 16, TOK])
    st2.close()
    fetched = sb(st, "fetched", [P, 16, D])
    wrows = wbuf[:, :, :, :].rearrange("p a b c -> p (a b c)").rearrange("p (s d) -> p s d", d=D)
    uslot = [fetched[:, 8 + k % 8, :] for k in range(GRP)]
    vslot = [wrows[:, k, :] if k < 8 else fetched[:, k - 8, :] for k in range(GRP)]
    st.close()

    block = ctx.enter_context(nc.Block())

    def bank(key):
        return psum[:, JOB[key] % 8, :]

    def filled(eng, key):
        eng.wait_ge(bank_full[JOB[key] % 8], JOB[key] // 8 + 1)

    def evacuated(eng, key):
        eng.wait_ge(bank_free[JOB[key] % 8], JOB[key] // 8 + 1)

    def release(eng, ins, key, wait=False):
        ins.then_inc(bank_free[JOB[key] % 8], 1)
        if wait:
            evacuated(eng, key)

    def copy_out(eng, key, dst, src, scale=None):
        on_act = JOB[key] % 2 == 1
        if (eng is nc.scalar) != on_act:
            return
        filled(eng, key)
        if on_act:
            ins = nc.scalar.activation(dst, src, ACT.Copy, scale=1.0 if scale is None else scale)
        elif scale is None:
            ins = nc.vector.tensor_copy(dst, src)
        else:
            ins = nc.vector.tensor_scalar(dst, src, scale, None, ALU.mult)
        release(eng, ins, key)

    def bc(ap, axis, n):
        v = ap.unsqueeze(axis)
        shape = list(v.shape)
        shape[axis] = n
        return v.to_broadcast(shape)

    def split(ap, n):
        return ap.rearrange("p (a b) -> p a b", b=n)

    def toks(t):
        return TILES[t][0], TILES[t][1]

    def copy_xT(eng, name, ntile=3, dst=None):
        for t in range(ntile):
            t0, n = toks(t)
            for c in range(2):
                d = (xT if dst is None else dst)[:, 4 * c:4 * c + 4, t0:t0 + n]
                copy_out(eng, (name, t, c), d, split(bank((name, t, c)), P)[:, :, 0:n])

    def copy_hq(eng):
        for h in range(H):
            copy_out(eng, ("zf", H + h), qT[:, h, :], bank(("zf", H + h))[:, 0:TOK])

    def copy_z(eng, g):
        _, o, w = Z_GROUPS[g]
        for t in range(3):
            n = toks(t)[1]
            copy_out(eng, ("z", g, t), z[0:n, t, o:o + w], bank(("z", g, t))[0:n, 0:w])

    def copy_zq(eng):
        for j in range(4):
            copy_out(eng, ("zq", j), qn[:, j, :], bank(("zq", j))[:, 0:TOK], 0.125)

    def copy_subT(eng, kv):
        if kv == 1:
            filled(eng, ("hidp", 0))
        g = 1 if eng is nc.vector else 0
        for i in range(4):
            n = 4 * kv + i
            eng.wait_ge(s_sub[n % NSUBS], 16 * (n // NSUBS + 1))
            if n == 0:
                filled(eng, ("z", 3, 2))
            else:
                filled(eng, ("subT", (n - 1) // 4, (n - 1) % 4, 2 * g + 1))
            dst, src = subg[:, 1024 * g:1024 * g + 1024], sub[n % NSUBS].rearrange("p (s g d) -> p g s d", g=2, s=16)[:, g]
            if g == 1:
                nc.vector.tensor_copy(split(dst, 64), src).then_inc(s_sorted[1], 1)
            else:
                nc.scalar.copy(split(dst, 64), src).then_inc(s_sorted[0], 1)
            for q in range(4):
                copy_out(eng, ("subT", kv, i, q), subT[:, 4 * q:4 * q + 4, i * P:(i + 1) * P], split(bank(("subT", kv, i, q)), P))
        copy_out(eng, ("subT", kv, 4, 0), subT[:, :, 512:528], split(bank(("subT", kv, 4, 0))[:, 0:256], 16))

    def copy_pT(eng, t):
        if t == 1:
            filled(eng, ("pv", 0))
        for k in range(4 * (t + 1)):
            copy_out(eng, ("pT", t, k), PTp[:, 4 * k:4 * k + 4, :], split(bank(("pT", t, k)), P))
        for k in range(2):
            copy_out(eng, ("pcT", t, k), PCT[0:NCP, 4 * k:4 * k + 4, :], split(bank(("pcT", t, k))[0:NCP], P))

    def copy_skT(eng, u):
        if u == 1:
            filled(eng, ("sn", 0))
        for b in range(4):
            for k in range(3):
                copy_out(eng, ("skT", u, b, k), KT[:, b, 512 * k:512 * k + 512], bank(("skT", u, b, k)))

    def copy_spT(eng, u):
        if u == 1:
            filled(eng, ("spv", 0))
        for k in range(3):
            copy_out(eng, ("spT", u, k), PTs[:, 4 * k:4 * k + 4, :], split(bank(("spT", u, k)), P))
        copy_out(eng, ("spT", u, 3), PTs[0:32, 12:14, :], split(bank(("spT", u, 3))[0:32, 0:256], P))

    def copy_mkT(eng, seq):
        if seq >= 2:
            filled(eng, ("ms", 1, 1) if seq == 2 else ("sms", (seq - 3) // 4, (seq - 3) % 4))
        for q in range(4):
            copy_out(eng, ("mkT", seq, q), KTm[:, seq % 2, 2 * q:2 * q + 2, :], split(bank(("mkT", seq, q)), 256))

    def copy_oT(eng, k):
        t0, n = toks(k)
        copy_out(eng, ("oT", k), mixT[:, 0:4, t0:t0 + n], split(bank(("oT", k)), P)[:, :, 0:n])

    def copy_mkv(eng):
        for name, dst in (("mk", mkt), ("mv", mvt)):
            for c in range(2):
                for t in range(2):
                    copy_out(eng, (name, c, t), dst[:, t, GW * c:GW * c + GW], bank((name, c, t)))

    def copy_mq(eng):
        for c in range(KC):
            copy_out(eng, ("mq", c), mqT[:, c, :], bank(("mq", c))[:, 0:TOK], 1.0 / 16)

    def copy_mp(eng, t):
        for k in range(2):
            copy_out(eng, ("mpT", t, k), PTm[:, 4 * k:4 * k + 4, :], split(bank(("mpT", t, k)), P))
        for k in range(2):
            copy_out(eng, ("mo", t, k), mixT[:, 4 * k:4 * k + 4, P * t:P * t + P], split(bank(("mo", t, k)), P))

    def copy_sms(eng, u, b):
        if b == 0:
            filled(eng, ("mpT", 1, 1) if u == 0 else ("smpT", 0))
        copy_out(eng, ("sms", u, b), Pm[32 * b:32 * b + 32, 0, :], bank(("sms", u, b))[32 * b:32 * b + 32, 0:256])

    def copy_smpT(eng, u):
        filled(eng, ("mo", 1, 1) if u == 0 else ("smo", 0, 1))
        copy_out(eng, ("smpT", u), PTm[:, 0:2, :], split(bank(("smpT", u))[:, 0:256], P))

    def copy_skeyT(eng):
        for q in range(4):
            copy_out(eng, ("skeyT", q), skT[:, 4 * q:4 * q + 4, :], split(bank(("skeyT", q)), P))

    def copy_pq(eng, first, last):
        for c in range(first, last):
            copy_out(eng, ("pq", c), pqT[:, c, :], bank(("pq", c))[:, 0:TOK])

    def copy_ps(eng, t, qs=range(4)):
        n = toks(t)[1]
        for q in qs:
            copy_out(eng, ("ps", t, q), sc[0:n, 8 * t + 2 * q:8 * t + 2 * q + 2].rearrange("p h c k -> p (h c) k"), split(bank(("ps", t, q)), P)[0:n])

    @block.sync
    def _(sp):
        def weights(n):
            name, o, w, _ = W_GROUPS[n]
            if n >= 2:
                filled(sp, W_GROUPS[n - 2][3])
            dst, src, done = wbuf[:, n % 2], A[name][0], s_w[n % 2]
            if name == "w_out":
                sp.dma_start(dst[:, 0:4, 0:w], src[0:512, o:o + w].rearrange("(c p) n -> p c n", p=P)).then_inc(done, 16)
                for g in range(2):
                    rows = src[512 + 256 * g:768 + 256 * g, o:o + w].rearrange("(j d) n -> d j n", d=64)
                    sp.dma_start(dst[64 * g:64 * g + 64, 4:8, 0:w], rows).then_inc(done, 16)
            elif (name, o) == ("w_in", NQ):
                for h in range(8):
                    to, cols = P * (h % 4) + 64 * (h // 4), slice(o + 64 * h, o + 64 * h + 64)
                    sp.dma_start(dst[:, :, to:to + 64], src[:, cols].rearrange("(c p) n -> p c n", p=P)).then_inc(done, 16)
            else:
                sp.dma_start(dst[:, :, 0:w], src[:, o:o + w].rearrange("(c p) n -> p c n", p=P)).then_inc(done, 16)

        sp.dma_start(cst[:, 0:P], A["consts"][:, 0:P]).then_inc(s_const, 16)
        sp.dma_start(xt[:, 0:2, :], A["x_prompt"][0].rearrange("(t p) d -> p t d", p=P)).then_inc(s_x, 16)
        sp.dma_start(xt[0:32, 2, :], A["x_sample"].rearrange("b s d -> (b s) d")).then_inc(s_x, 16)
        weights(0)
        weights(1)
        sp.dma_start(cst[:, P:], A["consts"][:, P:]).then_inc(s_const, 16)
        sp.dma_start(lbl, A["hgrn_lb_logits"].rearrange("a (h p) -> p a h", p=P), allow_slow_non_contiguous=True).then_inc(s_par, 16)
        sp.dma_start(b1[:, 0:1], A["cmp_k_b1"].rearrange("a h -> h a"), allow_slow_non_contiguous=True).then_inc(s_par, 16)
        sp.dma_start(b1[:, 1:2], A["cmp_v_b1"].rearrange("a h -> h a"), allow_slow_non_contiguous=True).then_inc(s_par, 16)
        for g in range(2):
            sp.dma_start(b2k[64 * g:64 * g + 64, :], A["cmp_k_b2"].rearrange("a h -> h a"), allow_slow_non_contiguous=True).then_inc(s_par, 16)
            sp.dma_start(b2v[:, 64 * g:64 * g + 64], A["cmp_v_b2"].to_broadcast([P, 64])).then_inc(s_par, 16)
        sp.dma_start(hng, A["hgrn_norm_g"].to_broadcast([P, P])).then_inc(s_par, 16)
        w1_dram = [A[n][0].rearrange("a d h -> (a d) h").rearrange("(c k) h -> k c h", k=P) for n in ("cmp_k_w1", "cmp_v_w1")]
        sp.dma_start(w2[:, 0, :], A["cmp_k_w2"][0]).then_inc(s_cw, 16)
        sp.dma_start(w2[:, 1, :], A["cmp_v_w2"][0]).then_inc(s_cw, 16)
        sp.dma_start(w1[:, :, :], w1_dram[0]).then_inc(s_cw, 16)
        for n in range(2, 9):
            weights(n)
        for g in range(2, 4):
            for t in range(3):
                evacuated(sp, ("z", g, t))
        for i, c in enumerate((KCC, VCC, KSC, VSC, KWC, VWC)):
            sp.dma_start(O[2 + i][0, 0].rearrange("(t p) g d -> p t (g d)", p=P), z[:, 0:2, c:c + P]).then_inc(s_kvout, 16)
            sp.dma_start(O[11 + i][0].rearrange("b s g d -> (b s) (g d)"), z[0:32, 2, c:c + P]).then_inc(s_kvout, 16)
            if i < 2:
                sp.wait_ge(s_kvout, 32 * (i + 1))
                if i == 1:
                    filled(sp, ("subT", 0, 4, 0))
                for g in range(2):
                    sp.dma_start(subp[:, 1024 * g:1024 * g + 1024], O[2 + i][0, 0].rearrange("(n s) g d -> n g s d", s=16)[:, g]).then_inc(s_subp, 16)
        filled(sp, ("hidp", 0))
        sp.dma_start(w1[:, :, :], w1_dram[1]).then_inc(s_cw, 16)
        for s in s_end["cmp"]:
            sp.wait_ge(s, 1)
        sp.dma_start(sstate[:, :, :, :], A["state_hgrn"][0].rearrange("b h d e -> d b h e")).then_inc(s_stin, 16)
        evacuated(sp, ("U", NCH - 1))
        sp.dma_start(O[8][0, 0].rearrange("h d e -> d h e"), state[:, NCH]).then_inc(s_stout, 16)
        evacuated(sp, ("US", N_SAMPLE - 1))
        sp.dma_start(O[17][0].rearrange("b h d e -> d b h e"), sstate[:, :, :, :]).then_inc(s_out, 16)
        for s in s_end["nsa"]:
            sp.wait_ge(s, 1)
        sp.dma_start(memp[:, :, :], A["mem_prompt"][0].rearrange("(t p) d -> p t d", p=P)).then_inc(s_mem, 16)
        sp.dma_start(lnp[:, 0, :], A["ln1_g"].to_broadcast([P, D])).then_inc(s_lnp, 16)
        sp.dma_start(lnp[:, 1, :], A["ln1_b"].to_broadcast([P, D])).then_inc(s_lnp, 16)
        for n in range(9, 14):
            weights(n)
        for i, (buf, key) in enumerate(((mkt, "mk"), (mvt, "mv"))):
            for c in range(2):
                for t in range(2):
                    evacuated(sp, (key, c, t))
            sp.dma_start(O[9 + i][0, 0].rearrange("(t p) h d -> p t (h d)", p=P), buf[:, :, :]).then_inc(s_mkout, 16)
        sp.wait_ge(s_ln, 3)
        sp.dma_start(lnp[:, 0, :], A["ln2_g"].to_broadcast([P, D])).then_inc(s_lnp, 16)
        sp.dma_start(lnp[:, 1, :], A["ln2_b"].to_broadcast([P, D])).then_inc(s_lnp, 16)
        for n in range(14, 17):
            weights(n)
        sp.wait_ge(s_mkout, 32)
        for s in s_end["mem"]:
            sp.wait_ge(s, 1)
        sp.dma_start(skey[:, :, :], A["peer_sub_keys"][0].rearrange("h c k d -> k (h c) d")).then_inc(s_skey, 16)
        weights(17)
        weights(18)
        sp.wait_ge(s_ln, 6)
        sp.dma_start(lnp3[:, 0, :], A["ln3_g"].to_broadcast([P, D])).then_inc(s_lnp, 16)
        sp.dma_start(lnp3[:, 1, :], A["ln3_b"].to_broadcast([P, D])).then_inc(s_lnp, 16)
        weights(19)
        weights(20)
        for q in range(1, 4):
            sp.dma_start(xt[32 * q:32 * q + 32, 2, :], xt[0:32, 2, :]).then_inc(s_fold, 16)
        sp.wait_ge(s_route, 12)
        for q in range(4):
            h0 = NGRP + 2 * q
            sp.dma_start(E_all[32 * q:32 * q + 32, 16:18, :], E_all[0:32, h0:h0 + 2, :]).then_inc(s_fold, 16)
            sp.dma_start(W_all[32 * q:32 * q + 32, 16:18, :], W_all[0:32, h0:h0 + 2, :]).then_inc(s_fold, 16)
        sp.wait_ge(s_ln, 8)
        sp.dma_start(O[0][0].rearrange("(t p) d -> p t d", p=P), xt[:, 0:2, :]).then_inc(s_out, 16)
        sp.wait_ge(s_ln, 9)
        sp.dma_start(O[1].rearrange("b s d -> (b s) d"), xt[0:32, 2, :]).then_inc(s_out, 16)
        sp.wait_ge(s_out, 48)
        sp.wait_ge(s_stout, 16)
        sp.wait_ge(s_kvout, 192)

    @block.gpsimd
    def _(pool):
        def gather(dst, table, index, done):
            return nc.gpsimd.indirect_dma_start(out=dst, out_offset=None, in_=table,
                                                in_offset=bass.IndirectOffsetOnAxis(ap=index, axis=0)).then_inc(done, 16)

        pages = A["page_table"].rearrange("b j -> (b j)").rearrange("(i q) -> q i", q=16)
        for q in range(16):
            nc.gpsimd.dma_start(pt[8 * q:8 * q + 8, :], pages[q:q + 1, :].to_broadcast([8, 4]), allow_slow_non_contiguous=True).then_inc(s_pt, 16)
        pages = A["page_table"].rearrange("b j -> j b")
        for q in range(8):
            nc.gpsimd.dma_start(ptab[16 * q:16 * q + 16, :], pages[q:q + 1, :].to_broadcast([16, 8]), allow_slow_non_contiguous=True).then_inc(s_pts, 16)
        pool.wait_ge(s_idx, 1)
        fetches = []
        for kv, cache in enumerate((A["cache_k_cmp"], A["cache_v_cmp"])):
            rows = cache[0].rearrange("n (r s) g d -> (n r) (s g d)", s=16)
            for i in range(4):
                fetches.append((rows, i))
        for n, (rows, i) in enumerate(fetches):
            if n >= NSUBS:
                for g in range(2):
                    pool.wait_ge(s_sorted[g], n - NSUBS + 1)
            gather(sub[n % NSUBS], rows, idx[:, i:i + 1], s_sub[n % NSUBS])
        pool.wait_ge(s_sgate, 2)
        pool.wait_ge(s_par, 16 * 8)
        for ts, rows in ((slice(0, 2), P), (slice(2, 3), 32)):
            gate = z[0:rows, ts, HG:HG + 512].rearrange("p t (h e) -> p t h e", e=P)
            for t in range(ts.stop - ts.start):
                ins = nc.gpsimd.tensor_tensor(gate[:, t], gate[:, t], bc(hng[0:rows], 1, H), ALU.mult)
            ins.then_inc(s_gz, 1)
        for s in s_end["hgrn"]:
            pool.wait_ge(s, 1)
        pool.wait_ge(s_stout, 16)
        pool.wait_ge(s_idx, 2)
        rk, rv = (A[n][0].rearrange("n (r s) g d -> (n r) (s g d)", s=8) for n in ("cache_k_slc", "cache_v_slc"))
        for b in range(N_SAMPLE):
            u, b4 = b // 4, b % 4
            if b >= 2:
                filled(pool, ("skT", (b - 2) // 4, (b - 2) % 4, 2))
            gather(slk[:, b % 2, :], rk, sidx[:, b:b + 1], s_slk[b % 2])
            nc.gpsimd.dma_start(wk[:, b % 2, :], A["cache_k_win"][0, b].rearrange("(p s) g d -> p (s g d)", s=4)).then_inc(s_slk[b % 2], 16)
            if b == 4:
                filled(pool, ("spv", 0))
            gather(slv[:, b4, :], rv, sidx[:, b:b + 1], s_slv[b4])
            nc.gpsimd.dma_start(wv[:, b4, :], A["cache_v_win"][0, b].rearrange("(p s) g d -> p (s g d)", s=4)).then_inc(s_slv[b4], 16)
        for s in s_end["nsa"]:
            pool.wait_ge(s, 1)
        filled(pool, ("mk", 0, 0))
        for b in range(N_SAMPLE):
            if b >= 2:
                filled(pool, ("mkT", b - 1, 3))
            nc.gpsimd.dma_start(mck[:, b % 2, :, :], A["cache_mem_k"][0, b].rearrange("(p i) h d -> p i (h d)", i=2)).then_inc(s_mck[b % 2], 16)
            if b == 4:
                filled(pool, ("smo", 0, 1))
            nc.gpsimd.dma_start(mcv[:, b % 4, :, :], A["cache_mem_v"][0, b].rearrange("(p i) h d -> p i (h d)", i=2)).then_inc(s_mcv[b % 4], 16)
        u_count, v_count = (pool.alloc_register(n) for n in ("u_count", "v_count"))
        pool.reg_mov(u_count, 1)
        pool.reg_mov(v_count, 1)

        def slot_read(free, count, g, k):
            if isinstance(g, int):
                pool.wait_ge(free, GRP * g + k + 1)
            else:
                pool.wait_ge(free, count)
                pool.reg_add(count, count, 1)

        def two_turns(pair):
            for odd in range(2):
                g = pair * 2 + odd
                nc.gpsimd.tensor_copy(E_cur[:, odd, :], E_all[:, bass.ds(g, 1), :].rearrange("p a k -> p (a k)")).then_inc(pool_step, 1)
                pool.wait_ge(pool_step, g + 1)
                for k in range(GRP):
                    slot_read(u_free, u_count, g, k)
                    gather(uslot[k], A["peer_u"][0], E_cur[:, odd, k:k + 1], s_u[k % 8])
                for k in range(GRP):
                    slot_read(v_free, v_count, g, k)
                    gather(vslot[k], A["peer_v"][0], E_cur[:, odd, k:k + 1], s_v[k])

        with pool.Fori(0, 8) as pair:
            pool.wait_ge(s_route, pair + 1)
            two_turns(pair)
        pool.wait_ge(s_fold, 16 * 11)
        two_turns(8)

    @block.scalar
    def _(act):
        S = Lane(act, act_step)
        copy_xT(act, "xT")
        for h in range(H):
            key = ("zf", h)
            filled(act, key)
            S(nc.scalar.activation(e1[:, h, :], bank(key)[:, 0:TOK], ACT.Sigmoid), wait=False)
            release(act, nc.scalar.activation(kT[:, h, :], bank(key)[:, 0:TOK], ACT.Sigmoid, scale=-1.0), key)
        copy_hq(act)
        act.wait_ge(s_lb, 1)
        S(nc.scalar.activation(lb, small[:, 0:4], ACT.Sigmoid), s_lb)
        copy_z(act, 0)
        act.wait_ge(s_f, 1)
        S(nc.scalar.activation(e2, e1, ACT.Ln), s_lnf)
        copy_z(act, 1)
        act.wait_ge(s_g, 1)
        S(nc.scalar.activation(e2, e1, ACT.Exp), wait=False)
        S(nc.scalar.activation(e3, e1, ACT.Exp, scale=-1.0), s_hexp)
        copy_zq(act)
        act.wait_ge(s_g, 2)
        S(nc.scalar.activation(G, G, ACT.Exp), wait=False)
        S(nc.scalar.activation(dec[:, :, :], dec[:, :, :], ACT.Exp), wait=False)
        S(nc.scalar.activation(e1, e1, ACT.Exp), s_hexp)
        copy_z(act, 2)
        copy_z(act, 3)
        act.wait_ge(s_par, 16 * 8)
        for kv in range(2):
            copy_subT(act, kv)
            if kv == 1:
                filled(act, ("kcTp",))
            for g in range(2):
                filled(act, ("hid", kv, g))
                release(act, nc.scalar.activation(hid[:, g, 0:504], bank(("hid", kv, g))[:, 0:504], ACT.Gelu_apprx_tanh,
                                                  bias=b1[:, kv:kv + 1]), ("hid", kv, g))
            filled(act, ("hidp", kv))
            release(act, nc.scalar.activation(hid[:, :, 504:519], split(bank(("hidp", kv))[:, 0:30], 15), ACT.Gelu_apprx_tanh,
                                              bias=b1[:, kv:kv + 1]), ("hidp", kv), wait=True)
        filled(act, ("vcp",))
        act.sem_inc(s_end["cmp"][1], 1)
        for s in s_end["cmp"]:
            act.wait_ge(s, 1)
        for t, rows in ((slice(0, 2), P), (slice(2, 3), 32)):
            S(nc.scalar.activation(z[0:rows, t, HG:HG + 512], z[0:rows, t, HG:HG + 512], ACT.Sigmoid), s_sgate)
            S(nc.scalar.activation(z[0:rows, t, NG:NG + 24], z[0:rows, t, NG:NG + 24], ACT.Sigmoid), s_gates)
        for t in range(3):
            n = toks(t)[1]
            filled(act, ("kE", t))
            release(act, nc.scalar.copy(ktok[0:n, t], split(bank(("kE", t)), P)[0:n]), ("kE", t))
        for t in range(3):
            n = toks(t)[1]
            filled(act, ("oin", t))
            release(act, nc.scalar.copy(otok[0:n, t], split(bank(("oin", t)), P)[0:n]), ("oin", t), wait=True)
        act.wait_ge(s_ms, 1)
        S(nc.scalar.activation(small[:, 16:28], small[:, 0:12], ACT.Sqrt), s_rs)
        act.sem_inc(s_end["hgrn"][1], 1)
        for s in s_end["hgrn"]:
            act.wait_ge(s, 1)
        for t in range(2):
            K = P * (t + 1)
            act.wait_ge(s_mx, 3 * t + 1)
            S(nc.scalar.activation(PCp[:, :, :], PCp[:, :, :], ACT.Exp), s_exp)
            for br in range(2):
                act.wait_ge(s_mx, 3 * t + 2 + br)
                for h in range(8):
                    i = 8 * br + h
                    S(nc.scalar.activation(PS[:, br, h, 0:K], PS[:, br, h, 0:K], ACT.Exp, bias=small[:, i:i + 1],
                                           accum_out=small[:, 16 + i:17 + i]), s_exp if h == 7 else None, wait=(h == 7))
            if t == 0:
                for k in range(3):
                    copy_oT(act, k)
                act.wait_ge(s_out, 16)
            copy_pT(act, t)
        evacuated(act, ("pv", 1))
        for u in range(2):
            act.wait_ge(s_cmx, u + 1)
            S(nc.scalar.activation(LC[:, 0, :], LC[:, 0, :], ACT.Exp, bias=small[:, 64:65], accum_out=small[:, 65:66]), s_cexp)
            copy_skT(act, u)
            act.wait_ge(s_smx, u + 1)
            S(nc.scalar.activation(L[:, 0:1056], L[:, 0:1056], ACT.Exp, bias=small[:, 72:73], accum_out=small[:, 74:75]), wait=False)
            S(nc.scalar.activation(L[:, 1056:1600], L[:, 1056:1600], ACT.Exp, bias=small[:, 73:74], accum_out=small[:, 75:76]), s_sexp)
            copy_spT(act, u)
        evacuated(act, ("spvT", 1))
        act.sem_inc(s_end["nsa"][1], 1)
        for s in s_end["nsa"]:
            act.wait_ge(s, 1)

        def roots(k, tiles=range(3)):
            for t in tiles:
                n = toks(t)[1]
                act.wait_ge(s_lnv, 3 * k + t + 1)
                S(nc.scalar.activation(small[0:n, 104 + t:105 + t], small[0:n, 100 + t:101 + t], ACT.Sqrt), s_lnr)

        roots(0, range(1))
        copy_xT(act, "memT", 2, memT)
        roots(0, range(1, 3))
        copy_mkv(act)
        copy_xT(act, "x1T")
        copy_mq(act)
        copy_mkT(act, 0)
        for t in range(2):
            act.wait_ge(s_mmx, t + 1)
            for h in range(H):
                ins = nc.scalar.activation(Pmt[t][:, h, :], bank(("ms", t, h // 2))[:, 256 * (h % 2):256 * (h % 2) + 256], ACT.Exp,
                                           bias=mst[t][:, h:h + 1], accum_out=mst[t][:, 4 + h:5 + h])
                if h % 2:
                    release(act, ins, ("ms", t, h // 2))
                else:
                    S(ins, wait=False)
        copy_mkT(act, 1)
        for t in range(2):
            copy_mp(act, t)
        for u in range(2):
            for b in range(4):
                if u + b > 0:
                    copy_mkT(act, 1 + 4 * u + b)
                copy_sms(act, u, b)
            act.wait_ge(s_mmx, 3 + u)
            S(nc.scalar.activation(Pm[:, 0, :], Pm[:, 0, :], ACT.Exp, bias=small[:, 80:81], accum_out=small[:, 84:85]), s_mexp)
            copy_smpT(act, u)
        evacuated(act, ("smoT", 1, 1))
        act.sem_inc(s_end["mem"][1], 1)
        for s in s_end["mem"]:
            act.wait_ge(s, 1)
        roots(1, range(2))
        copy_skeyT(act)
        roots(1, range(2, 3))
        copy_xT(act, "x2T")
        copy_pq(act, 0, 4)
        copy_ps(act, 0, [0])
        copy_pq(act, 4, 6)
        act.wait_ge(s_tmx, 1)
        S(nc.scalar.activation(R2["texp"][:, :, :], R2["texp"][:, :, :], ACT.Exp), s_texp)
        copy_pq(act, 6, 8)
        copy_ps(act, 0, [1])
        copy_pq(act, 8, 10)
        act.wait_ge(s_tmx, 2)
        S(nc.scalar.activation(R2["texp"][:, :, :], R2["texp"][:, :, :], ACT.Exp), s_texp)
        copy_pq(act, 10, 16)
        for t in range(3):
            copy_ps(act, t, range(2 if t == 0 else 0, 4))

        def turn(g):
            act.wait_ge(h_done, g + 1)
            nc.scalar.activation(g_cur[:, :], h_cur[:, :], ACT.Gelu_apprx_tanh).then_inc(gelu_done, 1)
            act.wait_ge(w_done, g + 1)
            for k in range(GRP):
                act.wait_ge(v_free, GRP * g + k + 1)
                nc.scalar.activation(diag[:, k, :], ident, ACT.Copy, scale=w_cur[:, k:k + 1]).then_inc(diag_done, 1)

        turn(0)
        with act.Fori(1, 11) as g:
            turn(g)
            act.wait_ge(s_tmx, g + 2)
            nc.scalar.activation(R2["texp"][:, :, :], R2["texp"][:, :, :], ACT.Exp).then_inc(s_texp, 1)
        with act.Fori(11, 16) as g:
            turn(g)
        roots(2, range(2))
        with act.Fori(16, NGRP) as g:
            turn(g)
        roots(2, range(2, 3))

    @block.vector
    def _(dve):
        V = Lane(dve, dve_step)
        v = nc.vector

        def residual(name, t):
            for c in range(2):
                n = toks(t)[1]
                x = xt[0:n, t, GW * c:GW * c + GW]
                filled(dve, (name, t, c))
                release(dve, v.scalar_tensor_tensor(out=x, in0=x, scalar=ALPHA, in1=bank((name, t, c))[0:n], op0=ALU.mult, op1=ALU.add),
                        (name, t, c), wait=True)

        copy_xT(dve, "xT")
        dve.wait_ge(s_const, 32)
        dve.wait_ge(s_pt, 16 * 16)
        V(v.tensor_scalar(idx[:, :], pt[:, :], 8.0, C("mod8"), ALU.mult, ALU.add), s_idx)
        dve.wait_ge(s_par, 16 * 8)
        V(v.tensor_tensor(small[:, 0:4], lbl[:, 0, :], lbl[:, 1, :], ALU.subtract), s_lb)
        copy_hq(dve)
        dve.wait_ge(s_pts, 16 * 8)
        V(v.tensor_scalar(sidx[:, :], ptab[:, :], 16.0, C("mod16"), ALU.mult, ALU.add), s_idx)
        dve.wait_ge(s_lb, 2)
        V(v.tensor_scalar(omlb, lb, -1.0, 1.0, ALU.mult, ALU.add))
        copy_z(dve, 0)
        for h in range(H):
            evacuated(dve, ("zf", h))
        for h in range(H):
            V(v.tensor_scalar(e1[:, h, :], e1[:, h, :], omlb[:, h:h + 1], lb[:, h:h + 1], ALU.mult, ALU.add), wait=False)
        for h in range(H):
            V(v.tensor_scalar(kT[:, h, :], kT[:, h, :], omlb[:, h:h + 1], None, ALU.mult), s_f if h == 3 else None, wait=(h == 3))
        copy_z(dve, 1)
        dve.wait_ge(s_lnf, 1)
        for h in range(H):
            V(v.tensor_tensor_scan(G[:, h, :], C("keep"), e2[:, h, :], 0.0, ALU.mult, ALU.add), wait=(h == 3))
        Gp = G[:, :, 0:T_PROMPT].rearrange("p h (c s) -> p h c s", s=CH)
        Gs = G[:, :, T_PROMPT:TOK].rearrange("p h (b s) -> p h b s", s=STEPS)
        Ep = e1[:, :, 0:T_PROMPT].rearrange("p h (c s) -> p h c s", s=CH)
        Es = e1[:, :, T_PROMPT:TOK].rearrange("p h (b s) -> p h b s", s=STEPS)
        for h in range(H):
            V(v.tensor_tensor(Ep[:, h], Gp[:, h], Gp[:, h, :, CH // 2 - 1:CH // 2].to_broadcast([P, NCH, CH]), ALU.subtract), wait=False)
        V(v.tensor_copy(e1[:, :, T_PROMPT:TOK], G[:, :, T_PROMPT:TOK]), s_g)
        copy_zq(dve)
        dve.wait_ge(s_hexp, 1)
        V(v.tensor_tensor(e2, qT[:, :, :], e2, ALU.mult), wait=False)
        V(v.tensor_tensor(e3, kT[:, :, :], e3, ALU.mult), s_ke)
        for h in range(H):
            V(v.tensor_tensor(Ep[:, h], Gp[:, h, :, CH - 1:CH].to_broadcast([P, NCH, CH]), Gp[:, h], ALU.subtract), wait=False)
            V(v.tensor_tensor(Es[:, h], Gs[:, h, :, STEPS - 1:STEPS].to_broadcast([P, N_SAMPLE, STEPS]), Gs[:, h], ALU.subtract), wait=False)
        V(v.tensor_copy(dec[:, :, 0:NCH], Gp[:, :, :, CH - 1]), wait=False)
        V(v.tensor_copy(dec[:, :, NCH:], Gs[:, :, :, STEPS - 1]), s_g)
        copy_z(dve, 2)
        dve.wait_ge(s_hexp, 2)
        for h in range(H):
            evacuated(dve, ("zf", H + h))
        V(v.tensor_tensor(qT[:, :, :], qT[:, :, :], G, ALU.mult), wait=False)
        V(v.tensor_tensor(kT[:, :, :], kT[:, :, :], e1, ALU.mult), s_ke)
        copy_z(dve, 3)
        copy_subT(dve, 0)
        for key, o, w in ((("kcT",), 0, 504), (("kcTp",), 504, NCP)):
            filled(dve, key)
            release(dve, v.tensor_scalar(kcT[:, o:o + w], bank(key)[:, 0:w], b2k, None, ALU.add), key)
        copy_subT(dve, 1)
        for k in range(2):
            filled(dve, ("vc", k))
            release(dve, v.tensor_tensor(vcS[0:NCB, 4 * k:4 * k + 4, :], split(bank(("vc", k))[0:NCB], P), bc(b2v[0:NCB], 1, 4), ALU.add), ("vc", k))
        filled(dve, ("vcp",))
        release(dve, v.tensor_tensor(vcP[0:NCP, :], bank(("vcp",))[0:NCP, 0:P], b2v[0:NCP], ALU.add), ("vcp",), wait=True)
        for t in range(3):
            t0, n = toks(t)
            filled(dve, ("nkT", t))
            release(dve, v.tensor_copy(kn[:, :, t0:t0 + n], split(bank(("nkT", t))[:, 0:256], P)[:, :, 0:n]), ("nkT", t))
        dve.sem_inc(s_end["cmp"][0], 1)
        for s in s_end["cmp"]:
            dve.wait_ge(s, 1)

        V(v.memset(state[:, 0], 0.0), wait=False)
        for h in range(H):
            V(v.tensor_tensor(qGm[:, h], C("bmask", 32), bc(qT[:, h, T_PROMPT:TOK], 1, N_SAMPLE), ALU.mult), s_ke if h == 3 else None, wait=(h == 3))
        for t in range(3):
            n = toks(t)[1]
            filled(dve, ("att", t))
            m = C("hmask") if t < 2 else C("hmask_s")[0:32]
            release(dve, v.tensor_tensor(attS[0:n, t, :, 0:n], split(bank(("att", t)), P)[0:n, :, 0:n], bc(m, 1, H), ALU.mult), ("att", t), wait=True)
        for b in range(N_SAMPLE):
            V(v.tensor_scalar(vm[0:32, b, :], z[0:32, 2, HI:HI + 512], C("brow")[0:32, b:b + 1], None, ALU.mult), s_vm, wait=False)
        for c in range(NCH):
            key = ("U", c)
            filled(dve, key)
            for h in range(H):
                ins = v.scalar_tensor_tensor(out=state[:, c + 1, h, :], in0=state[:, c, h, :], scalar=dec[:, h, c:c + 1],
                                             in1=bank(key)[:, P * h:P * h + P], op0=ALU.mult, op1=ALU.add)
                if h < 3:
                    V(ins, wait=False)
                else:
                    release(dve, ins, key, wait=True)
        for t in range(3):
            n = toks(t)[1]
            filled(dve, ("ost", t))
            evacuated(dve, ("oin", t))
            release(dve, v.tensor_tensor(otok[0:n, t], split(bank(("ost", t)), P)[0:n], otok[0:n, t], ALU.add), ("ost", t), wait=True)
        for b in range(N_SAMPLE):
            key = ("US", b)
            filled(dve, key)
            for h in range(H):
                ins = v.scalar_tensor_tensor(out=sstate[:, b, h, :], in0=sstate[:, b, h, :], scalar=dec[:, h, NCH + b:NCH + b + 1],
                                             in1=bank(key)[:, P * h:P * h + P], op0=ALU.mult, op1=ALU.add)
                if h < 3:
                    V(ins, wait=False)
                else:
                    release(dve, ins, key)
        V(v.memset(small[:, 0:12], 1.0))
        last = (2, H - 1)
        for t in range(3):
            n = toks(t)[1]
            for h in range(H):
                i, o = 4 * t + h, otok[0:n, t, h, :]
                V(v.tensor_tensor_reduce(out=attS[0:n, t, h, :], in0=o, in1=o, scale=1.0, scalar=0.0, op0=ALU.mult, op1=ALU.add,
                                         accum_out=small[0:n, i:i + 1]), wait=((t, h) == last))
        V(v.tensor_scalar(small[:, 0:12], small[:, 0:12], 1.0 / P, EPS, ALU.mult, ALU.add), s_ms)
        dve.wait_ge(s_rs, 1)
        V(v.reciprocal(small[:, 32:44], small[:, 16:28]))
        dve.wait_ge(s_gz, 2)
        for t in range(3):
            n = toks(t)[1]
            for h in range(H):
                i, o = 4 * t + h, otok[0:n, t, h, :]
                V(v.scalar_tensor_tensor(out=o, in0=o, scalar=small[0:n, 32 + i:33 + i], in1=z[0:n, t, HG + P * h:HG + P * h + P],
                                         op0=ALU.mult, op1=ALU.mult), s_otok if h == H - 1 else None, wait=((t, h) == last))
        dve.sem_inc(s_end["hgrn"][0], 1)
        for s in s_end["hgrn"]:
            dve.wait_ge(s, 1)
        dve.wait_ge(s_stout, 16)

        V(v.memset(qpad[:, :, :], 0.0))
        for j in range(4):
            evacuated(dve, ("zq", j))
        for g in range(2):
            rows = slice(64 * g, 64 * g + 64)
            V(v.tensor_copy(qpad[rows].rearrange("p b (g j t) -> p b g j t", g=2, j=4)[:, :, g],
                            qn[rows, :, T_PROMPT:TOK].rearrange("p j (b t) -> p b j t", t=STEPS)), s_qpad)
        for t in range(2):
            K = P * (t + 1)
            if t == 1:
                filled(dve, ("pcT", 0, 1))
            for g in range(2):
                key, hs = ("sc", t, g), slice(4 * g, 4 * g + 4)
                filled(dve, key)
                release(dve, v.tensor_tensor(PCp[:, hs, :], split(bank(key)[:, 0:4 * NCP], NCP), C("cbias", 8, NCP)[:, t, hs], ALU.add), key, wait=True)
            V(v.tensor_reduce(small[:, 48:56], PCp[:, :, :], AX, ALU.max))
            V(v.tensor_tensor(PCp[:, :, :], PCp[:, :, :], bc(small[:, 48:56], 2, NCP), ALU.subtract), s_mx)
            dist = C("dist")[:, 256 - K:256] if t == 0 else C("dist")
            per = 4 // (t + 1)
            for br in range(2):
                if (t, br) == (0, 1):
                    dve.wait_ge(s_out, 16)
                for k in range(2 * (t + 1)):
                    key = ("s", t, br, k)
                    filled(dve, key)
                    for i in range(per):
                        h = per * k + i
                        ins = v.scalar_tensor_tensor(out=PS[:, br, h, 0:K], in0=dist, scalar=SLOPES[h], in1=bank(key)[:, K * i:K * i + K],
                                                     op0=ALU.mult, op1=ALU.add)
                        if i < per - 1:
                            V(ins, wait=False)
                        else:
                            release(dve, ins, key, wait=(k == 2 * t + 1))
                V(v.tensor_reduce(small[:, 8 * br:8 * br + 8], PS[:, br, :, 0:K], AX, ALU.max))
                V(v.tensor_scalar(small[:, 8 * br:8 * br + 8], small[:, 8 * br:8 * br + 8], -1.0, None, ALU.mult), s_mx)
            dve.wait_ge(s_exp, 3 * t + 1)
            gate = z[:, t, NG:NG + 24].rearrange("p (h c) -> p c h", c=3)
            dve.wait_ge(s_gates, 2)
            V(v.tensor_reduce(small[:, 48:56], PCp[:, :, :], AX, ALU.add))
            V(v.reciprocal(small[:, 56:64], small[:, 48:56]))
            V(v.tensor_tensor(small[:, 56:64], small[:, 56:64], gate[:, 0], ALU.mult))
            V(v.tensor_tensor(PCp[:, :, :], PCp[:, :, :], C("cmask", 8, NCP)[:, t], ALU.mult))
            V(v.tensor_tensor(PCp[:, :, :], PCp[:, :, :], bc(small[:, 56:64], 2, NCP), ALU.mult))
            for br in range(2):
                dve.wait_ge(s_exp, 3 * t + 2 + br)
                w = small[:, 32 + 8 * br:40 + 8 * br]
                V(v.reciprocal(w, small[:, 16 + 8 * br:24 + 8 * br]))
                V(v.tensor_tensor(w, w, gate[:, 1 + br], ALU.mult))
                V(v.tensor_tensor(PS[:, br, :, 0:K], PS[:, br, :, 0:K], bc(w, 2, K), ALU.mult), s_pn)
            if t == 0:
                for k in range(3):
                    copy_oT(dve, k)
            copy_pT(dve, t)
            filled(dve, ("pv", t))
            release(dve, v.tensor_copy(mixT[:, 4:8, P * t:P * t + P], split(bank(("pv", t)), P)), ("pv", t), wait=True)
        evacuated(dve, ("pT", 1, 7))
        evacuated(dve, ("pcT", 1, 1))
        for u in range(2):
            filled(dve, ("gs", u))
            release(dve, v.tensor_tensor(small[:, 32:56], bank(("gs", u))[:, 0:24], C("headsel"), ALU.mult), ("gs", u), wait=True)
            V(v.tensor_reduce(gsm[:, u, :], small[:, 32:56].rearrange("p (h c) -> p c h", c=3), AX, ALU.add))
        for u in range(2):
            if u == 1:
                evacuated(dve, ("spT", 0, 3))
            filled(dve, ("sc4", u))
            release(dve, v.tensor_tensor(LC[:, 0, :], bank(("sc4", u))[:, 0:NCB], C("bcmp"), ALU.add), ("sc4", u), wait=True)
            V(v.tensor_reduce(small[:, 64:65], LC[:, 0, :], AX, ALU.max))
            V(v.tensor_scalar(small[:, 64:65], small[:, 64:65], -1.0, None, ALU.mult), s_cmx)
            copy_skT(dve, u)
            dve.wait_ge(s_cexp, u + 1)
            V(v.reciprocal(small[:, 66:67], small[:, 65:66]))
            V(v.tensor_scalar(LC[:, 0, :], LC[:, 0, :], small[:, 66:67], None, ALU.mult))
            V(v.tensor_scalar(LC[:, 1, :], LC[:, 0, :], gsm[:, u, 0:1], None, ALU.mult), s_cpn)
            for k in range(2):
                filled(dve, ("ss", u, k))
                release(dve, v.tensor_tensor(L[:, 512 * k:512 * k + 512], bank(("ss", u, k)), C("bsel")[:, 512 * k:512 * k + 512], ALU.add), ("ss", u, k))
            filled(dve, ("sw", u))
            release(dve, v.tensor_tensor(L[:, 1056:1568], bank(("sw", u)), C("bwin"), ALU.add), ("sw", u))
            filled(dve, ("sn", u))
            V(v.tensor_tensor(L[:, 1024:1056], bank(("sn", u))[:, 0:32], C("bnew", 32)[:, u], ALU.add), wait=False)
            release(dve, v.tensor_tensor(L[:, 1568:1600], bank(("sn", u))[:, 32:64], C("bnew", 32)[:, u], ALU.add), ("sn", u), wait=True)
            filled(dve, ("spcT", u))
            release(dve, v.tensor_copy(pcs[0:NCB, :, :], split(bank(("spcT", u))[0:NCB, 0:256], P)), ("spcT", u))
            filled(dve, ("imp", u))
            release(dve, v.tensor_copy(small[:, 108:125], bank(("imp", u))[:, 0:17]), ("imp", u))
            filled(dve, ("impj", u))
            release(dve, v.tensor_copy(small[:, 128:145], bank(("impj", u))[:, 0:17]), ("impj", u), wait=True)
            V(v.tensor_reduce(small[:, 68:69], small[:, 129:144], AX, ALU.min))
            V(v.tensor_scalar(small[:, 108:123], small[:, 129:144], small[:, 68:69], None, ALU.is_equal))
            V(v.tensor_tensor(small[:, 108:123], small[:, 108:123], C("blk")[:, 1:16], ALU.mult))
            V(v.tensor_reduce(small[:, 69:70], small[:, 108:123], AX, ALU.max))
            V(v.tensor_scalar(pen[:, :], C("pblk"), small[:, 69:70], NEG, ALU.is_equal, ALU.mult))
            V(v.tensor_tensor(split(L[:, 0:1024], P), split(L[:, 0:1024], P), bc(pen[:, :], 1, 8), ALU.add))
            V(v.tensor_reduce(small[:, 70:71], L[:, 0:1056], AX, ALU.max), wait=False)
            V(v.tensor_reduce(small[:, 71:72], L[:, 1056:1600], AX, ALU.max))
            V(v.tensor_scalar(small[:, 72:74], small[:, 70:72], -1.0, None, ALU.mult), s_smx)
            residual("wo", u)
            dve.wait_ge(s_sexp, u + 1)
            V(v.reciprocal(small[:, 76:78], small[:, 74:76]))
            V(v.tensor_tensor(small[:, 76:78], small[:, 76:78], gsm[:, u, 1:3], ALU.mult))
            V(v.tensor_scalar(L[:, 0:1056], L[:, 0:1056], small[:, 76:77], None, ALU.mult), wait=False)
            V(v.tensor_scalar(L[:, 1056:1600], L[:, 1056:1600], small[:, 77:78], None, ALU.mult), s_spn)
            copy_spT(dve, u)
            filled(dve, ("spv", u))
            release(dve, v.tensor_copy(ov[:, :], bank(("spv", u))[:, 0:P]), ("spv", u))
            filled(dve, ("spvT", u))
            for g in range(2):
                rows = slice(64 * g, 64 * g + 64)
                src = bank(("spvT", u))[rows, 0:P].rearrange("p (b g j t) -> p g j b t", g=2, j=4, t=STEPS)[:, g]
                dst = mixT[rows, 4:8, T_PROMPT + 16 * u:T_PROMPT + 16 * u + 16].rearrange("p j (b t) -> p j b t", t=STEPS)
                if g == 0:
                    V(v.tensor_copy(dst, src), wait=False)
                else:
                    release(dve, v.tensor_copy(dst, src), ("spvT", u), wait=True)
        dve.sem_inc(s_end["nsa"][0], 1)
        for s in s_end["nsa"]:
            dve.wait_ge(s, 1)

        def norm(k, t, lnp):
            n = toks(t)[1]
            x = xt[0:n, t, :]
            for c in range(2):
                V(v.bn_stats(small[0:n, 150 + 6 * c:156 + 6 * c], x[:, 512 * c:512 * c + 512]), wait=(c == 1))
            V(v.bn_aggr(small[0:n, 162 + 2 * t:164 + 2 * t], small[0:n, 150:162]))
            V(v.tensor_scalar(small[0:n, 100 + t:101 + t], small[0:n, 163 + 2 * t:164 + 2 * t], EPS, None, ALU.add), s_lnv)
            dve.wait_ge(s_lnr, 3 * k + t + 1)
            V(v.reciprocal(small[0:n, 96 + t:97 + t], small[0:n, 104 + t:105 + t]))
            dve.wait_ge(s_lnp, 32 * (k + 1))
            V(v.tensor_scalar(x, x, small[0:n, 162 + 2 * t:163 + 2 * t], small[0:n, 96 + t:97 + t], ALU.subtract, ALU.mult))
            V(v.tensor_tensor(x, x, lnp[0:n, 0, :], ALU.mult))
            V(v.tensor_tensor(x, x, lnp[0:n, 1, :], ALU.add), s_ln)

        V(v.memset(qpm[:, :, :, :], 0.0))
        norm(0, 0, lnp)
        residual("wo", 2)
        copy_xT(dve, "memT", 2, memT)
        norm(0, 1, lnp)
        norm(0, 2, lnp)
        copy_mkv(dve)
        copy_xT(dve, "x1T")
        copy_mq(dve)
        evacuated(dve, ("mq", KC - 1))
        evacuated(dve, ("mq", KC - 2))
        for c in range(KC):
            o = 4 * (c // 2)
            V(v.tensor_copy(qpm[:, :, c, o:o + 4], mqT[:, c, T_PROMPT:TOK].rearrange("p (b t) -> p b t", t=STEPS)), s_mpad, wait=False)
        copy_mkT(dve, 0)
        for t in range(2):
            for k in range(2):
                filled(dve, ("ms", t, k))
                V(v.tensor_reduce(mst[t][:, 8 + 2 * k:10 + 2 * k], split(bank(("ms", t, k)), 256), AX, ALU.max))
            V(v.tensor_scalar(mst[t][:, 0:4], mst[t][:, 8:12], -1.0, None, ALU.mult), s_mmx)
        for t in range(2):
            evacuated(dve, ("ms", t, 0))
            evacuated(dve, ("ms", t, 1))
            V(v.reciprocal(mst[t][:, 12:16], mst[t][:, 4:8]))
            V(v.tensor_tensor(Pmt[t][:, :, :], Pmt[t][:, :, :], bc(mst[t][:, 12:16], 2, 256), ALU.mult), s_mpn)
        copy_mkT(dve, 1)
        for t in range(2):
            copy_mp(dve, t)
        filled(dve, ("mpT", 1, 1))
        for u in range(2):
            for b in range(4):
                if u + b > 0:
                    copy_mkT(dve, 1 + 4 * u + b)
                copy_sms(dve, u, b)
            evacuated(dve, ("sms", u, 3))
            evacuated(dve, ("sms", u, 2))
            V(v.tensor_reduce(small[:, 88:89], Pm[:, 0, :], AX, ALU.max))
            V(v.tensor_scalar(small[:, 80:81], small[:, 88:89], -1.0, None, ALU.mult), s_mmx)
            dve.wait_ge(s_mexp, u + 1)
            V(v.reciprocal(small[:, 92:93], small[:, 84:85]))
            V(v.tensor_scalar(Pm[:, 0, :], Pm[:, 0, :], small[:, 92:93], None, ALU.mult), s_mpn)
            copy_smpT(dve, u)
            for k in range(2):
                filled(dve, ("smo", u, k))
                release(dve, v.tensor_copy(so[:, GW * k:GW * k + GW], bank(("smo", u, k))), ("smo", u, k))
            for k in range(2):
                key = ("smoT", u, k)
                filled(dve, key)
                for m in range(2):
                    h, c = 2 * k + m, 4 * k + 2 * m
                    dst = mixT[:, c:c + 2, T_PROMPT + 16 * u:T_PROMPT + 16 * u + 16].rearrange("p c (b t) -> p c b t", t=STEPS)
                    src = split(bank(key), P)[:, 2 * m:2 * m + 2].rearrange("p c (b r) -> p c b r", r=32)[:, :, :, 4 * h:4 * h + 4]
                    for i in range(2):
                        ins = v.tensor_copy(dst[:, i], src[:, i])
                        if (m, i) != (1, 1):
                            V(ins, wait=False)
                release(dve, ins, key, wait=True)
        dve.sem_inc(s_end["mem"][0], 1)
        for t in range(2):
            residual("mw", t)
            norm(1, t, lnp)
        for s in s_end["mem"]:
            dve.wait_ge(s, 1)
        dve.wait_ge(s_mkout, 32)
        copy_skeyT(dve)
        residual("mw", 2)
        norm(1, 2, lnp)
        V(v.memset(sc[:, 16:24], 0.0))
        copy_xT(dve, "x2T")
        copy_pq(dve, 0, 4)
        copy_ps(dve, 0, [0])
        evacuated(dve, ("ps", 0, 0))

        def best16(step, items):
            for op in range(5):
                for i, (vals, inds, x) in enumerate(items):
                    h = slice(0, 8) if op < 3 else slice(8, 16)
                    if op in (0, 3):
                        ins = v.max(vals[:, h], x)
                    elif op in (1, 4):
                        ins = v.max_index(inds[:, h], vals[:, h], x)
                    else:
                        ins = v.match_replace(x, vals[:, 0:8], x, NEG)
                    step(ins, wait=(i == len(items) - 1))

        def experts(step, M, scores):
            R, tv, ti, tif, cand, cv, cj = (M[k] for k in ("R", "tv", "ti", "tif", "cand", "cv", "cj"))
            best16(step, [(tv[:, r, c], ti[:, r, c], scores(r, c)) for r in range(R) for c in range(2)])
            step(v.tensor_copy(tif[:, :, :, :], ti[:, :, :, :]), wait=False)
            for r in range(R):
                step(v.tensor_tensor(split(cand[:, r], 16), bc(tv[:, r, 0], 2, 16), bc(tv[:, r, 1], 1, 16), ALU.add), wait=(r == R - 1))
            best16(step, [(cv[:, r], cj[:, r], cand[:, r]) for r in range(R)])
            step(v.tensor_tensor(M["texp"][:, :, :], cv[:, :, :], cv[:, :, 0:1].to_broadcast([P, R, 16]), ALU.subtract), wait=False)
            flat, ja, jaf, eqm, ef = cj[:, :, :].rearrange("p h k -> p (h k)"), M["ja"], M["jaf"], M["eqm"], M["ef"]
            step(v.tensor_scalar(ja[:, 0], flat, 4, None, ALU.logical_shift_right), wait=False)
            step(v.tensor_scalar(ja[:, 1], flat, 15, None, ALU.bitwise_and))
            dve.sem_inc(s_tmx, 1)
            step(v.tensor_copy(jaf[:, :, :], ja[:, :, :]))
            for c in range(2):
                step(v.tensor_tensor(eqm[:, :, :], bc(jaf[:, c], 2, 16), bc(C("iota16"), 1, 16 * R), ALU.is_equal))
                for r in range(R):
                    rows = slice(16 * r, 16 * r + 16)
                    step(v.tensor_tensor(eqm[:, rows], eqm[:, rows], bc(tif[:, r, c], 1, 16), ALU.mult), wait=(r == R - 1))
                step(v.tensor_reduce(ef[:, c], eqm[:, :, :], AX, ALU.add))

        def gates(step, M, out):
            R, texp, tsum = M["R"], M["texp"], M["tsum"]
            step(v.tensor_reduce(tsum[:, 0], texp[:, :, :], AX, ALU.add))
            step(v.reciprocal(tsum[:, 1], tsum[:, 0]))
            step(v.tensor_tensor(out, texp[:, :, :], bc(tsum[:, 1], 2, 16), ALU.mult))

        def route_first(i):
            V(v.tensor_copy(xs[:, :, :, :], sc[:, 2 * i:2 * i + 2]))
            experts(V, R2, lambda r, c: xs[:, r, c])
            V(v.scalar_tensor_tensor(out=E_all[:, 2 * i:2 * i + 2, :].rearrange("p a k -> p (a k)"), in0=R2["ef"][:, 0], scalar=128.0,
                                     in1=R2["ef"][:, 1], op0=ALU.mult, op1=ALU.add))
            dve.wait_ge(s_texp, i + 1)
            gates(V, R2, W_all[:, 2 * i:2 * i + 2, :])
            dve.sem_inc(s_route, 1)

        route_first(0)
        dve.sem_inc(u_free, 8)

        route_count = dve.alloc_register("route_count")
        dve.reg_mov(route_count, 1)

        def loop_step(ins, wait=True):
            if wait:
                ins.then_inc(route_step, 1)
                dve.wait_ge(route_step, route_count)
                dve.reg_add(route_count, route_count, 1)

        def route(g, skip=0):
            step = loop_step
            step(v.tensor_copy(xs[:, :, :, :], sc[:, bass.ds(g * 2 + 2, 2)]))
            experts(step, R2, lambda r, c: xs[:, r, c])
            step(v.scalar_tensor_tensor(out=e_two[:, :, :].rearrange("p r k -> p (r k)"), in0=R2["ef"][:, 0], scalar=128.0,
                                        in1=R2["ef"][:, 1], op0=ALU.mult, op1=ALU.add))
            dve.wait_ge(s_texp, g + 2)
            gates(step, R2, w_two[:, :, :])
            step(v.tensor_copy(E_all[:, bass.ds(g * 2 + (2 + skip), 2), :], e_two[:, :, :]), wait=False)
            step(v.tensor_copy(W_all[:, bass.ds(g * 2 + (2 + skip), 2), :], w_two[:, :, :]))
            dve.sem_inc(s_route, 1)

        def dots(g, half):
            if half == 0:
                v.tensor_copy(x_cur, xt[:, bass.ds(g // 8, 1), :].rearrange("p a d -> p (a d)")).then_inc(x_ready, 1)
                dve.wait_ge(x_ready, g + 1)
            for k in range(8 * half, 8 * half + 8):
                dve.wait_ge(s_u[k % 8], 32 * g + 16 * (half + 1))
                v.tensor_tensor_reduce(out=uslot[k], in0=uslot[k], in1=x_cur, scale=1.0, scalar=0.0,
                                       op0=ALU.mult, op1=ALU.add, accum_out=h_cur[:, k:k + 1]).then_inc(u_free, 1)

        def turn(g, between=None, last=False):
            dots(g, 1)
            dve.wait_ge(u_free, GRP * g + GRP + 8)
            dve.sem_inc(h_done, 1)
            dve.wait_ge(gelu_done, g + 1)
            v.tensor_tensor(w_cur[:, :], g_cur[:, :], W_all[:, bass.ds(g, 1), :].rearrange("p a k -> p (a k)"), ALU.mult).then_inc(w_done, 1)
            if between is not None:
                between(g)
            if not last:
                dots(g + 1, 0)
            dve.wait_ge(v_free, GRP * g + 2 * GRP)
            ysl = Y[:, bass.ds(g // 8, 1), :].rearrange("p a (c n) -> p (a c) n", n=512)
            v.tensor_tensor(ysl, psum[:, 0:2, :], ysl, ALU.add).then_inc(y_free, 1)

        copy_pq(dve, 4, 8)
        copy_ps(dve, 0, [1])
        evacuated(dve, ("ps", 0, 1))
        route_first(1)
        dots(0, 0)
        copy_pq(dve, 8, 16)
        filled(dve, ("pq", 15))
        dve.sem_inc(v_free, 8)
        for t in range(3):
            copy_ps(dve, t, range(2 if t == 0 else 0, 4))
        for t in range(3):
            for q in range(4):
                evacuated(dve, ("ps", t, q))
        dve.sem_inc(v_free, 8)
        V(v.memset(Y[:, :, :], 0.0))
        dve.sem_inc(y_free, 1)
        turn(0)
        with dve.Fori(1, 7) as g:
            turn(g, route)
        with dve.Fori(7, 11) as g:
            turn(g, lambda g: route(g, 2))
        with dve.Fori(11, 15) as g:
            turn(g)
        dve.wait_ge(s_fold, 16 * 11)
        turn(15)
        dve.wait_ge(y_free, 17)
        for t in range(2):
            x = xt[:, t, :]
            V(v.scalar_tensor_tensor(out=x, in0=x, scalar=ALPHA, in1=Y[:, t, :], op0=ALU.mult, op1=ALU.add))
            norm(2, t, lnp3)
        turn(16)
        turn(17, last=True)
        dve.wait_ge(y_free, NGRP + 1)
        dve.sem_inc(s_y, 1)
        for c in range(2):
            x = xt[0:32, 2, GW * c:GW * c + GW]
            filled(dve, ("yfold", c))
            release(dve, v.scalar_tensor_tensor(out=x, in0=x, scalar=ALPHA, in1=bank(("yfold", c))[0:32], op0=ALU.mult, op1=ALU.add), ("yfold", c), wait=True)
        norm(2, 2, lnp3)

    @block.tensor
    def _(pe):
        def begin(key):
            if JOB[key] >= 8:
                pe.wait_ge(bank_free[JOB[key] % 8], JOB[key] // 8)
            return bank(key)

        def done(ins, key):
            ins.then_inc(bank_full[JOB[key] % 8], 1)

        mm, tr = nc.tensor.matmul, nc.tensor.transpose

        def landed(n):
            pe.wait_ge(s_w[n % 2], w_value(n))
            return wbuf[:, n % 2]

        def turn_tokens(name, src, ntile=3, norms=None):
            for t in range(ntile):
                n = toks(t)[1]
                if norms is not None:
                    pe.wait_ge(s_ln, 3 * norms + t + 1)
                for c in range(2):
                    o = begin((name, t, c))
                    for i in range(4):
                        k = 4 * c + i
                        ins = tr(o[:, P * i:P * i + n], src[0:n, t, P * k:P * k + P], ident[0:n, 0:n])
                    done(ins, (name, t, c))

        def by_token(name, group, xs, c, ntile=3, w=GW):
            wt = landed(group)
            for t in range(ntile):
                t0, n = toks(t)
                o = begin((name, c, t))
                for k in range(KC):
                    ins = mm(o[0:n, 0:w], xs[:, k, t0:t0 + n], wt[:, k, 0:w], start=(k == 0), stop=(k == KC - 1))
                done(ins, (name, c, t))

        def by_tile(name, w, tiles=range(3)):
            wt = [landed(WG[w, c]) for c in range(2)]
            for t in tiles:
                t0, n = toks(t)
                for c in range(2):
                    o = begin((name, t, c))
                    for k in range(KC):
                        ins = mm(o[0:n, :], mixT[:, k, t0:t0 + n], wt[c][:, k, :], start=(k == 0), stop=(k == KC - 1))
                    done(ins, (name, t, c))

        def by_feature(name, group, c, cols):
            wt = landed(group)
            o = begin((name, c))
            for k in range(KC):
                ins = mm(o[:, 0:TOK], wt[:, k, cols:cols + P], xT[:, k, :], start=(k == 0), stop=(k == KC - 1))
            done(ins, (name, c))

        def all_evacuated(keys):
            for key in keys:
                evacuated(pe, key)

        pe.wait_ge(s_const, 16)
        pe.wait_ge(s_x, 32)
        turn_tokens("xT", xt)
        all_evacuated([("xT", t, c) for t in range(3) for c in range(2)])
        for c in range(8):
            by_feature("zf", WG["w_in", (HF if c < 4 else HQ) // GW], c, P * (c % 4))
        for g, (col, _, w_) in enumerate(Z_GROUPS):
            by_token("z", WG["w_in", col // GW], xT, g, 3, w_)
            if g == 1:
                for j in range(4):
                    by_feature("zq", WG["w_in", NQ // GW], j, P * j)

        for kv in range(2):
            for i in range(4):
                for q in range(4):
                    if q % 2 == 0:
                        pe.wait_ge(s_sorted[q // 2], 4 * kv + i + 1)
                    o = begin(("subT", kv, i, q))
                    for m in range(4):
                        at = P * (4 * q + m)
                        ins = tr(o[:, P * m:P * m + P], subg[:, at:at + P], ident)
                    done(ins, ("subT", kv, i, q))
            pe.wait_ge(s_subp, 32 * (kv + 1))
            o = begin(("subT", kv, 4, 0))
            for m in range(16):
                ins = tr(o[:, 16 * m:16 * m + 16], subp[:, P * m:P * m + P], ident[0:16, 0:16])
            done(ins, ("subT", kv, 4, 0))
            all_evacuated([("subT", kv, i, q) for i in range(4) for q in range(4)] + [("subT", kv, 4, 0)])
            pe.wait_ge(s_cw, 16 * (3 + kv))
            for g in range(2):
                o = begin(("hid", kv, g))
                for n in range(16):
                    part = subT[:, 8 * g + n % 8, 0:512].rearrange("p (b s) -> p b s", s=64)[:, :, n // 8:n // 8 + NCB]
                    ins = mm(o[:, 0:504].rearrange("p (b s) -> p b s", s=NCB), w1[:, n, :], part, start=(n == 0), stop=(n == 15))
                done(ins, ("hid", kv, g))
            o = begin(("hidp", kv))
            both = subT[:, :, :].rearrange("p (g r) b -> p r g b", g=2)
            for n in range(16):
                ins = mm(split(o[:, 0:30], 15), w1[:, n, :], both[:, n % 8, :, 512 + n // 8:512 + n // 8 + NCP],
                         start=(n == 0), stop=(n == 15))
            done(ins, ("hidp", kv))
            all_evacuated([("hid", kv, 0), ("hid", kv, 1), ("hidp", kv)])
            if kv == 0:
                for key, o_, w_ in ((("kcT",), 0, 504), (("kcTp",), 504, NCP)):
                    o = begin(key)
                    for g in range(2):
                        ins = mm(o[64 * g:64 * g + 64, 0:w_], w2[:, 0, :], hid[:, g, o_:o_ + w_], start=True, stop=True)
                    done(ins, key)
            else:
                for c in range(2):
                    o = begin(("vc", c))
                    for b in range(4):
                        for g in range(2):
                            at = NCB * (4 * c + b)
                            ins = mm(o[0:NCB, P * b + 64 * g:P * b + 64 * g + 64], hid[:, g, at:at + NCB], w2[:, 1, :], start=True, stop=True)
                    done(ins, ("vc", c))
                o = begin(("vcp",))
                for g in range(2):
                    ins = mm(o[0:NCP, 64 * g:64 * g + 64], hid[:, g, 504:519], w2[:, 1, :], start=True, stop=True)
                done(ins, ("vcp",))

        for t in range(3):
            n = toks(t)[1]
            o = begin(("nkT", t))
            for i, c in enumerate((KSC, KWC)):
                ins = tr(o[:, P * i:P * i + n], z[0:n, t, c:c + P], ident[0:n, 0:n])
            done(ins, ("nkT", t))
        pe.wait_ge(s_ke, 1)
        for t in range(3):
            t0, n = toks(t)
            o = begin(("att", t))
            for h in range(H):
                ins = mm(o[0:n, P * h:P * h + n], e3[:, h, t0:t0 + n], e2[:, h, t0:t0 + n], start=True, stop=True)
            done(ins, ("att", t))
        pe.wait_ge(s_ke, 2)
        for t in range(3):
            t0, n = toks(t)
            o = begin(("kE", t))
            for h in range(H):
                ins = tr(o[0:n, P * h:P * h + P], kT[:, h, t0:t0 + n], ident)
            done(ins, ("kE", t))
        for t in range(3):
            n = toks(t)[1]
            evacuated(pe, ("att", t))
            o = begin(("oin", t))
            for h in range(H):
                ins = mm(o[0:n, P * h:P * h + P], attS[0:n, t, h, 0:n], z[0:n, t, HI + P * h:HI + P * h + P], start=True, stop=True)
            done(ins, ("oin", t))
        all_evacuated([("kE", t) for t in range(3)])
        for c in range(NCH):
            t, r = c // 4, slice(32 * (c % 4), 32 * (c % 4) + 32)
            o = begin(("U", c))
            for h in range(H):
                ins = mm(o[:, P * h:P * h + P], ktok[r, t, h, :], z[r, t, HI + P * h:HI + P * h + P], start=True, stop=True,
                         tile_position=(r.start, 0))
            done(ins, ("U", c))
        pe.wait_ge(s_ke, 3)
        pe.wait_ge(s_stin, 16)
        for t in range(3):
            if t < 2:
                evacuated(pe, ("U", 4 * t + 2))
            o = begin(("ost", t))
            for h in range(H):
                if t < 2:
                    for j in range(4):
                        c = 4 * t + j
                        ins = mm(o[32 * j:32 * j + 32, P * h:P * h + P], qT[:, h, CH * c:CH * c + CH], state[:, c, h, :], start=True, stop=True)
                else:
                    for b in range(N_SAMPLE):
                        ins = mm(o[0:32, P * h:P * h + P], qGm[:, h, b, :], sstate[:, b, h, :], start=(b == 0), stop=(b == N_SAMPLE - 1))
            done(ins, ("ost", t))
        pe.wait_ge(s_vm, N_SAMPLE)
        for b in range(N_SAMPLE):
            o = begin(("US", b))
            for h in range(H):
                ins = mm(o[:, P * h:P * h + P], ktok[0:32, 2, h, :], vm[0:32, b, P * h:P * h + P], start=True, stop=True)
            done(ins, ("US", b))

        all_evacuated([("zq", j) for j in range(4)] + [("nkT", t) for t in range(3)])
        for t in range(2):
            K, t0, per = P * (t + 1), P * t, 4 // (t + 1)
            for g in range(2):
                o, r = begin(("sc", t, g)), slice(64 * g, 64 * g + 64)
                for j in range(4):
                    ins = mm(o[:, NCP * j:NCP * j + NCP], qn[r, j, t0:t0 + P], kcT[r, 504:519], start=True, stop=True)
                done(ins, ("sc", t, g))
            for br in range(2):
                for k in range(2 * (t + 1)):
                    o = begin(("s", t, br, k))
                    for i in range(per):
                        h = per * k + i
                        r = slice(64 * (h // 4), 64 * (h // 4) + 64)
                        ins = mm(o[:, K * i:K * i + K], qn[r, h % 4, t0:t0 + P], kn[r, br, 0:K], start=True, stop=True)
                    done(ins, ("s", t, br, k))
            if t == 0:
                pe.wait_ge(s_otok, 3)
                for k in range(3):
                    n = toks(k)[1]
                    o = begin(("oT", k))
                    for h in range(H):
                        ins = tr(o[:, P * h:P * h + n], otok[0:n, k, h, :], ident[0:n, 0:n])
                    done(ins, ("oT", k))
            blocks = [(br, h, i) for br in range(2) for h in range(8) for i in range(t + 1)]
            for k in range(4 * (t + 1)):
                if k % (2 * (t + 1)) == 0:
                    pe.wait_ge(s_pn, 2 * t + 1 + k // (2 * (t + 1)))
                o = begin(("pT", t, k))
                for m in range(4):
                    br, h, i = blocks[4 * k + m]
                    ins = tr(o[:, P * m:P * m + P], PS[:, br, h, P * i:P * i + P], ident)
                done(ins, ("pT", t, k))
            for k in range(2):
                o = begin(("pcT", t, k))
                for m in range(4):
                    ins = tr(o[0:NCP, P * m:P * m + P], PCp[:, 4 * k + m, :], ident)
                done(ins, ("pcT", t, k))
            all_evacuated([("pT", t, k) for k in range(4 * (t + 1))] + [("pcT", t, k) for k in range(2)])
            o = begin(("pv", t))
            for h in range(8):
                g, j = h // 4, h % 4
                terms = [(z[:, i, (VSC, VWC)[br] + 64 * g:(VSC, VWC)[br] + 64 * g + 64], PTp[:, blocks.index((br, h, i)), :])
                         for br in range(2) for i in range(t + 1)]
                terms.append((vcP[0:NCP, 64 * g:64 * g + 64], PCT[0:NCP, h, :]))
                for n, (lhsT, rhs) in enumerate(terms):
                    ins = mm(o[64 * g:64 * g + 64, P * j:P * j + P], lhsT, rhs, start=(n == 0), stop=(n == len(terms) - 1))
            done(ins, ("pv", t))
        pe.wait_ge(s_gates, 2)
        for u in range(2):
            o = begin(("gs", u))
            done(mm(o[:, 0:24], C("rowsel", P)[0:32, u, :], z[0:32, 2, NG:NG + 24], start=True, stop=True), ("gs", u))
        pe.wait_ge(s_qpad, 2)
        for u in range(2):
            o = begin(("sc4", u))
            for b in range(4):
                s = 4 * u + b
                ins = mm(o[32 * b:32 * b + 32, 0:NCB], qpad[:, s, :], kcT[:, NCB * s:NCB * s + NCB], start=True, stop=True)
            done(ins, ("sc4", u))
            for b in range(4):
                s = 4 * u + b
                pe.wait_ge(s_slk[s % 2], 32 * (s // 2 + 1))
                for k in range(3):
                    src = slk[:, s % 2, 512 * k:512 * k + 512] if k < 2 else wk[:, s % 2, :]
                    o = begin(("skT", u, b, k))
                    for i in range(4):
                        ins = tr(o[:, P * i:P * i + P], src[:, P * i:P * i + P], ident)
                    done(ins, ("skT", u, b, k))
            all_evacuated([("skT", u, b, k) for b in range(4) for k in range(3)])
            for key, c0 in ((("ss", u, 0), 0), (("ss", u, 1), 512), (("sw", u), 1024)):
                o = begin(key)
                for b in range(4):
                    ins = mm(o[32 * b:32 * b + 32, :], qpad[:, 4 * u + b, :], KT[:, b, c0:c0 + 512], start=True, stop=True)
                done(ins, key)
            o = begin(("sn", u))
            for b in range(4):
                for br in range(2):
                    ins = mm(o[32 * b:32 * b + 32, 32 * br:32 * br + 32], qpad[:, 4 * u + b, :], kn[:, br, T_PROMPT:TOK], start=True, stop=True)
            done(ins, ("sn", u))
            pe.wait_ge(s_cpn, u + 1)
            o = begin(("spcT", u))
            for i in range(2):
                ins = tr(o[0:NCB, P * i:P * i + P], LC[:, i, :], ident)
            done(ins, ("spcT", u))
            evacuated(pe, ("spcT", u))
            o = begin(("imp", u))
            done(mm(o[:, 0:17], pcs[0:NCB, 0, :], C("cover")[0:NCB], start=True, stop=True), ("imp", u))
            evacuated(pe, ("imp", u))
            o = begin(("impj", u))
            done(mm(o[:, 0:17], C("jsum"), small[:, 108:125], start=True, stop=True), ("impj", u))
            if u == 0:
                all_evacuated([("pv", 0), ("pv", 1)] + [("oT", k) for k in range(3)])
            by_tile("wo", "w_out", [u])
            pe.wait_ge(s_spn, u + 1)
            for k in range(3):
                o = begin(("spT", u, k))
                c0 = 512 * k if k < 2 else 1056
                for i in range(4):
                    ins = tr(o[:, P * i:P * i + P], L[:, c0 + P * i:c0 + P * i + P], ident)
                done(ins, ("spT", u, k))
            o = begin(("spT", u, 3))
            for i, c0 in enumerate((1024, 1568)):
                ins = tr(o[0:32, P * i:P * i + P], L[:, c0:c0 + 32], ident)
            done(ins, ("spT", u, 3))
            all_evacuated([("spT", u, k) for k in range(4)])
            o = begin(("spv", u))
            for b in range(4):
                r = slice(32 * b, 32 * b + 32)
                pe.wait_ge(s_slv[b], 32 * (u + 1))
                terms = [(PTs[:, i, r], slv[:, b, P * i:P * i + P]) for i in range(8)]
                terms += [(PTs[:, 8 + i, r], wv[:, b, P * i:P * i + P]) for i in range(4)]
                terms += [(PTs[0:32, 12, r], z[0:32, 2, VSC:VSC + P]), (PTs[0:32, 13, r], z[0:32, 2, VWC:VWC + P]),
                          (pcs[0:NCB, 1, r], vcS[0:NCB, 4 * u + b, :])]
                for n, (lhsT, rhs) in enumerate(terms):
                    ins = mm(o[r, 0:P], lhsT, rhs, start=(n == 0), stop=(n == len(terms) - 1))
            done(ins, ("spv", u))
            evacuated(pe, ("spv", u))
            o = begin(("spvT", u))
            done(tr(o[:, 0:P], ov[:, :], ident), ("spvT", u))
        all_evacuated([("spvT", 0), ("spvT", 1)])
        by_tile("wo", "w_out", [2])

        pe.wait_ge(s_mem, 16)
        turn_tokens("memT", memp, 2)
        all_evacuated([("memT", t, c) for t in range(2) for c in range(2)])
        for name, w in (("mk", "w_mem_k"), ("mv", "w_mem_v")):
            for c in range(2):
                by_token(name, WG[w, c], memT, c, 2)
        turn_tokens("x1T", xt, norms=0)
        all_evacuated([("x1T", t, c) for t in range(3) for c in range(2)])
        for c in range(KC):
            by_feature("mq", WG["w_mem_q", c // 4], c, P * (c % 4))
        all_evacuated([("mk", c, t) for c in range(2) for t in range(2)] + [("mv", c, t) for c in range(2) for t in range(2)])

        def turn_keys(seq, src):
            for q in range(4):
                o = begin(("mkT", seq, q))
                for m in range(4):
                    c, i = 2 * q + m // 2, m % 2
                    ins = tr(o[:, P * m:P * m + P], src[:, i, P * c:P * c + P], ident)
                done(ins, ("mkT", seq, q))

        turn_keys(0, mkt)
        all_evacuated([("mkT", 0, q) for q in range(4)] + [("mq", c) for c in range(KC)])
        for t in range(2):
            for k in range(2):
                o = begin(("ms", t, k))
                for m in range(2):
                    for i in range(2):
                        c = 2 * (2 * k + m) + i
                        ins = mm(o[:, 256 * m:256 * m + 256], mqT[:, c, P * t:P * t + P], KTm[:, 0, c, :], start=(i == 0), stop=(i == 1))
                done(ins, ("ms", t, k))
        pe.wait_ge(s_mck[0], 16)
        turn_keys(1, mck[:, 0])
        for t in range(2):
            pe.wait_ge(s_mpn, t + 1)
            for k in range(2):
                o = begin(("mpT", t, k))
                for m in range(4):
                    h, i = 2 * k + m // 2, m % 2
                    ins = tr(o[:, P * m:P * m + P], Pmt[t][:, h, P * i:P * i + P], ident)
                done(ins, ("mpT", t, k))
            all_evacuated([("mpT", t, 0), ("mpT", t, 1)])
            for k in range(2):
                o = begin(("mo", t, k))
                for m in range(4):
                    c = 4 * k + m
                    for i in range(2):
                        ins = mm(o[:, P * m:P * m + P], mvt[:, i, P * c:P * c + P], PTm[:, 2 * (c // 2) + i, :], start=(i == 0), stop=(i == 1))
                done(ins, ("mo", t, k))
        pe.wait_ge(s_mpad, KC)
        for u in range(2):
            for b in range(4):
                s = 4 * u + b
                if s > 0:
                    pe.wait_ge(s_mck[s % 2], 16 * (s // 2 + 1))
                    turn_keys(1 + s, mck[:, s % 2])
                all_evacuated([("mkT", 1 + s, q) for q in range(4)])
                o = begin(("sms", u, b))
                for c in range(KC):
                    ins = mm(o[32 * b:32 * b + 32, 0:256], qpm[:, s, c, :], KTm[:, (1 + s) % 2, c, :], start=(c == 0), stop=(c == KC - 1))
                done(ins, ("sms", u, b))
            pe.wait_ge(s_mpn, 3 + u)
            o = begin(("smpT", u))
            for i in range(2):
                ins = tr(o[:, P * i:P * i + P], Pm[:, 0, P * i:P * i + P], ident)
            done(ins, ("smpT", u))
            evacuated(pe, ("smpT", u))
            for k in range(2):
                o = begin(("smo", u, k))
                for b in range(4):
                    if k == 0:
                        pe.wait_ge(s_mcv[b], 16 * (u + 1))
                    r = slice(32 * b, 32 * b + 32)
                    for i in range(2):
                        ins = mm(o[r, :], PTm[:, i, r], mcv[:, b, i, GW * k:GW * k + GW], start=(i == 0), stop=(i == 1))
                done(ins, ("smo", u, k))
            for k in range(2):
                evacuated(pe, ("smo", u, k))
                o = begin(("smoT", u, k))
                for m in range(4):
                    ins = tr(o[:, P * m:P * m + P], so[:, GW * k + P * m:GW * k + P * m + P], ident)
                done(ins, ("smoT", u, k))
        all_evacuated([("mo", t, k) for t in range(2) for k in range(2)] + [("smoT", u, k) for u in range(2) for k in range(2)])
        by_tile("mw", "w_mem_o", range(2))
        pe.wait_ge(s_skey, 16)
        for q in range(4):
            o = begin(("skeyT", q))
            for m in range(4):
                ins = tr(o[:, P * m:P * m + P], skey[:, 4 * q + m, :], ident)
            done(ins, ("skeyT", q))
        by_tile("mw", "w_mem_o", [2])

        turn_tokens("x2T", xt, norms=1)
        all_evacuated([("x2T", t, c) for t in range(3) for c in range(2)])

        def key_scores(t, q):
            t0, n = toks(t)
            o = begin(("ps", t, q))
            for m in range(4):
                hc = 4 * q + m
                ins = mm(o[0:n, P * m:P * m + P], pqT[:, hc, t0:t0 + n], skT[:, hc, :], start=True, stop=True)
            done(ins, ("ps", t, q))

        def queries(first, last):
            for c in range(first, last):
                by_feature("pq", WG["peer_w_q", c // 4], c, P * (c % 4))

        queries(0, 4)
        all_evacuated([("pq", c) for c in range(4)] + [("skeyT", q) for q in range(4)])
        key_scores(0, 0)
        queries(4, 8)
        all_evacuated([("pq", c) for c in range(4, 8)])
        key_scores(0, 1)
        queries(8, 16)
        all_evacuated([("pq", c) for c in range(8, 16)])
        for t in range(3):
            for q in range(2 if t == 0 else 0, 4):
                key_scores(t, q)
        all_evacuated([("ps", t, q) for t in range(3) for q in range(4)])
        with pe.Fori(0, NGRP) as g:
            pe.wait_ge(y_free, g + 1)
            for k in range(GRP):
                pe.wait_ge(diag_done, GRP * g + k + 1)
                pe.wait_ge(s_v[k], 16 * g + 16)
                for c in range(2):
                    ins = mm(psum[:, c, :], diag[:, k, :], vslot[k][:, GW * c:GW * c + GW], start=(k == 0), stop=(k == GRP - 1))
                ins.then_inc(v_free, 1)
        pe.wait_ge(s_y, 1)
        for c in range(2):
            o = begin(("yfold", c))
            done(mm(o[0:32, :], C("fold"), Y[:, 2, GW * c:GW * c + GW], start=True, stop=True), ("yfold", c))

    ctx.close()


_INS = ["x_prompt", "x_sample", "cache_k_cmp", "cache_v_cmp", "cache_k_slc", "cache_v_slc", "cache_k_win", "cache_v_win",
        "state_hgrn", "cache_mem_k", "cache_mem_v", "page_table", "mem_prompt", "w_in", "hgrn_lb_logits", "hgrn_norm_g",
        "cmp_k_w1", "cmp_k_b1", "cmp_k_w2", "cmp_k_b2", "cmp_v_w1", "cmp_v_b1", "cmp_v_w2", "cmp_v_b2", "w_out", "ln1_g",
        "ln1_b", "w_mem_q", "w_mem_k", "w_mem_v", "w_mem_o", "ln2_g", "ln2_b", "peer_w_q", "peer_sub_keys", "peer_u",
        "peer_v", "ln3_g", "ln3_b"]
_KV = (1, 1, 256, 2, 64)
_KVS = (1, 8, 4, 2, 64)
_OUTS = [(1, 256, 1024), (8, 4, 1024)] + [_KV] * 6 + [(1, 1, 4, 128, 128)] + [(1, 1, 256, 4, 256)] * 2 + [_KVS] * 6 + [(1, 8, 4, 128, 128)]


def kernel(**inputs):
    import numpy as _np
    import concourse.bacc as _bacc
    from concourse import mybir as _mybir
    from concourse.bass_utils import run_bass_kernel_spmd as _run

    nc = _bacc.Bacc("TRN2", target_bir_lowering=False, num_devices=1)
    arrays, args = {}, {}
    for name in _INS:
        a = _np.ascontiguousarray(inputs[name])
        arrays[f"in_{name}"] = a
        args[name] = nc.dram_tensor(f"in_{name}", a.shape, _mybir.dt.from_np(a.dtype), kind="ExternalInput").ap()
    arrays["consts"] = const_table()[0]
    args["consts"] = nc.dram_tensor("consts", arrays["consts"].shape, _mybir.dt.float32, kind="ExternalInput").ap()
    outs = [nc.dram_tensor(f"out_{i}", s, _mybir.dt.float32, kind="ExternalOutput").ap() for i, s in enumerate(_OUTS)]
    layer_kernel(nc, args, outs)
    r = _run(nc, [arrays], core_ids=[0])
    return tuple(r.results[0][f"out_{i}"] for i in range(len(_OUTS)))
```
